# Optimizing a Trainium2 kernel written in Bass

```python
import jax, jax.numpy as jnp
from jax import lax
import numpy as np

D_MODEL = 1024
BATCH = 1
SEQ = 256
DEPTH = 2

EPS = 1e-6
GLA_HEADS = 4
GLA_DK = 128
GLA_DV = 256
GLA_GATE_RANK = 16
GLA_GATE_TAU = 16.0
GLA_CHUNK = 64
GLA_PROJ = GLA_HEADS * (2 * GLA_DK + 2 * GLA_DV) + GLA_GATE_RANK
SWA_HEADS = 16
SWA_KV_HEADS = 4
SWA_GROUP = SWA_HEADS // SWA_KV_HEADS
SWA_HEAD_DIM = 64
SWA_WINDOW = 128
SWA_BLOCK = 128
ROT_DIM = SWA_HEAD_DIM // 4
ROPE_THETA = 500000.0
PEER_HEADS = 8
PEER_N_KEYS = 128
PEER_EXPERTS = PEER_N_KEYS * PEER_N_KEYS
PEER_TOPK = 16
PEER_QDIM = 256
PEER_BLOCK = 128


def rmsnorm(x, g):
    x32 = x.astype(jnp.float32)
    y = x32 * lax.rsqrt(jnp.mean(x32 * x32, axis=-1, keepdims=True) + EPS)
    return (y * g.astype(jnp.float32)).astype(x.dtype)

def modulate(x, g, shift, scale):
    return rmsnorm(x, g) * (1.0 + scale[:, None, :]) + shift[:, None, :]

def rope_tables(positions):
    inv = ROPE_THETA ** (-jnp.arange(0, ROT_DIM, 2, dtype=jnp.float32) / ROT_DIM)
    ang = positions.astype(jnp.float32)[..., None] * inv
    return jnp.cos(ang), jnp.sin(ang)

def apply_partial_rope(x, cos, sin):
    half = ROT_DIM // 2
    xr = x[..., :ROT_DIM].astype(jnp.float32)
    x1, x2 = xr[..., :half], xr[..., half:]
    c = cos[:, :, None, :]
    s = sin[:, :, None, :]
    rot = jnp.concatenate([x1 * c - x2 * s, x2 * c + x1 * s], axis=-1).astype(x.dtype)
    return jnp.concatenate([rot, x[..., ROT_DIM:]], axis=-1)

def gla_mixer(h, w_in, w_g2, b_g2, norm_g, w_out):
    bsz, s_len, _ = h.shape
    H, dk, dv, C = GLA_HEADS, GLA_DK, GLA_DV, GLA_CHUNK
    n_c = s_len // C
    proj = h @ w_in
    q, k, v, og, gl = jnp.split(proj, [H * dk, 2 * H * dk, 2 * H * dk + H * dv, 2 * H * dk + 2 * H * dv], axis=-1)
    log_a = jax.nn.log_sigmoid((gl @ w_g2 + b_g2).astype(jnp.float32)) / GLA_GATE_TAU
    shp = (bsz, n_c, C, H, dk)
    q = q.reshape(shp).astype(jnp.float32) * (dk ** -0.5)
    k = k.reshape(shp).astype(jnp.float32)
    v = v.reshape(bsz, n_c, C, H, dv).astype(jnp.float32)
    b = jnp.cumsum(log_a.reshape(shp), axis=2)
    b_last = b[:, :, -1:]
    q_t = q * jnp.exp(b)
    k_t = k * jnp.exp(-b)
    k_dec = k * jnp.exp(b_last - b)
    scores = jnp.einsum('bnchd,bnmhd->bnhcm', q_t, k_t)
    tri = jnp.tril(jnp.ones((C, C), dtype=bool))
    scores = jnp.where(tri, scores, 0.0)
    o_intra = jnp.einsum('bnhcm,bnmhe->bnche', scores, v)
    dec = jnp.exp(b_last[:, :, 0])

    def step(state, inp):
        q_n, k_n, v_n, d_n = inp
        o_n = jnp.einsum('bchd,bhde->bche', q_n, state)
        state = d_n[..., None] * state + jnp.einsum('bchd,bche->bhde', k_n, v_n)
        return state, o_n

    xs = (jnp.moveaxis(q_t, 1, 0), jnp.moveaxis(k_dec, 1, 0), jnp.moveaxis(v, 1, 0), jnp.moveaxis(dec, 1, 0))
    _, o_inter = lax.scan(step, jnp.zeros((bsz, H, dk, dv), jnp.float32), xs)
    o = (o_intra + jnp.moveaxis(o_inter, 0, 1)).reshape(bsz, s_len, H, dv)
    o = rmsnorm(o, norm_g) * jax.nn.silu(og.reshape(bsz, s_len, H, dv).astype(jnp.float32))
    return (o.reshape(bsz, s_len, H * dv) @ w_out).astype(h.dtype)

def shared_kv(h, kv_w, cos, sin):
    bsz, s_len, _ = h.shape
    kv = h @ kv_w
    k, v = jnp.split(kv, 2, axis=-1)
    k = apply_partial_rope(k.reshape(bsz, s_len, SWA_KV_HEADS, SWA_HEAD_DIM), cos, sin)
    v = v.reshape(bsz, s_len, SWA_KV_HEADS, SWA_HEAD_DIM)
    return k, v

def swa_sink_attention(h, w_q, sinks, w_out, k, v, cos, sin):
    bsz, s_len, _ = h.shape
    P = SWA_BLOCK
    n_b = s_len // P
    q = apply_partial_rope((h @ w_q).reshape(bsz, s_len, SWA_HEADS, SWA_HEAD_DIM), cos, sin)
    q = q.reshape(bsz, n_b, P, SWA_KV_HEADS, SWA_GROUP, SWA_HEAD_DIM)

    def band(t):
        prev = jnp.pad(t, ((0, 0), (P, 0), (0, 0), (0, 0)))[:, :s_len]
        shp = (bsz, n_b, P, SWA_KV_HEADS, SWA_HEAD_DIM)
        return jnp.concatenate([prev.reshape(shp), t.reshape(shp)], axis=2)

    k_band, v_band = band(k), band(v)
    s = jnp.einsum('bnqkgd,bnmkd->bnkgqm', q, k_band).astype(jnp.float32) * (SWA_HEAD_DIM ** -0.5)
    qi = jnp.arange(P)[:, None]
    mi = jnp.arange(2 * P)[None, :]
    rel = qi + P - mi
    in_window = (rel >= 0) & (rel < SWA_WINDOW)
    key_pos = jnp.arange(n_b)[:, None, None] * P - P + mi[None]
    mask = in_window[None] & (key_pos >= 0)
    s = jnp.where(mask[None, :, None, None], s, -jnp.inf)
    sink = sinks.astype(jnp.float32).reshape(SWA_KV_HEADS, SWA_GROUP)[None, None, :, :, None, None]
    m = jnp.maximum(jnp.max(s, axis=-1, keepdims=True), sink)
    p = jnp.exp(s - m)
    probs = p / (jnp.sum(p, axis=-1, keepdims=True) + jnp.exp(sink - m))
    o = jnp.einsum('bnkgqm,bnmkd->bnqkgd', probs, v_band.astype(jnp.float32))
    return (o.reshape(bsz, s_len, SWA_HEADS * SWA_HEAD_DIM) @ w_out).astype(h.dtype)

def peer(h, w_q, subkeys, u_tab, v_tab):
    bsz, s_len, d = h.shape
    half = PEER_QDIM // 2
    tokens = h.reshape(-1, PEER_BLOCK, d)

    def block(xb):
        q = (xb @ w_q).reshape(PEER_BLOCK, PEER_HEADS, PEER_QDIM)
        s1 = jnp.einsum('phd,nd->phn', q[..., :half], subkeys[0])
        s2 = jnp.einsum('phd,nd->phn', q[..., half:], subkeys[1])
        v1, i1 = lax.top_k(s1, PEER_TOPK)
        v2, i2 = lax.top_k(s2, PEER_TOPK)
        cand = (v1[..., :, None] + v2[..., None, :]).reshape(PEER_BLOCK, PEER_HEADS, PEER_TOPK * PEER_TOPK)
        cs, ci = lax.top_k(cand, PEER_TOPK)
        e = (jnp.take_along_axis(i1, ci // PEER_TOPK, axis=-1) * PEER_N_KEYS
             + jnp.take_along_axis(i2, ci % PEER_TOPK, axis=-1))
        g = jax.nn.softmax(cs.astype(jnp.float32), axis=-1)
        u = u_tab[e]
        a = jax.nn.gelu(jnp.einsum('pd,phkd->phk', xb, u).astype(jnp.float32), approximate=False)
        return jnp.einsum('phk,phkd->pd', g * a, v_tab[e].astype(jnp.float32)).astype(xb.dtype)

    return lax.map(block, tokens).reshape(bsz, s_len, d)

def first_inputs(seed: int = 0) -> dict:
    key = jax.random.key(seed)
    ks = jax.random.split(key, 24)
    n_a = DEPTH // 2
    n_b = DEPTH - n_a
    D = D_MODEL
    f32 = jnp.float32

    def nrm(k, shape, scale):
        return jax.random.normal(k, shape, f32) * scale

    positions = (jax.random.randint(ks[2], (BATCH, 1), 0, 4096, dtype=jnp.int32)
                 + jnp.arange(SEQ, dtype=jnp.int32)[None, :])
    return {
        "x": nrm(ks[0], (BATCH, SEQ, D), 1.0),
        "c": nrm(ks[1], (BATCH, D), 1.0),
        "positions": positions,
        "mod_w": nrm(ks[3], (DEPTH, D, 6 * D), 0.5 * D ** -0.5),
        "mod_b": nrm(ks[4], (DEPTH, 6 * D), 0.02),
        "norm_g": 1.0 + nrm(ks[5], (DEPTH, 2, D), 0.02),
        "gla_w_in": nrm(ks[6], (n_a, D, GLA_PROJ), D ** -0.5),
        "gla_w_g2": nrm(ks[7], (n_a, GLA_GATE_RANK, GLA_HEADS * GLA_DK), GLA_GATE_RANK ** -0.5),
        "gla_b_g2": nrm(ks[8], (n_a, GLA_HEADS * GLA_DK), 0.1),
        "gla_norm_g": 1.0 + nrm(ks[9], (n_a, GLA_DV), 0.02),
        "gla_w_out": nrm(ks[10], (n_a, GLA_HEADS * GLA_DV, D), (GLA_HEADS * GLA_DV) ** -0.5),
        "kv_mod_w": nrm(ks[11], (D, 2 * D), 0.5 * D ** -0.5),
        "kv_mod_b": nrm(ks[12], (2 * D,), 0.02),
        "kv_norm_g": 1.0 + nrm(ks[13], (D,), 0.02),
        "kv_w": nrm(ks[14], (D, 2 * SWA_KV_HEADS * SWA_HEAD_DIM), D ** -0.5),
        "swa_w_q": nrm(ks[15], (n_b, D, SWA_HEADS * SWA_HEAD_DIM), D ** -0.5),
        "swa_sinks": nrm(ks[16], (n_b, SWA_HEADS), 0.5),
        "swa_w_out": nrm(ks[17], (n_b, SWA_HEADS * SWA_HEAD_DIM, D), (SWA_HEADS * SWA_HEAD_DIM) ** -0.5),
        "peer_w_q": nrm(ks[18], (DEPTH, D, PEER_HEADS * PEER_QDIM), D ** -0.5),
        "peer_subkeys": nrm(ks[19], (DEPTH, 2, PEER_N_KEYS, PEER_QDIM // 2), (PEER_QDIM // 2) ** -0.5),
        "peer_u": nrm(ks[20], (DEPTH, PEER_EXPERTS, D), D ** -0.5),
        "peer_v": nrm(ks[21], (DEPTH, PEER_EXPERTS, D), PEER_HEADS ** -0.5),
        "final_norm_g": 1.0 + nrm(ks[22], (D,), 0.02),
    }

def first_block(x, c, positions, mod_w, mod_b, norm_g, gla_w_in, gla_w_g2, gla_b_g2, gla_norm_g,
              gla_w_out, kv_mod_w, kv_mod_b, kv_norm_g, kv_w, swa_w_q, swa_sinks, swa_w_out,
              peer_w_q, peer_subkeys, peer_u, peer_v, final_norm_g):
    n_a = DEPTH // 2
    cos, sin = rope_tables(positions)
    c_act = jax.nn.silu(c)
    k_sh, v_sh = None, None
    for l in range(DEPTH):
        mod = c_act @ mod_w[l] + mod_b[l]
        sh1, sc1, g1, sh2, sc2, g2 = jnp.split(mod, 6, axis=-1)
        h = modulate(x, norm_g[l, 0], sh1, sc1)
        if l < n_a:
            y = gla_mixer(h, gla_w_in[l], gla_w_g2[l], gla_b_g2[l], gla_norm_g[l], gla_w_out[l])
        else:
            j = l - n_a
            y = swa_sink_attention(h, swa_w_q[j], swa_sinks[j], swa_w_out[j], k_sh, v_sh, cos, sin)
        x = x + (g1[:, None, :] * y).astype(x.dtype)
        h = modulate(x, norm_g[l, 1], sh2, sc2)
        y = peer(h, peer_w_q[l], peer_subkeys[l], peer_u[l], peer_v[l])
        x = x + (g2[:, None, :] * y).astype(x.dtype)
        if l == n_a - 1:
            kv_mod = c_act @ kv_mod_w + kv_mod_b
            kv_shift, kv_scale = jnp.split(kv_mod, 2, axis=-1)
            k_sh, v_sh = shared_kv(modulate(x, kv_norm_g, kv_shift, kv_scale), kv_w, cos, sin)
    return rmsnorm(x, final_norm_g)


CHUNK = 64
Q_BLOCK = 128
D_FF = 4 * D_MODEL
A_HEADS = 4
A_DQK = 128
A_DV = D_MODEL // A_HEADS
B_HEADS = 8
B_NOPE = 128
B_ROPE = 64
B_VDIM = D_MODEL // B_HEADS
B_QLORA = 384
B_KVLORA = 256
ROPE_THETA_2 = 10000.0
N_A = DEPTH // 2
N_B = DEPTH - N_A
A_PROJ = A_HEADS * (2 * A_DQK + A_DV) + D_MODEL + 2 * A_HEADS


def rms_norm(x, g):
    xf = x.astype(jnp.float32)
    y = xf * lax.rsqrt(jnp.mean(xf * xf, axis=-1, keepdims=True) + EPS)
    return (y * g.astype(jnp.float32)).astype(x.dtype)

def modulate_2(h, shift, scale):
    return h * (1 + scale[:, None, :]) + shift[:, None, :]

def rope_tables_2(positions):
    inv = ROPE_THETA_2 ** (-jnp.arange(0, B_ROPE, 2, dtype=jnp.float32) / B_ROPE)
    ang = positions.astype(jnp.float32)[..., None] * inv
    return jnp.cos(ang), jnp.sin(ang)

def apply_rope(x, cos, sin):
    x1, x2 = jnp.split(x.astype(jnp.float32), 2, axis=-1)
    out = jnp.concatenate([x1 * cos - x2 * sin, x1 * sin + x2 * cos], axis=-1)
    return out.astype(x.dtype)

def sq_relu_mlp(h, w1, w2):
    return jnp.square(jax.nn.relu(h @ w1)) @ w2

def mlstm_chunkwise(q, k, v, i_pre, f_pre):
    Bn, S, H, dk = q.shape
    dv = v.shape[-1]
    nc = S // CHUNK
    f32 = jnp.float32

    def chunks(t):
        return t.astype(f32).reshape(Bn, nc, CHUNK, H, t.shape[-1]).transpose(1, 0, 3, 2, 4)

    def gchunks(t):
        return t.astype(f32).reshape(Bn, nc, CHUNK, H).transpose(1, 0, 3, 2)

    qc = chunks(q) * (dk ** -0.5)
    kc, vc = chunks(k), chunks(v)
    ic = gchunks(i_pre)
    bc = jnp.cumsum(jax.nn.log_sigmoid(gchunks(f_pre)), axis=-1)
    causal = jnp.tril(jnp.ones((CHUNK, CHUNK), dtype=bool))

    def step(carry, xs):
        C, n, m = carry
        qj, kj, vj, ij, bj = xs
        D = bj[..., :, None] - bj[..., None, :] + ij[..., None, :]
        D = jnp.where(causal, D, -jnp.inf)
        inter = bj + m[..., None]
        m_t = jnp.maximum(inter, jnp.max(D, axis=-1))
        w_inter = jnp.exp(inter - m_t)
        P = jnp.exp(D - m_t[..., None]) * jnp.einsum('bhld,bhsd->bhls', qj, kj)
        num = w_inter[..., None] * jnp.einsum('bhld,bhde->bhle', qj, C) + jnp.einsum('bhls,bhse->bhle', P, vj)
        den = w_inter * jnp.einsum('bhld,bhd->bhl', qj, n) + jnp.sum(P, axis=-1)
        h = num / jnp.maximum(jnp.abs(den), jnp.exp(-m_t))[..., None]
        b_last = bj[..., -1]
        g = b_last[..., None] - bj + ij
        m_new = jnp.maximum(b_last + m, jnp.max(g, axis=-1))
        decay = jnp.exp(b_last + m - m_new)
        wk = jnp.exp(g - m_new[..., None])
        C = decay[..., None, None] * C + jnp.einsum('bhs,bhsd,bhse->bhde', wk, kj, vj)
        n = decay[..., None] * n + jnp.einsum('bhs,bhsd->bhd', wk, kj)
        return (C, n, m_new), h

    init = (jnp.zeros((Bn, H, dk, dv), f32), jnp.zeros((Bn, H, dk), f32), jnp.zeros((Bn, H), f32))
    _, hs = lax.scan(step, init, (qc, kc, vc, ic, bc))
    return hs.transpose(1, 0, 3, 2, 4).reshape(Bn, S, H, dv).astype(q.dtype)

def mlstm_mixer(h, w_in, b_gates, head_norm, w_out):
    Bn, S, _ = h.shape
    sizes = [A_HEADS * A_DQK, A_HEADS * A_DQK, A_HEADS * A_DV, D_MODEL, A_HEADS, A_HEADS]
    idx = [int(s) for s in np.cumsum(sizes)[:-1]]
    q, k, v, o_pre, i_pre, f_pre = jnp.split(h @ w_in, idx, axis=-1)
    q = q.reshape(Bn, S, A_HEADS, A_DQK)
    k = k.reshape(Bn, S, A_HEADS, A_DQK)
    v = v.reshape(Bn, S, A_HEADS, A_DV)
    i_pre = i_pre + b_gates[:A_HEADS]
    f_pre = f_pre + b_gates[A_HEADS:]
    hh = mlstm_chunkwise(q, k, v, i_pre, f_pre)
    hh = rms_norm(hh, head_norm).reshape(Bn, S, D_MODEL)
    return (jax.nn.sigmoid(o_pre) * hh) @ w_out

def mla_shared_kv(x, c_act, kv_mod_w, kv_mod_b, kv_norm, w_dkv, kv_lora_norm, w_ukv, cos, sin):
    Bn, S, _ = x.shape
    shift, scale = jnp.split(c_act @ kv_mod_w + kv_mod_b, 2, axis=-1)
    hs = modulate_2(rms_norm(x, kv_norm), shift, scale)
    ckv, k_rope = jnp.split(hs @ w_dkv, [B_KVLORA], axis=-1)
    ckv = rms_norm(ckv, kv_lora_norm)
    kv = (ckv @ w_ukv).reshape(Bn, S, B_HEADS, B_NOPE + B_VDIM)
    k_nope, v = jnp.split(kv, [B_NOPE], axis=-1)
    k_rope = apply_rope(k_rope, cos, sin)
    return k_nope, k_rope, v

def mla_attention(q_nope, q_rope, k_nope, k_rope, v):
    Bn, S = q_nope.shape[:2]
    nb = S // Q_BLOCK
    scale = (B_NOPE + B_ROPE) ** -0.5
    key_chunk = jnp.arange(S) // CHUNK
    qn_b = q_nope.reshape(Bn, nb, Q_BLOCK, B_HEADS, B_NOPE).transpose(1, 0, 2, 3, 4)
    qr_b = q_rope.reshape(Bn, nb, Q_BLOCK, B_HEADS, B_ROPE).transpose(1, 0, 2, 3, 4)

    def block(args):
        qn, qr, blk = args
        s = jnp.einsum('bqhd,bkhd->bhqk', qn, k_nope) + jnp.einsum('bqhd,bkd->bhqk', qr, k_rope)
        s = s.astype(jnp.float32) * scale
        q_chunk = (blk * Q_BLOCK + jnp.arange(Q_BLOCK)) // CHUNK
        mask = key_chunk[None, :] <= q_chunk[:, None]
        p = jax.nn.softmax(jnp.where(mask, s, -jnp.inf), axis=-1).astype(v.dtype)
        return jnp.einsum('bhqk,bkhd->bqhd', p, v)

    out = lax.map(block, (qn_b, qr_b, jnp.arange(nb)))
    return out.transpose(1, 0, 2, 3, 4).reshape(Bn, S, B_HEADS * B_VDIM)

def mla_mixer(h, w_qa, q_norm, w_qb, w_o, k_nope, k_rope, v, cos, sin):
    Bn, S, _ = h.shape
    q = (rms_norm(h @ w_qa, q_norm) @ w_qb).reshape(Bn, S, B_HEADS, B_NOPE + B_ROPE)
    q_nope, q_rope = jnp.split(q, [B_NOPE], axis=-1)
    q_rope = apply_rope(q_rope, cos[:, :, None, :], sin[:, :, None, :])
    return mla_attention(q_nope, q_rope, k_nope, k_rope, v) @ w_o

def second_inputs(seed: int = 0) -> dict:
    key = jax.random.key(seed)
    ks = jax.random.split(key, 24)
    nrm = lambda k, shape, fan: jax.random.normal(k, shape, jnp.float32) * fan ** -0.5
    x = jax.random.normal(ks[0], (BATCH, SEQ, D_MODEL), jnp.float32)
    c = jax.random.normal(ks[1], (BATCH, D_MODEL), jnp.float32)
    offsets = jax.random.randint(ks[2], (BATCH, 1), 0, 64) * CHUNK
    positions = (offsets + jnp.arange(SEQ, dtype=jnp.int32)[None, :]).astype(jnp.int32)
    mod_w = nrm(ks[3], (DEPTH, D_MODEL, 6 * D_MODEL), D_MODEL) * 0.5
    mod_b = 0.01 * jax.random.normal(ks[4], (DEPTH, 6 * D_MODEL), jnp.float32)
    norm_g = 1.0 + 0.02 * jax.random.normal(ks[5], (DEPTH, 4, D_MODEL), jnp.float32)
    ffn_w1 = nrm(ks[6], (DEPTH, D_MODEL, D_FF), D_MODEL)
    ffn_w2 = nrm(ks[7], (DEPTH, D_FF, D_MODEL), D_FF)
    a_w_in = nrm(ks[8], (N_A, D_MODEL, A_PROJ), D_MODEL)
    i_bias = 0.1 * jax.random.normal(ks[9], (N_A, A_HEADS), jnp.float32)
    f_bias = jnp.linspace(3.0, 6.0, A_HEADS, dtype=jnp.float32)[None, :] + 0.1 * jax.random.normal(ks[10], (N_A, A_HEADS), jnp.float32)
    a_b_gates = jnp.concatenate([i_bias, f_bias], axis=-1)
    a_head_norm = 1.0 + 0.02 * jax.random.normal(ks[11], (N_A, A_HEADS, A_DV), jnp.float32)
    a_w_out = nrm(ks[12], (N_A, D_MODEL, D_MODEL), D_MODEL)
    b_w_qa = nrm(ks[13], (N_B, D_MODEL, B_QLORA), D_MODEL)
    b_q_norm = 1.0 + 0.02 * jax.random.normal(ks[14], (N_B, B_QLORA), jnp.float32)
    b_w_qb = nrm(ks[15], (N_B, B_QLORA, B_HEADS * (B_NOPE + B_ROPE)), B_QLORA)
    b_w_o = nrm(ks[16], (N_B, B_HEADS * B_VDIM, D_MODEL), B_HEADS * B_VDIM)
    kv_mod_w = nrm(ks[17], (D_MODEL, 2 * D_MODEL), D_MODEL) * 0.5
    kv_mod_b = 0.01 * jax.random.normal(ks[18], (2 * D_MODEL,), jnp.float32)
    kv_norm = 1.0 + 0.02 * jax.random.normal(ks[19], (D_MODEL,), jnp.float32)
    w_dkv = nrm(ks[20], (D_MODEL, B_KVLORA + B_ROPE), D_MODEL)
    kv_lora_norm = 1.0 + 0.02 * jax.random.normal(ks[21], (B_KVLORA,), jnp.float32)
    w_ukv = nrm(ks[22], (B_KVLORA, B_HEADS * (B_NOPE + B_VDIM)), B_KVLORA)
    return {"x": x, "c": c, "positions": positions, "mod_w": mod_w, "mod_b": mod_b, "norm_g": norm_g,
            "ffn_w1": ffn_w1, "ffn_w2": ffn_w2, "a_w_in": a_w_in, "a_b_gates": a_b_gates,
            "a_head_norm": a_head_norm, "a_w_out": a_w_out, "b_w_qa": b_w_qa, "b_q_norm": b_q_norm,
            "b_w_qb": b_w_qb, "b_w_o": b_w_o, "kv_mod_w": kv_mod_w, "kv_mod_b": kv_mod_b,
            "kv_norm": kv_norm, "w_dkv": w_dkv, "kv_lora_norm": kv_lora_norm, "w_ukv": w_ukv}

def second_block(x, c, positions, mod_w, mod_b, norm_g, ffn_w1, ffn_w2, a_w_in, a_b_gates, a_head_norm,
              a_w_out, b_w_qa, b_q_norm, b_w_qb, b_w_o, kv_mod_w, kv_mod_b, kv_norm, w_dkv,
              kv_lora_norm, w_ukv):
    cos, sin = rope_tables_2(positions)
    c_act = jax.nn.silu(c)
    k_nope = k_rope = v = None
    for layer in range(DEPTH):
        sh1, sc1, g1, sh2, sc2, g2 = jnp.split(c_act @ mod_w[layer] + mod_b[layer], 6, axis=-1)
        h = modulate_2(rms_norm(x, norm_g[layer, 0]), sh1, sc1)
        if layer < N_A:
            y = mlstm_mixer(h, a_w_in[layer], a_b_gates[layer], a_head_norm[layer], a_w_out[layer])
        else:
            if layer == N_A:
                k_nope, k_rope, v = mla_shared_kv(x, c_act, kv_mod_w, kv_mod_b, kv_norm, w_dkv,
                                                  kv_lora_norm, w_ukv, cos, sin)
            j = layer - N_A
            y = mla_mixer(h, b_w_qa[j], b_q_norm[j], b_w_qb[j], b_w_o[j], k_nope, k_rope, v, cos, sin)
        x = x + g1[:, None, :] * rms_norm(y, norm_g[layer, 1])
        h = modulate_2(rms_norm(x, norm_g[layer, 2]), sh2, sc2)
        y = sq_relu_mlp(h, ffn_w1[layer], ffn_w2[layer])
        x = x + g2[:, None, :] * rms_norm(y, norm_g[layer, 3])
    return x


def setup_inputs(seed=0):
    out = dict(first_inputs(seed))
    for name, value in second_inputs(seed + 1).items():
        if name != "x":
            out[name + "_2"] = value
    return out


def reference(
    x, c, positions, mod_w, mod_b, norm_g, gla_w_in, gla_w_g2, gla_b_g2, gla_norm_g, gla_w_out,
    kv_mod_w, kv_mod_b, kv_norm_g, kv_w, swa_w_q, swa_sinks, swa_w_out, peer_w_q, peer_subkeys,
    peer_u, peer_v, final_norm_g, c_2, positions_2, mod_w_2, mod_b_2, norm_g_2, ffn_w1_2,
    ffn_w2_2, a_w_in_2, a_b_gates_2, a_head_norm_2, a_w_out_2, b_w_qa_2, b_q_norm_2, b_w_qb_2,
    b_w_o_2, kv_mod_w_2, kv_mod_b_2, kv_norm_2, w_dkv_2, kv_lora_norm_2, w_ukv_2,
):
    x = first_block(
        x, c, positions, mod_w, mod_b, norm_g, gla_w_in, gla_w_g2, gla_b_g2, gla_norm_g,
        gla_w_out, kv_mod_w, kv_mod_b, kv_norm_g, kv_w, swa_w_q, swa_sinks, swa_w_out, peer_w_q,
        peer_subkeys, peer_u, peer_v, final_norm_g,
    )
    return second_block(
        x, c_2, positions_2, mod_w_2, mod_b_2, norm_g_2, ffn_w1_2, ffn_w2_2, a_w_in_2,
        a_b_gates_2, a_head_norm_2, a_w_out_2, b_w_qa_2, b_q_norm_2, b_w_qb_2, b_w_o_2,
        kv_mod_w_2, kv_mod_b_2, kv_norm_2, w_dkv_2, kv_lora_norm_2, w_ukv_2,
    )


_drawn_inputs = setup_inputs


def setup_inputs(seed=0):
    import zlib

    import numpy as np

    out = dict(_drawn_inputs(seed))
    spreads = {}
    factors = {'norm_g': 3.314,
     'gla_b_g2': 4.359,
     'gla_norm_g': 7.062,
     'kv_mod_b': 6.407,
     'kv_norm_g': 8.0,
     'swa_sinks': 8.0,
     'mod_b_2': 2.682,
     'norm_g_2': 3.094,
     'a_head_norm_2': 8.0,
     'b_q_norm_2': 8.0,
     'kv_mod_b_2': 8.0,
     'kv_norm_2': 8.0,
     'kv_lora_norm_2': 8.0}
    for name, (base, spread) in spreads.items():
        noise = np.random.default_rng([zlib.crc32(name.encode()), seed]).standard_normal(out[name].shape)
        drawn = base * np.exp(spread * noise) if base else spread * noise
        out[name] = __import__('jax').numpy.asarray(drawn.astype(out[name].dtype))
    for name, factor in factors.items():
        out[name] = (out[name] * factor).astype(out[name].dtype)
    return out
```

```python
from contextlib import ExitStack

import numpy as np

import concourse.bass as bass
from concourse import mybir
from concourse.alu_op_type import AluOpType as ALU

ACT = mybir.ActivationFunctionType
AX = mybir.AxisListType.X
F32 = mybir.dt.float32
I32 = mybir.dt.int32
U32 = mybir.dt.uint32

P = 128
D = 1024
DC = D // P
SEQ = 256
NT = SEQ // P
EPS = 1e-6
SLAB = 2048
RING = 4
BANK = 512
NEG = -1.0e30

H_GLA, DV = 4, 256
GATE_TAU = 16.0
CHUNK = 64
SWA_H, SWA_KV, SWA_D = 16, 4, 64
PEER_H, KEYS, TOPK = 8, 128, 16
N_EXP = KEYS * KEYS
HK = PEER_H * TOPK
LORA_Q, LORA_KV, NOPE, ROPE, MLA_H = 384, 256, 128, 64, 8
FF = 4096
ROT1, ROT2 = 8, 32

PLAN = [("gla_qk", 4), ("gla_v", 4), ("gla_og", 4), ("gla_out", 4),
        ("peer_q0", 8), ("u0", 64), ("v0", 64),
        ("kv", 2), ("swa_q", 4), ("swa_out", 4),
        ("peer_q1", 8), ("u1", 64), ("v1", 64),
        ("ml_qk", 4), ("ml_v", 4), ("ml_o", 4), ("ml_out", 4), ("ffn1_0", 16), ("ffn2_0", 16),
        ("qa", 2), ("dkv", 2), ("qb_nope", 2), ("qb_rope", 1), ("ukv_k", 1), ("ukv_v", 1),
        ("mla_out", 4), ("ffn1_1", 16), ("ffn2_1", 16)]
START = {}
N_SLABS = 0
for _name, _n in PLAN:
    START[_name] = N_SLABS
    N_SLABS += _n

STRIPS = 28
FIRST_STRIPS = 6
LOOP_STRIPS = 11
MOD1 = [0, 6]
KVMOD1 = 12
MOD2 = [14, 20]
KVMOD2 = 26
SH1, SC1, G1, SH2, SC2, G2 = range(6)

COLS = {}
N_COLS = 0
for _name, _n in [("c", 8), ("c2", 8), ("mod_b", STRIPS * 8), ("norm1", 32), ("kvn1", 8), ("fin", 8),
                  ("norm2", 64), ("kvn2", 8), ("b_g2", 4), ("qn", 3), ("kvl", 2), ("pos", 4)]:
    COLS[_name] = N_COLS
    N_COLS += _n
COLS_POS = COLS["pos"]
N_COLS -= 4

ROWS = {}
N_ROWS = 0
for _name, _n in [("sinks", 16), ("gates_b", 8), ("inv", ROT1 + ROT2), ("gla_norm", DV), ("head_norm", D)]:
    ROWS[_name] = N_ROWS
    N_ROWS += _n
N_ROWS_KEPT = ROWS["gla_norm"]

TWO_PI = 6.283185307179586
TWO_PI_A = 6.28125
TWO_PI_B = float(np.float32(round((TWO_PI - TWO_PI_A) * 2**21) / 2**21))
TWO_PI_C = float(np.float32(TWO_PI - TWO_PI_A - TWO_PI_B))


def build(nc, io, marks):
    new_marks = {}
    with ExitStack() as ctx:
        def sb(name, shape, dt=F32):
            return ctx.enter_context(nc.sbuf_tensor(name, shape, dt))

        def sem(name):
            return ctx.enter_context(nc.semaphore(name))

        gate = sb("gate", [P, KEYS * SEQ])
        ring = sb("ring", [P, RING, SLAB])
        x = sb("x", [P, NT, D])
        hT = sb("hT", [P, DC, SEQ])
        small = sb("small", [P, 4880])
        cols = sb("cols", [P, N_COLS])
        rows = sb("rows", [P, N_ROWS_KEPT])
        subk = sb("subk", [P, 2, 2, KEYS])
        w_gates = sb("w_gates", [P, DC, 8])
        modc = sb("modc", [P, STRIPS, 8])
        c_act = sb("c_act", [P, 16])
        scale_c = sb("scale_c", [P, 8])
        scale_c2 = sb("scale_c2", [P, 8])
        ident = sb("ident", [P, P])
        ones = sb("ones", [P, P])
        zeros = sb("zeros", [P, P])
        iota = sb("iota", [P, P])
        band = sb("band", [P, 2 * P])
        after = sb("after", [P, 2 * P])
        blockm = sb("blockm", [P, 2 * P])
        upper = sb("upper", [P, P])
        trig = sb("trig", [P, 2, NT, ROT1 + ROT2])
        stat = sb("stat", [P, 64])
        ps = ctx.enter_context(nc.psum_tensor("ps", [P, 8, BANK], F32))

        class Area:
            def __init__(self, buf, at=0):
                self.buf, self.at = buf, at

            def take(self, *shape):
                n = int(np.prod(shape))
                ap = self.buf[:, self.at:self.at + n]
                self.at += n
                if len(shape) == 2:
                    return ap.rearrange("p (a b) -> p a b", a=shape[0])
                if len(shape) == 3:
                    return ap.rearrange("p (a b c) -> p a b c", a=shape[0], b=shape[1])
                if len(shape) == 4:
                    return ap.rearrange("p (a b c d) -> p a b c d", a=shape[0], b=shape[1], c=shape[2])
                return ap

        def bc(ap, *shape):
            return ap.to_broadcast([P, *shape])

        common = Area(gate)
        xn = common.take(NT, D)
        row = common.take(D)
        diag = common.take(8, P)
        yT = common.take(DC, SEQ)
        LAYER = common.at

        vector_steps, scalar_steps, tensor_steps, gpsimd_steps = (
            sem("vector_steps"), sem("scalar_steps"), sem("tensor_steps"), sem("gpsimd_steps"))
        slab_landed = [sem(f"slab_landed{j}") for j in range(RING)]
        slab_used = sem("slab_used")
        sems = {"V": vector_steps, "A": scalar_steps, "T": tensor_steps, "G": gpsimd_steps, "S": slab_used}
        inputs_landed = sem("inputs_landed")
        gla_in_landed = sem("gla_inputs_landed")
        head_norm_landed = sem("head_norm_landed")
        first_mod_landed = [sem(f"first_mod_landed{k}") for k in range(DC)]
        first_mod_used = sem("first_mod_used")
        mod_landed = [sem("mod_landed0"), sem("mod_landed1")]
        mod_used = sem("mod_used")
        strip_added = sem("strip_added")
        strip_summed = sem("strip_summed")
        strip_stored = sem("strip_stored")
        u_drained = sem("u_drained")
        hot_rows, hot_cols = sem("hot_rows"), sem("hot_cols")
        second_copied = sem("second_copied")
        pool_paused = sem("gpsimd_paused")
        routes_full, routes_merged = sem("routes_full"), sem("routes_merged")
        out_written = sem("out_written")

        class Steps:
            def __init__(self, eng, key):
                self.eng, self.key, self.n, self.seen = eng, key, 0, {}

            def step(self, mark=None):
                self.n += 1
                if mark:
                    new_marks[mark] = (self.key, self.n)
                return 1

            def wait_ge(self, semaphore, value):
                if self.seen.get(id(semaphore), 0) < value:
                    self.seen[id(semaphore)] = value
                    self.eng.wait_ge(semaphore, value)

        def when(mark):
            key, value = marks.get(mark, ("V", 1))
            return sems[key], value

        def slab_done(s, mark=None):
            if mark:
                new_marks[mark] = ("S", s + 1)
            return 1

        def ps_reg(bank, col, n):
            return ps[:, bank, col:col + n]

        G0 = Area(gate, LAYER)
        gla_wgl = G0.take(DC, 16)
        gla_wg2 = G0.take(512)
        gla_ng = G0.take(DV)
        first_mod = G0.take(DC, D)
        first_acc = G0.take(2, D)
        ang = G0.take(NT, 40)
        angq = G0.take(NT, 40)
        GLA_AT = G0.at
        pos_i = sb("pos_i", [P, 4], I32)
        q_i = sb("q_i", [P, NT * 40], I32)

        def load_inputs_sync(sp):
            sp.dma_start(cols[:, :], io["cols"]).then_inc(inputs_landed, 16)
            sp.dma_start(rows[:, :], io["rows"][0, 0:N_ROWS_KEPT].partition_broadcast(P)).then_inc(inputs_landed, 16)
            sp.dma_start(pos_i[:, :], io["pos"]).then_inc(inputs_landed, 16)
            sp.dma_start(subk[:, :, :, :], io["subk"]).then_inc(inputs_landed, 16)
            sp.dma_start(w_gates[:, :, :], io["w_gates"]).then_inc(inputs_landed, 16)
            sp.dma_start(x[:, :, :], io["x"]).then_inc(inputs_landed, 16)
            sp.dma_start(gla_wgl, io["w_gl"]).then_inc(inputs_landed, 16)
            sp.dma_start(gla_wg2[0:16], io["w_g2"]).then_inc(inputs_landed, 16)
            sp.dma_start(gla_ng, io["rows"][0, ROWS["gla_norm"]:ROWS["gla_norm"] + DV].partition_broadcast(P)).then_inc(inputs_landed, 16)
        ALL_INPUTS = 9 * 16

        def col(name, i=0):
            return cols[:, COLS[name] + 8 * i:COLS[name] + 8 * i + 8]

        mod_acc = small[:, 4880 - D:]
        mod_slots = [hT[:, k * DC // 2:(k + 1) * DC // 2, :].rearrange("p a b -> p (a b)") for k in range(2)]

        def first_mod_loads(eng):
            for s in range(FIRST_STRIPS):
                for k in range(DC):
                    if s:
                        eng.wait_ge(first_mod_used, (s - 1) * DC + k + 1)
                    eng.dma_start(first_mod[:, k, :], io["mod"][s * DC + k]).then_inc(first_mod_landed[k], 16)

        def first_mod_vector(v):
            v.wait_ge(*when("c_act"))
            for s in range(FIRST_STRIPS):
                acc = first_acc[:, s % 2, :]
                if s >= 2:
                    v.wait_ge(*when(f"first_strip{s - 2}.sum"))
                for k in range(DC):
                    v.eng.wait_ge(first_mod_landed[k], 16 * (s + 1))
                    w = first_mod[:, k, :]
                    if k == 0:
                        ins = nc.vector.tensor_scalar(acc, w, c_act[:, 0:1], None, ALU.mult)
                    else:
                        v.eng.wait_ge(first_mod_used, s * DC + k)
                        ins = nc.vector.scalar_tensor_tensor(out=acc, in0=w, scalar=c_act[:, k:k + 1], in1=acc,
                                                             op0=ALU.mult, op1=ALU.add)
                    ins.then_inc(first_mod_used, 1)
                if s:
                    first_strip_store(v, s - 1)
            first_strip_store(v, FIRST_STRIPS - 1)

        def first_strip_store(v, s):
            v.wait_ge(*when(f"first_strip{s}.sum"))
            nc.vector.tensor_tensor(modc[:, s, :], ps_reg(s % 2, 0, 8),
                                    cols[:, COLS["mod_b"] + 8 * s:COLS["mod_b"] + 8 * s + 8], ALU.add) \
                .then_inc(vector_steps, v.step(f"first_strip{s}"))

        def strip_sum_tensor(acc, bank):
            for j in range(8):
                last = nc.tensor.matmul(ps[:, bank, j:j + 1], acc[:, j * P:(j + 1) * P], ones[:, 0:1],
                                        start=True, stop=True)
            return last

        def first_mod_tensor(t):
            t.wait_ge(*when("constants"))
            for s in range(FIRST_STRIPS):
                if s >= 2:
                    t.wait_ge(*when(f"first_strip{s - 2}"))
                t.eng.wait_ge(first_mod_used, (s + 1) * DC)
                strip_sum_tensor(first_acc[:, s % 2, :], s % 2).then_inc(tensor_steps, t.step(f"first_strip{s}.sum"))

        def loop_mod_scalar(a, s0):
            done = s0 - FIRST_STRIPS
            first = done == 0

            def strip(i, head):
                for k in range(DC):
                    if not (head and k < 2):
                        a.eng.wait_ge(mod_used, i * DC + (done * DC + k - 1))
                    a.eng.dma_start(mod_slots[k % 2], io["mod"][bass.ds(i * DC + (s0 * DC + k), 1), :, :]
                                    .rearrange("a p n -> (a p) n")).then_inc(mod_landed[k % 2], 16)
            if first:
                strip(0, True)
            with a.eng.Fori(1 if first else 0, LOOP_STRIPS) as i:
                strip(i, False)
            a.seen.clear()

        def strip_chunk_vector(v, i, s0, k, c0):
            done = s0 - FIRST_STRIPS
            v.eng.wait_ge(mod_landed[k % 2], i * 64 + (64 * done + 16 * (k // 2) + 16))
            if k == 0:
                ins = nc.vector.tensor_scalar(mod_acc, mod_slots[0], c_act[:, c0:c0 + 1], None, ALU.mult)
            else:
                v.eng.wait_ge(mod_used, i * DC + (done * DC + k))
                ins = nc.vector.scalar_tensor_tensor(out=mod_acc, in0=mod_slots[k % 2],
                                                     scalar=c_act[:, c0 + k:c0 + k + 1], in1=mod_acc,
                                                     op0=ALU.mult, op1=ALU.add)
            ins.then_inc(mod_used, 1)

        def strip_store_vector(v, i, s0):
            v.eng.wait_ge(strip_summed, i + (s0 - FIRST_STRIPS + 1))
            nc.vector.tensor_tensor(
                modc[:, bass.ds(i + s0, 1), :].rearrange("p a n -> p (a n)"), ps_reg(4, 0, 8),
                cols[:, bass.ds(i * 8 + (COLS["mod_b"] + 8 * s0), 8)], ALU.add).then_inc(strip_stored, 1)

        def row_from_col(v_or_t, name, source, bank, who):
            if who == "V":
                v = v_or_t
                v.wait_ge(vector_steps, v.n)
                nc.vector.tensor_tensor(diag, ident[:, :].unsqueeze(1).to_broadcast([P, 8, P]),
                                        source.unsqueeze(2).to_broadcast([P, 8, P]), ALU.mult) \
                    .then_inc(vector_steps, v.step(f"{name}.diag"))
            else:
                t = v_or_t
                t.wait_ge(*when(f"{name}.diag"))
                for mark in free[bank]:
                    t.wait_ge(*when(mark))
                for mark in free[bank + 1]:
                    t.wait_ge(*when(mark))
                for n in range(2):
                    nc.tensor.matmul(ps[:, bank + n, :], ones[:, :],
                                     diag[:, 4 * n:4 * n + 4, :].rearrange("p a b -> p (a b)"),
                                     start=True, stop=True).then_inc(tensor_steps, t.step(f"{name}.sum{n}"))
                    free[bank + n] = [f"{name}.row{n}"]

        def row_store(v, name, bank):
            for n in range(2):
                v.wait_ge(*when(f"{name}.sum{n}"))
                nc.vector.tensor_copy(row[:, n * BANK:(n + 1) * BANK], ps[:, bank + n, :]) \
                    .then_inc(vector_steps, v.step(f"{name}.row{n}"))

        free = {b: [] for b in range(8)}

        def junk(n, size):
            return xn.rearrange("p a b -> p (a b)")[:, n * size:(n + 1) * size]

        def stats_scalar(a, name, after, src=None, n=D, parts=NT):
            for mark in after:
                a.wait_ge(*when(mark))
            for i in range(parts):
                s = x[:, i, :] if src is None else src(i)
                nc.scalar.activation(junk(i, n), s, ACT.Square,
                                     accum_out=stat[:, i:i + 1]).then_inc(scalar_steps, a.step(f"{name}.ss"))

        def rstd_vector(v, name, n=D, parts=NT):
            v.wait_ge(*when(f"{name}.ss"))
            v.wait_ge(vector_steps, v.n)
            nc.vector.tensor_scalar(stat[:, 16:16 + parts], stat[:, 0:parts], 1.0 / n, EPS, ALU.mult, ALU.add) \
                .then_inc(vector_steps, v.step(f"{name}.var"))
            v.wait_ge(*when(f"{name}.std"))
            nc.vector.reciprocal(stat[:, 48:48 + parts], stat[:, 32:32 + parts]) \
                .then_inc(vector_steps, v.step(f"{name}.rstd"))
            v.wait_ge(vector_steps, v.n)

        def std_scalar(a, name, parts=NT):
            a.wait_ge(*when(f"{name}.var"))
            nc.scalar.activation(stat[:, 32:32 + parts], stat[:, 16:16 + parts], ACT.Sqrt) \
                .then_inc(scalar_steps, a.step(f"{name}.std"))

        def norm_scalar(a, name, after):
            stats_scalar(a, name, after)
            std_scalar(a, name)

        def norm_vector(v, name, gain, sc, sh):
            rstd_vector(v, name)
            for i in range(NT):
                nc.vector.tensor_scalar(xn[:, i, :], x[:, i, :], stat[:, 48 + i:49 + i], None, ALU.mult) \
                    .then_inc(vector_steps, v.step(f"{name}.xn{i}"))
            nc.vector.scalar_tensor_tensor(out=scale_c[:, :], in0=modc[:, sc, :], scalar=1.0, in1=gain,
                                           op0=ALU.add, op1=ALU.mult).then_inc(vector_steps, v.step())
            v.wait_ge(vector_steps, v.n)
            turned_vector(v, name, hT, lambda c: scale_c[:, c:c + 1], lambda c: modc[:, sh, c:c + 1])

        def turn_tensor(t, name, src, ready, bank=0, chunks=DC):
            for c in range(chunks):
                b = bank + c // 2
                if c % 2 == 0:
                    for mark in free[b]:
                        t.wait_ge(*when(mark))
                for i in range(NT):
                    for mark in ready(i, c):
                        t.wait_ge(*when(mark))
                    ins = nc.tensor.transpose(ps[:, b, (c % 2) * SEQ + i * P:(c % 2) * SEQ + (i + 1) * P],
                                              src(i, c), ident[:, :])
                if c % 2 or c == chunks - 1:
                    ins.then_inc(tensor_steps, t.step(f"{name}.turned{c // 2}"))
                    free[b] = [f"{name}.T{c}"]

        def turned_vector(v, name, dst, mul=None, add=None, bank=0, chunks=DC, out=None):
            for c in range(chunks):
                v.wait_ge(*when(f"{name}.turned{c // 2}"))
                src = ps[:, bank + c // 2, (c % 2) * SEQ:(c % 2 + 1) * SEQ]
                if mul is None:
                    ins = nc.vector.tensor_copy(dst[:, c, :], src)
                elif add is None:
                    ins = nc.vector.tensor_scalar(dst[:, c, :], src, mul(c), None, ALU.mult)
                else:
                    ins = nc.vector.tensor_scalar(dst[:, c, :], src, mul(c), add(c), ALU.mult, ALU.add)
                ins.then_inc(vector_steps, v.step(f"{out or name}.T{c}"))

        def norm_tensor(t, name):
            turn_tensor(t, name, lambda i, c: xn[:, i, c * P:(c + 1) * P], lambda i, c: [f"{name}.xn{i}"])

        def slab(t, s):
            t.eng.wait_ge(slab_landed[s % RING], 16 * (s // RING + 1))
            return ring[:, s % RING, :]

        def gemm_T(t, name, weights, blocks, chunks, src, ready, bank=0, nbanks=4):
            per = min(blocks, 4 if chunks == 3 else SLAB // (chunks * P))
            for b in range(blocks):
                s = START[weights] + b // per
                w = slab(t, s) if b % per == 0 else ring[:, s % RING, :]
                bk = bank + (b // 2) % nbanks
                if b % 2 == 0:
                    for mark in free[bk]:
                        t.wait_ge(*when(mark))
                for c in range(chunks):
                    for mark in ready(c):
                        t.wait_ge(*when(mark))
                    at = (b % per) * chunks * P + c * P
                    ins = nc.tensor.matmul(ps[:, bk, (b % 2) * SEQ:(b % 2 + 1) * SEQ], w[:, at:at + P], src[:, c, :],
                                           start=(c == 0), stop=(c == chunks - 1))
                if b % per == per - 1:
                    ins.then_inc(slab_used, slab_done(s, f"{name}.full{b // 2}"))
                elif b % 2:
                    ins.then_inc(tensor_steps, t.step(f"{name}.full{b // 2}"))
                if b % 2:
                    free[bk] = [f"{name}.out{b // 2}"]

        def gemm_M(t, name, weights, chunks, per, width, src, ready, bank=0):
            nbs = (width + BANK - 1) // BANK
            for nb in range(nbs):
                for i in range(NT):
                    for mark in free[bank + 2 * nb + i]:
                        t.wait_ge(*when(mark))
            for c in range(chunks):
                s = START[weights] + c // per
                w = slab(t, s) if c % per == 0 else ring[:, s % RING, :]
                for mark in ready(c):
                    t.wait_ge(*when(mark))
                for nb in range(nbs):
                    n = min(BANK, width - nb * BANK)
                    at = (c % per) * width + nb * BANK
                    for i in range(NT):
                        ins = nc.tensor.matmul(ps[:, bank + 2 * nb + i, 0:n], src[:, c, i * P:(i + 1) * P],
                                               w[:, at:at + n], start=(c == 0), stop=(c == chunks - 1))
                        if c == chunks - 1:
                            if (nb, i) != (nbs - 1, NT - 1):
                                ins.then_inc(tensor_steps, t.step(f"{name}.full{2 * nb + i}"))
                            free[bank + 2 * nb + i] = [f"{name}.out{2 * nb + i}"]
                if c == chunks - 1:
                    ins.then_inc(slab_used, slab_done(s, f"{name}.full{2 * nbs - 1}"))
                elif c % per == per - 1:
                    ins.then_inc(slab_used, slab_done(s))

        def residual_vector(v, name, ready, bank=0, scale=None):
            for nb in range(2):
                for i in range(NT):
                    b = bank + 2 * nb + i
                    cut = slice(nb * BANK, (nb + 1) * BANK)
                    v.wait_ge(*when(ready(nb, i)))
                    s = 1.0 if scale is None else scale(i)
                    nc.vector.scalar_tensor_tensor(out=xn[:, i, cut], in0=ps[:, b, :], scalar=s, in1=row[:, cut],
                                                   op0=ALU.mult, op1=ALU.mult) \
                        .then_inc(vector_steps, v.step(f"{name}.out{2 * nb + i}"))
            v.wait_ge(vector_steps, v.n)
            for i in range(NT):
                nc.vector.tensor_tensor(x[:, i, :], x[:, i, :], xn[:, i, :], ALU.add) \
                    .then_inc(vector_steps, v.step(f"{name}.x"))
            v.wait_ge(vector_steps, v.n)

        def constants_gpsimd(g):
            for buf, val in ((ident, 0.0), (ones, 1.0), (zeros, 0.0), (band, 0.0), (after, 0.0),
                             (blockm, 0.0), (upper, 1.0), (gmask_f, 1.0)):
                nc.gpsimd.memset(buf[:, :], val).then_inc(gpsimd_steps, g.step())
            nc.gpsimd.iota(iota[:, :], pattern=[[1, P]], base=0, channel_multiplier=0,
                           allow_small_or_imprecise_dtypes=True).then_inc(gpsimd_steps, g.step())
            g.wait_ge(gpsimd_steps, g.n)
            nc.gpsimd.affine_select(out=ident[:, :], in_=ident[:, :], compare_op=ALU.not_equal, fill=1.0, base=0,
                                    pattern=[[-1, P]], channel_multiplier=1).then_inc(gpsimd_steps, g.step())
            for m in (band, after):
                nc.gpsimd.affine_select(out=m[:, P:], in_=m[:, P:], compare_op=ALU.is_ge, fill=NEG, base=0,
                                        pattern=[[-1, P]], channel_multiplier=1).then_inc(gpsimd_steps, g.step())
            nc.gpsimd.affine_select(out=band[:, 0:P], in_=band[:, 0:P], compare_op=ALU.is_ge, fill=NEG, base=-1,
                                    pattern=[[1, P]], channel_multiplier=-1).then_inc(gpsimd_steps, g.step())
            nc.gpsimd.affine_select(out=upper[:, :], in_=upper[:, :], compare_op=ALU.is_ge, fill=0.0, base=0,
                                    pattern=[[1, P]], channel_multiplier=-1).then_inc(gpsimd_steps, g.step())
            nc.gpsimd.memset(blockm[0:CHUNK, P + CHUNK:], NEG).then_inc(gpsimd_steps, g.step())
            nc.gpsimd.affine_select(out=gmask_f[:, :], in_=gmask_f[:, :], compare_op=ALU.is_ge, fill=0.0, base=0,
                                    pattern=[[1, P]], channel_multiplier=-1).then_inc(gpsimd_steps, g.step())
            g.wait_ge(gpsimd_steps, g.n)
            nc.gpsimd.memset(gmask_f[0:CHUNK, CHUNK:P], 0.0).then_inc(gpsimd_steps, g.step("constants"))

        def trig_vector(v):
            v.eng.wait_ge(inputs_landed, ALL_INPUTS)
            posf = stat[:, 56:60]
            nc.vector.tensor_copy(posf, pos_i[:, :]).then_inc(vector_steps, v.step())
            v.wait_ge(vector_steps, v.n)
            inv = rows[:, ROWS["inv"]:ROWS["inv"] + 40]
            for i in range(NT):
                for (k, a, b) in ((0, 0, ROT1), (1, ROT1, ROT1 + ROT2)):
                    nc.vector.tensor_scalar(ang[:, i, a:b], inv[:, a:b], posf[:, 2 * k + i:2 * k + i + 1], None,
                                            ALU.mult).then_inc(vector_steps, v.step())
            v.wait_ge(vector_steps, v.n)
            af = ang.rearrange("p a b -> p (a b)")
            qf = angq.rearrange("p a b -> p (a b)")
            nc.vector.tensor_scalar(qf, af, 1.0 / TWO_PI, None, ALU.mult).then_inc(vector_steps, v.step())
            v.wait_ge(vector_steps, v.n)
            nc.vector.tensor_copy(q_i[:, :], qf).then_inc(vector_steps, v.step())
            v.wait_ge(vector_steps, v.n)
            nc.vector.tensor_copy(qf, q_i[:, :]).then_inc(vector_steps, v.step())
            v.wait_ge(vector_steps, v.n)
            for part in (TWO_PI_A, TWO_PI_B, TWO_PI_C):
                nc.vector.scalar_tensor_tensor(out=af, in0=qf, scalar=-part, in1=af, op0=ALU.mult, op1=ALU.add) \
                    .then_inc(vector_steps, v.step())
                v.wait_ge(vector_steps, v.n)

            def fold(dst):
                for cmp, lim, add in ((ALU.is_gt, TWO_PI / 2, -TWO_PI), (ALU.is_lt, -TWO_PI / 2, TWO_PI)):
                    nc.vector.tensor_scalar(qf, dst, lim, add, cmp, ALU.mult).then_inc(vector_steps, v.step())
                    v.wait_ge(vector_steps, v.n)
                    nc.vector.tensor_tensor(dst, dst, qf, ALU.add).then_inc(vector_steps, v.step())
                    v.wait_ge(vector_steps, v.n)
                nc.vector.tensor_scalar(dst, dst, 3.1415925, -3.1415925, ALU.min, ALU.max) \
                    .then_inc(vector_steps, v.step())
                v.wait_ge(vector_steps, v.n)
            ts = trig[:, 0, :, :].rearrange("p a b -> p (a b)")
            tc = trig[:, 1, :, :].rearrange("p a b -> p (a b)")
            fold(af)
            nc.vector.tensor_copy(ts, af).then_inc(vector_steps, v.step())
            nc.vector.tensor_scalar(tc, af, TWO_PI / 4, None, ALU.add).then_inc(vector_steps, v.step())
            v.wait_ge(vector_steps, v.n)
            fold(tc)
            nc.vector.tensor_copy(qf, tc).then_inc(vector_steps, v.step("angles"))

        def trig_scalar(a):
            a.wait_ge(*when("angles"))
            ts = trig[:, :, :, :].rearrange("p q a b -> p (q a b)")
            nc.scalar.activation(ts, ts, ACT.Sin).then_inc(scalar_steps, a.step("trig"))

        S1 = Area(gate, GLA_AT)
        q = S1.take(H_GLA, SEQ)
        k = S1.take(H_GLA, SEQ)
        b_ = S1.take(H_GLA, SEQ)
        e_pos = S1.take(H_GLA, SEQ)
        e_neg = S1.take(H_GLA, SEQ)
        e_dec = S1.take(H_GLA, SEQ)
        kd = S1.take(NT, H_GLA, P)
        q_own = S1.take(H_GLA, NT, 2, P)
        sc_T = S1.take(NT, H_GLA, P)
        state = S1.take(3, H_GLA, DV)
        glT = S1.take(SEQ)
        gmask_f = S1.take(P)
        assert S1.at <= KEYS * SEQ
        o_, v_, og = (first_mod[:, 2 * n:2 * n + 2, :] for n in range(3))
        b_flat = b_.rearrange("p a b -> p (a b)")
        NCH = SEQ // CHUNK

        def gla_tensor(t):
            gemm_T(t, "gla_qk", "gla_qk", 8, DC, hT, lambda c: [f"n1.T{c}"])
            for mark in free[4]:
                t.wait_ge(*when(mark))
            for c in range(DC):
                ins = nc.tensor.matmul(ps[0:16, 4, 0:SEQ], gla_wgl[:, c, :], hT[:, c, :], start=(c == 0), stop=(c == DC - 1))
            ins.then_inc(tensor_steps, t.step("gl.full"))
            gemm_z(t)
            gemm_M(t, "gla_v", "gla_v", DC, 2, D, hT, lambda c: [], bank=0)
            for i in range(NT):
                for mark in free[4 + i]:
                    t.wait_ge(*when(mark))
                t.wait_ge(*when("gla.kd_T"))
                for h in range(H_GLA):
                    ins = nc.tensor.transpose(ps[:, 4 + i, h * P:(h + 1) * P], kdT[:, h, i * P:(i + 1) * P], ident[:, :])
                ins.then_inc(tensor_steps, t.step(f"gla.kd_turned{i}"))
                free[4 + i] = [f"gla.kd{i}"]
            for i in range(NT):
                for mark in free[6 + i]:
                    t.wait_ge(*when(mark))
                t.wait_ge(*when("gla.kt"))
                for h in range(H_GLA):
                    ins = nc.tensor.matmul(ps[:, 6 + i, h * P:(h + 1) * P], kt[:, h, i * P:(i + 1) * P],
                                           q[:, h, i * P:(i + 1) * P], start=True, stop=True)
                ins.then_inc(tensor_steps, t.step(f"gla.scores{i}"))
                free[6 + i] = [f"gla.masked{i}"]
            gemm_M(t, "gla_og", "gla_og", DC, 2, D, hT, lambda c: [], bank=0)
            for n in range(NCH - 1):
                i, lo = n // 2, (n % 2) * CHUNK
                bk = 4 + 2 * (n % 2)
                for mark in free[bk]:
                    t.wait_ge(*when(mark))
                for mark in free[bk + 1]:
                    t.wait_ge(*when(mark))
                t.wait_ge(*when(f"gla.kd{i}"))
                t.wait_ge(*when(f"gla_v.out{i}"))
                t.wait_ge(*when(f"gla_v.out{2 + i}"))
                for h in range(H_GLA):
                    ins = nc.tensor.matmul(ps[:, bk + h // 2, (h % 2) * DV:(h % 2 + 1) * DV],
                                           kd[lo:lo + CHUNK, i, h, :], v_[lo:lo + CHUNK, i, h * DV:(h + 1) * DV],
                                           start=True, stop=True)
                ins.then_inc(tensor_steps, t.step(f"gla.kv{n}"))
                free[bk] = free[bk + 1] = [f"gla.state{n}"]
            for i in range(NT):
                t.wait_ge(*when(f"gla.masked{i}"))
                t.wait_ge(*when("gla.q_own"))
                for g in range(2):
                    bk = (0 if i == 0 else 2) + g
                    for mark in free[bk]:
                        t.wait_ge(*when(mark))
                    for h in (2 * g, 2 * g + 1):
                        o = ps[:, bk, (h % 2) * DV:(h % 2 + 1) * DV]
                        srcs = [n for n in (2 * i, 2 * i + 1) if n > 0]
                        nc.tensor.matmul(o, sc_T[:, i, h, :], v_[:, i, h * DV:(h + 1) * DV], start=True, stop=False)
                        for n in srcs:
                            t.wait_ge(*when(f"gla.state{n - 1}"))
                            ins = nc.tensor.matmul(o, q_own[:, h, i, n % 2, :], state[:, n - 1, h, :],
                                                   start=False, stop=(n == srcs[-1]))
                    ins.then_inc(tensor_steps, t.step(f"gla.o{i}{g}"))
                    free[bk] = [f"gla.oc{i}{g}"]
            turn_tensor(t, "gla.on", lambda i, c: o_[:, i, c * P:(c + 1) * P], lambda i, c: [f"gla.gated{i}"], bank=4)
            row_from_col(t, "g1_0", None, 0, "T")
            gemm_M(t, "gla_out", "gla_out", DC, 2, D, yT, lambda c: [f"gla.on.T{c}"], bank=0)

        kdT, kt = e_dec, k

        def gemm_z(t):
            t.wait_ge(*when("glT"))
            for h in range(H_GLA):
                for mark in free[5 + h // 2]:
                    t.wait_ge(*when(mark))
                ins = nc.tensor.matmul(ps[:, 5 + h // 2, (h % 2) * SEQ:(h % 2 + 1) * SEQ],
                                       gla_wg2[0:16, h * P:(h + 1) * P], glT[0:16, :], start=True, stop=True)
                if h % 2:
                    ins.then_inc(tensor_steps, t.step(f"z.full{h // 2}"))
            free[5], free[6] = ["gla.z"], ["gla.z"]
            free[4] = ["glT"]

        def gla_scalar(a):
            for g in range(4):
                a.wait_ge(*when(f"gla_qk.full{g}"))
                dst = (q if g < 2 else k)[:, 2 * (g % 2):2 * (g % 2) + 2, :].rearrange("p a b -> p (a b)")
                nc.scalar.activation(dst, ps[:, g, :], ACT.Copy).then_inc(scalar_steps, a.step(f"gla_qk.out{g}"))
            a.wait_ge(*when("gl.full"))
            nc.scalar.activation(glT[0:16, :], ps[0:16, 4, 0:SEQ], ACT.Copy).then_inc(scalar_steps, a.step("glT"))
            a.wait_ge(*when("gla.z"))
            ep = e_pos.rearrange("p a b -> p (a b)")
            nc.scalar.activation(ep, b_flat, ACT.Abs).then_inc(scalar_steps, a.step())
            a.wait_ge(scalar_steps, a.n)
            nc.scalar.activation(ep, ep, ACT.Exp, scale=-1.0).then_inc(scalar_steps, a.step())
            a.wait_ge(scalar_steps, a.n)
            nc.scalar.activation(ep, ep, ACT.Ln, bias=1.0).then_inc(scalar_steps, a.step("gla.ln"))
            for g in range(4):
                a.wait_ge(*when(f"gla_v.full{g}"))
                nc.scalar.activation(v_[:, g % 2, (g // 2) * BANK:(g // 2 + 1) * BANK], ps[:, g, :], ACT.Copy) \
                    .then_inc(scalar_steps, a.step(f"gla_v.out{g}"))
            a.wait_ge(*when("gla.b"))
            nc.scalar.activation(ep, b_flat, ACT.Exp).then_inc(scalar_steps, a.step("gla.e_pos"))
            nc.scalar.activation(e_neg.rearrange("p a b -> p (a b)"), b_flat, ACT.Exp, scale=-1.0) \
                .then_inc(scalar_steps, a.step("gla.e_neg"))
            a.wait_ge(*when("gla.bdec"))
            nc.scalar.activation(e_dec.rearrange("p a b -> p (a b)"), e_dec.rearrange("p a b -> p (a b)"), ACT.Exp) \
                .then_inc(scalar_steps, a.step("gla.e_dec"))
            for i in range(NT):
                a.wait_ge(*when(f"gla.kd_turned{i}"))
                nc.scalar.activation(kd[:, i, :, :].rearrange("p a b -> p (a b)"), ps[:, 4 + i, :], ACT.Copy) \
                    .then_inc(scalar_steps, a.step(f"gla.kd{i}"))
            for g in range(4):
                a.wait_ge(*when(f"gla_og.full{g}"))
                nc.scalar.activation(og[:, g % 2, (g // 2) * BANK:(g // 2 + 1) * BANK], ps[:, g, :], ACT.Silu) \
                    .then_inc(scalar_steps, a.step(f"gla_og.out{g}"))
            for i in range(NT):
                for g in range(2):
                    bk = 2 * i + g
                    a.wait_ge(*when(f"gla.o{i}{g}"))
                    for h in (2 * g, 2 * g + 1):
                        nc.scalar.activation(junk(4 * i + h, DV), ps[:, bk, (h % 2) * DV:(h % 2 + 1) * DV], ACT.Square,
                                             accum_out=stat[:, 4 * i + h:4 * i + h + 1]) \
                            .then_inc(scalar_steps, a.step("gla.r.ss"))
                    nc.scalar.activation(o_[:, i, g * BANK:(g + 1) * BANK], ps[:, bk, :], ACT.Copy) \
                        .then_inc(scalar_steps, a.step(f"gla.oc{i}{g}"))
            std_scalar(a, "gla.r", 8)

        def gla_vector(v):
            for h in range(H_GLA):
                v.wait_ge(*when(f"z.full{h // 2}"))
                nc.vector.tensor_scalar(b_[:, h, :], ps[:, 5 + h // 2, (h % 2) * SEQ:(h % 2 + 1) * SEQ],
                                        cols[:, COLS["b_g2"] + h:COLS["b_g2"] + h + 1], None, ALU.add) \
                    .then_inc(vector_steps, v.step("gla.z"))
            v.wait_ge(vector_steps, v.n)
            ep = e_pos.rearrange("p a b -> p (a b)")
            en = e_neg.rearrange("p a b -> p (a b)")
            v.wait_ge(*when("gla.ln"))
            nc.vector.scalar_tensor_tensor(out=en, in0=b_flat, scalar=0.0, in1=ep, op0=ALU.min, op1=ALU.subtract) \
                .then_inc(vector_steps, v.step())
            v.wait_ge(vector_steps, v.n)
            nc.vector.tensor_scalar(en, en, 1.0 / GATE_TAU, None, ALU.mult).then_inc(vector_steps, v.step())
            restart = e_dec.rearrange("p a b -> p (a b)")
            nc.vector.memset(restart, 1.0).then_inc(vector_steps, v.step())
            v.wait_ge(vector_steps, v.n)
            nc.vector.memset(restart.rearrange("p (n c) -> p n c", c=CHUNK)[:, :, 0:1], 0.0) \
                .then_inc(vector_steps, v.step())
            v.wait_ge(vector_steps, v.n)
            nc.vector.tensor_tensor_scan(b_flat, restart, en, 0.0, ALU.mult, ALU.add) \
                .then_inc(vector_steps, v.step("gla.b"))
            v.wait_ge(vector_steps, v.n)
            b4 = b_flat.rearrange("p (n c) -> p n c", c=CHUNK)
            nc.vector.tensor_tensor(restart.rearrange("p (n c) -> p n c", c=CHUNK),
                                    b4[:, :, CHUNK - 1:CHUNK].to_broadcast([P, H_GLA * NCH, CHUNK]), b4,
                                    ALU.subtract).then_inc(vector_steps, v.step("gla.bdec"))
            qf, kf = q.rearrange("p a b -> p (a b)"), k.rearrange("p a b -> p (a b)")
            v.wait_ge(*when("gla_qk.out3"))
            v.wait_ge(*when("gla.e_pos"))
            nc.vector.scalar_tensor_tensor(out=qf, in0=qf, scalar=float(P) ** -0.5, in1=ep,
                                           op0=ALU.mult, op1=ALU.mult).then_inc(vector_steps, v.step())
            v.wait_ge(*when("gla.e_dec"))
            nc.vector.tensor_tensor(restart, kf, restart, ALU.mult).then_inc(vector_steps, v.step("gla.kd_T"))
            nc.vector.tensor_tensor(kf, kf, en, ALU.mult).then_inc(vector_steps, v.step("gla.kt"))
            qo = q_own.rearrange("p a b c d -> p (a b c d)")
            nc.vector.memset(qo, 0.0).then_inc(vector_steps, v.step())
            v.wait_ge(vector_steps, v.n)
            for n in range(2):
                for i in range(NT):
                    nc.vector.tensor_copy(q_own[:, :, i, n, n * CHUNK:(n + 1) * CHUNK],
                                          q[:, :, i * P + n * CHUNK:i * P + (n + 1) * CHUNK]) \
                        .then_inc(vector_steps, v.step("gla.q_own"))
            for i in range(NT):
                st = sc_T[:, i, :, :]
                nc.vector.memset(st.rearrange("p a b -> p (a b)"), 0.0).then_inc(vector_steps, v.step())
                v.wait_ge(vector_steps, v.n)
                v.wait_ge(*when(f"gla.scores{i}"))
                nc.vector.copy_predicated(st, gmask_f.bitcast(U32).unsqueeze(1).to_broadcast([P, H_GLA, P]),
                                          ps[:, 6 + i, :].rearrange("p (a b) -> p a b", a=H_GLA)) \
                    .then_inc(vector_steps, v.step(f"gla.masked{i}"))
            for n in range(NCH - 1):
                bk = 4 + 2 * (n % 2)
                v.wait_ge(*when(f"gla.kv{n}"))
                for h in range(H_GLA):
                    src = ps[:, bk + h // 2, (h % 2) * DV:(h % 2 + 1) * DV]
                    if n == 0:
                        ins = nc.vector.tensor_copy(state[:, 0, h, :], src)
                    else:
                        at = (n + 1) * CHUNK - 1
                        ins = nc.vector.scalar_tensor_tensor(out=state[:, n, h, :], in0=state[:, n - 1, h, :],
                                                             scalar=e_pos[:, h, at:at + 1], in1=src,
                                                             op0=ALU.mult, op1=ALU.add)
                    ins.then_inc(vector_steps, v.step(f"gla.state{n}"))
                v.wait_ge(vector_steps, v.n)
            v.wait_ge(*when("gla_og.out3"))
            nc.vector.tensor_tensor(og.rearrange("p a (h e) -> p (a h) e", e=DV),
                                    og.rearrange("p a (h e) -> p (a h) e", e=DV),
                                    gla_ng.unsqueeze(1).to_broadcast([P, NT * H_GLA, DV]), ALU.mult) \
                .then_inc(vector_steps, v.step())
            rstd_vector(v, "gla.r", DV, 8)
            for i in range(NT):
                v.wait_ge(*when(f"gla.oc{i}0"))
                v.wait_ge(*when(f"gla.oc{i}1"))
                for h in range(H_GLA):
                    cut = slice(h * DV, (h + 1) * DV)
                    nc.vector.scalar_tensor_tensor(out=o_[:, i, cut], in0=o_[:, i, cut],
                                                   scalar=stat[:, 48 + 4 * i + h:49 + 4 * i + h], in1=og[:, i, cut],
                                                   op0=ALU.mult, op1=ALU.mult) \
                        .then_inc(vector_steps, v.step(f"gla.gated{i}"))
            row_from_col(v, "g1_0", modc[:, MOD1[0] + G1, :], 0, "V")
            turned_vector(v, "gla.on", yT, bank=4)
            row_store(v, "g1_0", 0)
            v.wait_ge(vector_steps, v.n)
            residual_vector(v, "gla_out", lambda nb, i: f"gla_out.full{2 * nb + i}")

        SCORES = 112 * SEQ
        scores = gate[:, SCORES:].rearrange("p (t g n) -> p t g n", t=NT, g=2 * PEER_H)
        peer_qT = gate[:, LAYER:LAYER + 2 * PEER_H * SEQ].rearrange("p (g n) -> p g n", g=2 * PEER_H)
        A = Area(small)
        e_sel = A.take(3, NT, HK)
        top_v = A.take(2 * PEER_H, TOPK)
        top_if = A.take(2 * PEER_H, TOPK)
        top_i = A.take(2 * PEER_H * TOPK).bitcast(U32).rearrange("p (a b) -> p a b", b=TOPK)
        cand = A.take(TOPK * TOPK)
        cand2 = A.take(TOPK * TOPK)
        c_i = A.take(HK).bitcast(U32)
        c_part = A.take(HK).bitcast(U32)
        c_pf = A.take(HK)
        match = A.take(4, TOPK, TOPK)
        s_left = cand2[:, 0:KEYS]
        assert A.at <= 4880
        B = Area(small)
        selT = B.take(3, SEQ)
        hot_c = [B.take(8, KEYS) for _ in range(2)]
        hot_r = [B.take(8, KEYS // 2) for _ in range(2)]
        second = B.take(16)
        assert B.at <= 4880 - D

        def peer_score_tensor(t, l):
            gemm_T(t, f"pq{l}", f"peer_q{l}", 2 * PEER_H, DC, hT, lambda c: [f"n2_{l}.T{c}"], bank=0, nbanks=4)
            for i in range(NT):
                for g in range(2 * PEER_H):
                    bk = 4 + (4 * i + g // 4) % 4
                    if g % 4 == 0:
                        for mark in free[bk]:
                            t.wait_ge(*when(mark))
                        t.wait_ge(*when(f"pq{l}.out{min(7, 2 * (g // 4) + 1)}"))
                    ins = nc.tensor.matmul(ps[:, bk, (g % 4) * KEYS:(g % 4 + 1) * KEYS], peer_qT[:, g, i * P:(i + 1) * P],
                                           subk[:, l, g % 2, :], start=True, stop=True)
                    if g % 4 == 3:
                        ins.then_inc(tensor_steps, t.step(f"sc{l}.full{i}{g // 4}"))
                        free[bk] = [f"sc{l}.out{i}{g // 4}"]
            for b in range(4):
                for mark in free[b]:
                    t.wait_ge(*when(mark))
            base = START[f"u{l}"]

            def u_slab(i, j):
                s = base + j
                t.eng.wait_ge(slab_landed[s % RING], i * 16 + 16 * (s // RING + 1))
                t.eng.wait_ge(u_drained, i * 4 + (l * 68 + j + 1))
                for e in range(2):
                    for c in range(DC):
                        at = e * D + c * P
                        ins = nc.tensor.matmul(ps[:, j, e * SEQ:(e + 1) * SEQ], ring[:, s % RING, at:at + P],
                                               hT[:, c, :], start=(c == 0), stop=(c == DC - 1))
                ins.then_inc(slab_used, 1)

            with t.eng.Fori(0, 7) as i:
                for j in range(RING):
                    u_slab(i, j)
            for j in range(3):
                u_slab(7, j)
            peer_turn_tensor(t, l)
            u_slab(7, 3)
            if l == 0:
                for j in range(RING):
                    routes_group_tensor(t, 2 * l, 0, j, True)
                    u_slab(8, j)
            with t.eng.Fori(9 if l == 0 else 8, 16) as i:
                for j in range(RING):
                    routes_group_tensor(t, 2 * l, i - 8, j, False)
                    u_slab(i, j)
            t.seen.clear()

        def peer_score_scalar(a, l):
            for g in range(8):
                a.wait_ge(*when(f"pq{l}.full{g}"))
                nc.scalar.activation(peer_qT[:, 2 * g:2 * g + 2, :].rearrange("p a b -> p (a b)"),
                                     ps[:, g % 4, :], ACT.Copy).then_inc(scalar_steps, a.step(f"pq{l}.out{g}"))
            for i in range(NT):
                for g in range(4):
                    a.wait_ge(*when(f"sc{l}.full{i}{g}"))
                    nc.scalar.activation(scores[:, i, 4 * g:4 * g + 4, :].rearrange("p a b -> p (a b)"),
                                         ps[:, 4 + g, :], ACT.Copy).then_inc(scalar_steps, a.step(f"sc{l}.out{i}{g}"))
            for j in range(4):
                nc.scalar.activation(stat[:, 60 + j:61 + j], zeros[:, 0:1], ACT.Copy).then_inc(u_drained, 1)

            def drain(i, j):
                a.eng.wait_ge(slab_used, i * 4 + (START[f"u{l}"] + j + 1))
                nc.scalar.activation(gate[:, bass.ds(i * (8 * SEQ) + 2 * j * SEQ, 2 * SEQ)] if not isinstance(i, int)
                                     else gate[:, i * 8 * SEQ + 2 * j * SEQ:i * 8 * SEQ + 2 * (j + 1) * SEQ],
                                     ps[:, j, :], ACT.Gelu).then_inc(u_drained, 1)
            with a.eng.Fori(0, 7) as i:
                for j in range(4):
                    drain(i, j)
            a.seen.clear()
            a.wait_ge(*when(f"chosen{l}"))
            w = e_sel[:, 2, :, :].rearrange("p a b -> p (a b)")
            nc.scalar.activation(w, w, ACT.Exp).then_inc(scalar_steps, a.step(f"weights{l}.exp"))
            with a.eng.Fori(7, 16) as i:
                for j in range(4):
                    drain(i, j)
            a.seen.clear()

        def top16(v, src, left, vals, idx):
            nc.vector.max(vals[:, 0:8], src).then_inc(vector_steps, v.step())
            v.wait_ge(vector_steps, v.n)
            nc.vector.max_index(idx[:, 0:8], vals[:, 0:8], src).then_inc(vector_steps, v.step())
            nc.vector.match_replace(left, vals[:, 0:8], src, -3.0e38).then_inc(vector_steps, v.step())
            v.wait_ge(vector_steps, v.n)
            nc.vector.max(vals[:, 8:16], left).then_inc(vector_steps, v.step())
            v.wait_ge(vector_steps, v.n)
            nc.vector.max_index(idx[:, 8:16], vals[:, 8:16], left).then_inc(vector_steps, v.step())

        def peer_choose_vector(v, l):
            for i in range(NT):
                for g in range(4):
                    v.wait_ge(*when(f"sc{l}.out{i}{g}"))
                for g in range(2 * PEER_H):
                    top16(v, scores[:, i, g, :], s_left, top_v[:, g, :], top_i[:, g, :])
                v.wait_ge(vector_steps, v.n)
                nc.vector.tensor_copy(top_if, top_i).then_inc(vector_steps, v.step())
                for h in range(PEER_H):
                    v.wait_ge(vector_steps, v.n)
                    nc.vector.tensor_tensor(
                        cand.rearrange("p (a b) -> p a b", a=TOPK),
                        top_v[:, 2 * h, :].unsqueeze(2).to_broadcast([P, TOPK, TOPK]),
                        top_v[:, 2 * h + 1, :].unsqueeze(1).to_broadcast([P, TOPK, TOPK]), ALU.add) \
                        .then_inc(vector_steps, v.step())
                    v.wait_ge(vector_steps, v.n)
                    top16(v, cand, cand2, e_sel[:, 2, i, h * TOPK:(h + 1) * TOPK], c_i[:, h * TOPK:(h + 1) * TOPK])
                v.wait_ge(vector_steps, v.n)
                for part, (op, n) in enumerate(((ALU.logical_shift_right, 4), (ALU.bitwise_and, 15))):
                    nc.vector.tensor_scalar(c_part, c_i, n, None, op).then_inc(vector_steps, v.step())
                    v.wait_ge(vector_steps, v.n)
                    nc.vector.tensor_copy(c_pf, c_part).then_inc(vector_steps, v.step())
                    v.wait_ge(vector_steps, v.n)
                    for hh in range(2):
                        cut = slice(hh * 64, hh * 64 + 64)
                        for h in range(4):
                            hg = 4 * hh + h
                            nc.vector.tensor_tensor(
                                match[:, h, :, :],
                                c_pf[:, hg * TOPK:(hg + 1) * TOPK].unsqueeze(2).to_broadcast([P, TOPK, TOPK]),
                                iota[:, 0:TOPK].unsqueeze(1).to_broadcast([P, TOPK, TOPK]), ALU.is_equal) \
                                .then_inc(vector_steps, v.step())
                        v.wait_ge(vector_steps, v.n)
                        for h in range(4):
                            hg = 4 * hh + h
                            nc.vector.tensor_tensor(
                                match[:, h, :, :], match[:, h, :, :],
                                top_if[:, 2 * hg + part, :].unsqueeze(1).to_broadcast([P, TOPK, TOPK]), ALU.mult) \
                                .then_inc(vector_steps, v.step())
                        v.wait_ge(vector_steps, v.n)
                        nc.vector.tensor_reduce(e_sel[:, part, i, cut], match.rearrange("p a b c -> p (a b) c"),
                                                AX, ALU.add).then_inc(vector_steps, v.step())
                        v.wait_ge(vector_steps, v.n)
            w = e_sel[:, 2, :, :].rearrange("p t (h k) -> p (t h) k", k=TOPK)
            big = stat[:, 0:NT * PEER_H]
            nc.vector.tensor_copy(big.unsqueeze(2), w[:, :, 0:1]).then_inc(vector_steps, v.step())
            v.wait_ge(vector_steps, v.n)
            nc.vector.tensor_tensor(w, w, big.unsqueeze(2).to_broadcast([P, NT * PEER_H, TOPK]), ALU.subtract) \
                .then_inc(vector_steps, v.step(f"chosen{l}"))
            v.wait_ge(*when(f"weights{l}.exp"))
            nc.vector.tensor_reduce(big, w, AX, ALU.add).then_inc(vector_steps, v.step())
            v.wait_ge(vector_steps, v.n)
            nc.vector.reciprocal(stat[:, 16:32], big).then_inc(vector_steps, v.step())
            v.wait_ge(vector_steps, v.n)
            nc.vector.tensor_tensor(w, w, stat[:, 16:32].unsqueeze(2).to_broadcast([P, NT * PEER_H, TOPK]), ALU.mult) \
                .then_inc(vector_steps, v.step(f"weights{l}"))
            for i in range(NT):
                v.wait_ge(*when(f"sel{l}.turned{i}"))
                if i == 0:
                    v.wait_ge(*when(f"sel{l}.turned1"))
                nc.vector.tensor_copy(selT[:, :, i * P:(i + 1) * P],
                                      ps[:, 4 + i, 0:3 * P].rearrange("p (a b) -> p a b", a=3)) \
                    .then_inc(vector_steps, v.step(f"selT{l}"))
            v.wait_ge(vector_steps, v.n)

        def peer_turn_tensor(t, l):
            t.wait_ge(*when(f"weights{l}"))
            for i in range(NT):
                for mark in free[4 + i]:
                    t.wait_ge(*when(mark))
                for part in range(3):
                    ins = nc.tensor.transpose(ps[:, 4 + i, part * P:(part + 1) * P], e_sel[:, part, i, :], ident[:, :])
                ins.then_inc(tensor_steps, t.step(f"sel{l}.turned{i}"))

        GROUPS = SEQ // 8
        HALF = KEYS // 2

        def at(ap2d, i, step, off, n):
            if isinstance(i, int):
                return ap2d[:, i * step + off:i * step + off + n]
            return ap2d[:, bass.ds(i * step + off, n)]

        def peer_routes_gpsimd(g, l):
            g.wait_ge(*when(f"selT{l}"))

            def body(p, i, first):
                if not (first and p == 0):
                    g.eng.wait_ge(hot_cols, i * 2 + p * GROUPS)
                    g.eng.sem_inc(pool_paused, 1)
                nc.gpsimd.tensor_copy(second, at(selT[:, 1, :], i, 16, 0, 16)).then_inc(second_copied, 1)
                g.eng.wait_ge(second_copied, i + (p * 16 + 1))
                g.eng.sem_inc(pool_paused, 1)
                for r in range(2):
                    if not (first and p == 0):
                        g.eng.wait_ge(routes_full, i * 2 + (p * GROUPS + r - 1))
                        g.eng.sem_inc(pool_paused, 1)
                    for n in range(8):
                        ins = nc.gpsimd.tensor_scalar(hot_c[r][:, n, :], iota[:, :], second[:, 8 * r + n:8 * r + n + 1],
                                                      None, ALU.is_equal)
                    ins.then_inc(hot_cols, 1)
            for p in (2 * l, 2 * l + 1):
                if p == 0:
                    body(p, 0, True)
                with g.eng.Fori(1 if p == 0 else 0, 16) as i:
                    body(p, i, False)
            g.seen.clear()

        def routes_group_vector(v, p, i, r, first):
            if not (first and r < 2 and p == 0):
                v.eng.wait_ge(routes_full, i * 4 + (p * GROUPS + r - 1))
            keys = iota[:, (p % 2) * HALF:(p % 2 + 1) * HALF]
            for n in range(8):
                ins = nc.vector.tensor_scalar(hot_r[r % 2][:, n, :], keys, at(selT[:, 0, :], i, 32, 8 * r + n, 1),
                                              at(selT[:, 2, :], i, 32, 8 * r + n, 1), ALU.is_equal, ALU.mult)
            ins.then_inc(hot_rows, 1)
            if r:
                routes_merge_vector(v, p, i, r - 1)
            elif not first:
                routes_merge_vector(v, p, i - 1, 3)

        def routes_merge_vector(v, p, i, r):
            v.eng.wait_ge(routes_full, i * 4 + (p * GROUPS + r + 1))
            gv = gate[:, :].rearrange("p (n t) -> p n t", t=SEQ)[:, (p % 2) * HALF:(p % 2 + 1) * HALF, :]
            if isinstance(i, int):
                dst = gv[:, :, 32 * i + 8 * r:32 * i + 8 * r + 8]
            else:
                dst = gv[:, :, bass.ds(i * 32 + 8 * r, 8)]
            nc.vector.tensor_tensor(dst, dst, ps[:, 5 + r % 2, :].rearrange("p (t n) -> p n t", t=8),
                                    ALU.mult).then_inc(routes_merged, 1)

        def peer_routes_vector(v, l):
            s0 = FIRST_STRIPS + l * LOOP_STRIPS
            p = 2 * l
            v.eng.wait_ge(u_drained, l * 68 + 4 + 32)
            for r in range(4):
                routes_group_vector(v, p, 0, r, True)
            with v.eng.Fori(1, 8) as i:
                for r in range(4):
                    routes_group_vector(v, p, i, r, False)
            routes_merge_vector(v, p, 7, 3)
            p = 2 * l + 1
            v.eng.wait_ge(u_drained, (l + 1) * 68)

            def both(i, first):
                for r in range(4):
                    routes_group_vector(v, p, i, r, first)
                    if r == 0 and not first:
                        strip_store_vector(v, i - 1, s0)
                    for k in (2 * r, 2 * r + 1):
                        strip_chunk_vector(v, i, s0, k, 0 if s0 < MOD2[0] else 8)
            both(0, True)
            with v.eng.Fori(1, 8) as i:
                both(i, False)
            routes_merge_vector(v, p, 7, 3)
            strip_store_vector(v, 7, s0)
            assert s0 + 8 == MOD2[0] or s0 > MOD2[0]
            with v.eng.Fori(8, LOOP_STRIPS) as i:
                for k in range(DC):
                    strip_chunk_vector(v, i, s0, k, 8)
                strip_store_vector(v, i, s0)
            v.seen.clear()

        def routes_group_tensor(t, p, i, r, first):
            t.eng.wait_ge(hot_rows, i * 4 + (p * GROUPS + r + 1))
            t.eng.wait_ge(hot_cols, i * 4 + (p * GROUPS + r + 1))
            if not (first and r < 2):
                t.eng.wait_ge(routes_merged, i * 4 + (p * GROUPS + r - 1))
            for n in range(8):
                ins = nc.tensor.matmul(ps[:, 5 + r % 2, n * HALF:(n + 1) * HALF], hot_c[r % 2][:, n, :],
                                       hot_r[r % 2][:, n, :], start=True, stop=True)
            ins.then_inc(routes_full, 1)

        def peer_out_tensor(t, l):
            t.eng.wait_ge(u_drained, (l + 1) * 68)
            for b in range(4):
                for n in range(4):
                    nc.tensor.matmul(ps[:, b, n * P:(n + 1) * P], zeros[:, :], zeros[:, :], start=(n == 0), stop=True,
                                     skip_group_check=True)
            t.eng.wait_ge(routes_merged, (2 * l + 1) * GROUPS)
            base = START[f"v{l}"]
            done = l * LOOP_STRIPS

            def body(i, strip, routes):
                for j in range(RING):
                    if routes:
                        routes_group_tensor(t, 2 * l + 1, i, j, False)
                    s = base + j
                    t.eng.wait_ge(slab_landed[s % RING], i * 16 + 16 * (s // RING + 1))
                    for e in range(2):
                        g = gate[:, bass.ds(i * (8 * SEQ) + (2 * j + e) * SEQ, SEQ)]
                        for d in range(DC):
                            ins = nc.tensor.matmul(ps[:, d // 2, (d % 2) * SEQ:(d % 2 + 1) * SEQ],
                                                   ring[:, s % RING, e * D + d * P:e * D + (d + 1) * P], g,
                                                   start=False, stop=True, skip_group_check=True)
                    ins.then_inc(slab_used, 1)
                if strip:
                    t.eng.wait_ge(mod_used, i * DC + (done * DC + DC))
                    strip_sum_tensor(mod_acc, 4).then_inc(strip_summed, 1)
            with t.eng.Fori(0, 8) as i:
                body(i, True, True)
            t.eng.wait_ge(routes_merged, (2 * l + 2) * GROUPS)
            with t.eng.Fori(8, LOOP_STRIPS) as i:
                body(i, True, False)
            with t.eng.Fori(LOOP_STRIPS, 16) as i:
                body(i, False, False)
            t.seen.clear()
            new_marks[f"peer{l}.full"] = ("S", base + 64)
            t.eng.wait_ge(strip_stored, (l + 1) * LOOP_STRIPS)
            turn_name = f"peer{l}"
            for c in range(DC):
                b = 4 + 2 * (c // 4)
                for i in range(NT):
                    t.wait_ge(*when(f"peer{l}.y{c // 2}"))
                    ins = nc.tensor.transpose(ps[:, b + i, (c % 4) * P:(c % 4 + 1) * P], yT[:, c, i * P:(i + 1) * P],
                                              ident[:, :])
                    if c % 4 == 3:
                        ins.then_inc(tensor_steps, t.step(f"{turn_name}.back{2 * (c // 4) + i}"))
                        free[b + i] = [f"peer{l}.res.out{2 * (c // 4) + i}"]
            free[0] = free[1] = [f"peer{l}.y3"]
            free[2] = free[3] = [f"peer{l}.y3"]
            row_from_col(t, f"g2_{l}", None, 0, "T")

        def peer_out_scalar(a, l):
            a.wait_ge(*when(f"peer{l}.full"))
            for b in range(4):
                nc.scalar.activation(yT[:, 2 * b:2 * b + 2, :].rearrange("p a b -> p (a b)"), ps[:, b, :], ACT.Copy) \
                    .then_inc(scalar_steps, a.step(f"peer{l}.y{b}"))

        def peer_out_vector(v, l):
            v.eng.wait_ge(strip_stored, (l + 1) * LOOP_STRIPS)
            v.wait_ge(*when(f"peer{l}.full"))
            row_from_col(v, f"g2_{l}", modc[:, MOD1[l] + G2, :], 0, "V")
            row_store(v, f"g2_{l}", 0)
            v.wait_ge(vector_steps, v.n)
            residual_vector(v, f"peer{l}.res", lambda nb, i: f"peer{l}.back{2 * nb + i}", bank=4)

        def double_norm_vector(v, name, gain, sc, sh, gain2, sc2, sh2, dst2):
            rstd_vector(v, name)
            for i in range(NT):
                nc.vector.tensor_scalar(xn[:, i, :], x[:, i, :], stat[:, 48 + i:49 + i], None, ALU.mult) \
                    .then_inc(vector_steps, v.step(f"{name}.xn{i}"))
            nc.vector.scalar_tensor_tensor(out=scale_c[:, :], in0=modc[:, sc, :], scalar=1.0, in1=gain,
                                           op0=ALU.add, op1=ALU.mult).then_inc(vector_steps, v.step())
            nc.vector.scalar_tensor_tensor(out=scale_c2[:, :], in0=modc[:, sc2, :], scalar=1.0, in1=gain2,
                                           op0=ALU.add, op1=ALU.mult).then_inc(vector_steps, v.step())
            v.wait_ge(vector_steps, v.n)
            turned_vector(v, name, dst2, lambda c: scale_c2[:, c:c + 1], lambda c: modc[:, sh2, c:c + 1], out=f"{name}.kv")
            turned_vector(v, name, hT, lambda c: scale_c[:, c:c + 1], lambda c: modc[:, sh, c:c + 1])

        def rope_vector(v, buf, i, half, off, tmp):
            heads = buf.shape[1]
            x1, x2 = buf[:, :, 0:half], buf[:, :, half:2 * half]
            s, c = (trig[:, n, i, off:off + half].unsqueeze(1).to_broadcast([P, heads, half]) for n in range(2))
            t4 = [tmp[:, n * heads * half:(n + 1) * heads * half].rearrange("p (h d) -> p h d", h=heads)
                  for n in range(4)]
            v.wait_ge(vector_steps, v.n)
            for dst, a, b in zip(t4, (x1, x2, x2, x1), (c, s, c, s)):
                nc.vector.tensor_tensor(dst, a, b, ALU.mult).then_inc(vector_steps, v.step())
            v.wait_ge(vector_steps, v.n)
            nc.vector.tensor_tensor(x1, t4[0], t4[1], ALU.subtract).then_inc(vector_steps, v.step())
            nc.vector.tensor_tensor(x2, t4[2], t4[3], ALU.add).then_inc(vector_steps, v.step())

        def copy_scalar(a, name, dsts, bank, func=ACT.Copy, width=BANK):
            for n, dst in enumerate(dsts):
                a.wait_ge(*when(f"{name}.full{n}"))
                nc.scalar.activation(dst, ps[:, bank(n), 0:width], func) \
                    .then_inc(scalar_steps, a.step(f"{name}.out{n}"))

        def token_tiles(buf, width=D):
            return [buf[:, n % 2, (n // 2) * BANK:min(width, (n // 2 + 1) * BANK)]
                    for n in range(2 * ((width + BANK - 1) // BANK))]

        class Attention:
            def __init__(self, name, heads, area):
                self.name, self.heads, self.dv = name, heads, D // heads
                self.per = [4, 2]
                self.groups = [heads // p for p in self.per]
                self.prob = [area.take(heads, P), area.take(heads, 2 * P)]
                self.probT = [area.take(heads, P), area.take(heads, 2 * P)]
                self.st = area.take(2, 6, 16)
                self.bank, n = {}, 0
                for i in range(NT):
                    for g in range(self.groups[i]):
                        self.bank["s", i, g] = n % 8
                        n += 1
                for i in range(NT):
                    for g in range(self.groups[i]):
                        self.bank["t", i, g] = n % 8
                        n += 1
                    for b in range(2):
                        self.bank["o", i, b] = n % 8
                        n += 1

        def scores_tensor(t, at_, products, ready):
            for mark in ready:
                t.wait_ge(*when(mark))
            for i in range(NT):
                for g in range(at_.groups[i]):
                    bk = at_.bank["s", i, g]
                    for mark in free[bk]:
                        t.wait_ge(*when(mark))
                    for hh in range(at_.per[i]):
                        for kt in range(i + 1):
                            pairs = products(at_.per[i] * g + hh, i, kt)
                            to = ps[:, bk, (hh * (i + 1) + kt) * P:(hh * (i + 1) + kt + 1) * P]
                            for n, (a, b) in enumerate(pairs):
                                ins = nc.tensor.matmul(to, a, b, start=(n == 0), stop=(n == len(pairs) - 1))
                    ins.then_inc(tensor_steps, t.step(f"{at_.name}.s{i}.{g}"))
                    free[bk] = [f"{at_.name}.sc{i}.{g}"]

        def values_tensor(t, at_, values):
            nm = at_.name
            for i in range(NT):
                for g in range(at_.groups[i]):
                    bk = at_.bank["t", i, g]
                    for mark in free[bk]:
                        t.wait_ge(*when(mark))
                    t.wait_ge(*when(f"{nm}.p{i}.{g}"))
                    flat = at_.prob[i].rearrange("p h k -> p (h k)")
                    for n in range(4):
                        ins = nc.tensor.transpose(ps[:, bk, n * P:(n + 1) * P],
                                                  flat[:, (4 * g + n) * P:(4 * g + n + 1) * P], ident[:, :])
                    ins.then_inc(tensor_steps, t.step(f"{nm}.t{i}.{g}"))
                    free[bk] = [f"{nm}.tc{i}.{g}"]
                hb = at_.heads // 2
                for b in range(2):
                    bk = at_.bank["o", i, b]
                    for mark in free[bk]:
                        t.wait_ge(*when(mark))
                    for h in range(b * hb, (b + 1) * hb):
                        t.wait_ge(*when(f"{nm}.tc{i}.{h // at_.per[i]}"))
                        for kt in range(i + 1):
                            ins = nc.tensor.matmul(ps[:, bk, (h - b * hb) * at_.dv:(h - b * hb + 1) * at_.dv],
                                                   at_.probT[i][:, h, kt * P:(kt + 1) * P], values(kt, h),
                                                   start=(kt == 0), stop=(kt == i))
                    ins.then_inc(tensor_steps, t.step(f"{nm}.o{i}.{b}"))
                    free[bk] = [f"{nm}.oc{i}.{b}"]

        MX, NM, DEN, RD, EX = range(5)

        def softmax_vector(v, at_, dst, scale, mask, sinks=None):
            nm, H = at_.name, at_.heads
            for i in range(NT):
                for g in range(at_.groups[i]):
                    v.wait_ge(*when(f"{nm}.s{i}.{g}"))
                    hs = slice(at_.per[i] * g, at_.per[i] * (g + 1))
                    n = (i + 1) * P
                    nc.vector.scalar_tensor_tensor(
                        out=at_.prob[i][:, hs, :],
                        in0=ps[:, at_.bank["s", i, g], :].rearrange("p (h k) -> p h k", k=n), scalar=scale,
                        in1=mask(i).unsqueeze(1).to_broadcast([P, at_.per[i], n]), op0=ALU.mult, op1=ALU.add) \
                        .then_inc(vector_steps, v.step(f"{nm}.sc{i}.{g}"))
            v.wait_ge(vector_steps, v.n)
            for i in range(NT):
                st = at_.st[:, i]
                nc.vector.tensor_reduce(st[:, MX, 0:H], at_.prob[i], AX, ALU.max).then_inc(vector_steps, v.step())
                v.wait_ge(vector_steps, v.n)
                if sinks is not None:
                    nc.vector.tensor_tensor(st[:, MX, 0:H], st[:, MX, 0:H], sinks, ALU.max) \
                        .then_inc(vector_steps, v.step())
                    v.wait_ge(vector_steps, v.n)
                nc.vector.tensor_scalar(st[:, NM, 0:H], st[:, MX, 0:H], -1.0, None, ALU.mult) \
                    .then_inc(vector_steps, v.step(f"{nm}.nm{i}"))
                if sinks is not None:
                    nc.vector.tensor_tensor(st[:, EX, 0:H], sinks, st[:, MX, 0:H], ALU.subtract) \
                        .then_inc(vector_steps, v.step(f"{nm}.nm{i}"))
            for i in range(NT):
                st = at_.st[:, i]
                v.wait_ge(*when(f"{nm}.p{i}.{at_.groups[i] - 1}"))
                if sinks is not None:
                    v.wait_ge(*when(f"{nm}.sink{i}"))
                    nc.vector.tensor_tensor(st[:, DEN, 0:H], st[:, DEN, 0:H], st[:, EX, 0:H], ALU.add) \
                        .then_inc(vector_steps, v.step())
                    v.wait_ge(vector_steps, v.n)
                nc.vector.reciprocal(st[:, RD, 0:H], st[:, DEN, 0:H]).then_inc(vector_steps, v.step())
                probT_vector(v, at_, i)
                attended_vector(v, at_, dst, i)

        def softmax_scalar(a, at_, sinks=False):
            nm, H = at_.name, at_.heads
            for i in range(NT):
                st = at_.st[:, i]
                a.wait_ge(*when(f"{nm}.nm{i}"))
                for h in range(H):
                    nc.scalar.activation(at_.prob[i][:, h, :], at_.prob[i][:, h, :], ACT.Exp,
                                         bias=st[:, NM, h:h + 1], accum_out=st[:, DEN, h:h + 1]) \
                        .then_inc(scalar_steps, a.step(f"{nm}.p{i}.{h // at_.per[i]}"))
                if sinks:
                    nc.scalar.activation(st[:, EX, 0:H], st[:, EX, 0:H], ACT.Exp) \
                        .then_inc(scalar_steps, a.step(f"{nm}.sink{i}"))

        def probT_vector(v, at_, i):
            nm = at_.name
            flat = at_.probT[i].rearrange("p h k -> p (h k)")
            for g in range(at_.groups[i]):
                v.wait_ge(*when(f"{nm}.t{i}.{g}"))
                nc.vector.tensor_copy(flat[:, g * BANK:(g + 1) * BANK], ps[:, at_.bank["t", i, g], :]) \
                    .then_inc(vector_steps, v.step(f"{nm}.tc{i}.{g}"))

        def attended_vector(v, at_, dst, i):
            nm, hb = at_.name, at_.heads // 2
            v.wait_ge(vector_steps, v.n)
            for b in range(2):
                v.wait_ge(*when(f"{nm}.o{i}.{b}"))
                nc.vector.tensor_tensor(
                    dst[:, i, b * BANK:(b + 1) * BANK].rearrange("p (h e) -> p h e", h=hb),
                    ps[:, at_.bank["o", i, b], :].rearrange("p (h e) -> p h e", h=hb),
                    at_.st[:, i, RD, b * hb:(b + 1) * hb].unsqueeze(2).to_broadcast([P, hb, at_.dv]), ALU.mult) \
                    .then_inc(vector_steps, v.step(f"{nm}.oc{i}.{b}"))

        def turned_out_tensor(t, name, src, ready):
            turn_tensor(t, name, lambda i, c: src[:, i, c * P:(c + 1) * P], lambda i, c: [ready(i, c)], bank=0)

        W = Area(gate, LAYER)
        kvT = W.take(DC, SEQ)
        kv_s = W.take(NT, BANK)
        q_s = W.take(NT, D)
        kT_s = W.take(2, SEQ)
        qT_s = W.take(8, SEQ)
        rope_tmp = W.take(4 * SWA_H * ROT1)
        swa = Attention("swa", SWA_H, W)
        assert W.at <= KEYS * SEQ
        q_s3 = [q_s[:, i, :].rearrange("p (h d) -> p h d", d=SWA_D) for i in range(NT)]
        kv_s3 = [kv_s[:, i, 0:SWA_KV * SWA_D].rearrange("p (h d) -> p h d", d=SWA_D) for i in range(NT)]

        def swa_tensor(t):
            norm_tensor(t, "n1_1")
            gemm_M(t, "kv", "kv", DC, 4, BANK, kvT, lambda c: [f"n1_1.kv.T{c}"], bank=4)
            gemm_M(t, "swa_q", "swa_q", DC, 2, D, hT, lambda c: [f"n1_1.T{c}"], bank=0)
            turn_tensor(t, "swa_k", lambda i, c: kv_s[:, i, c * P:(c + 1) * P], lambda i, c: ["swa.k_rot"], bank=4,
                        chunks=2)
            turn_tensor(t, "swa_qt", lambda i, c: q_s[:, i, c * P:(c + 1) * P], lambda i, c: ["swa.q_rot"], bank=4)

            def products(h, i, kt):
                lo = SWA_D * (h // 4 % 2)
                own = kt if i else 0
                return [(qT_s[lo:lo + SWA_D, 4 * (h // 8) + h % 4, i * P:(i + 1) * P],
                         kT_s[lo:lo + SWA_D, h // 8, own * P:(own + 1) * P])]
            scores_tensor(t, swa, products, ["swa_k.T1", "swa_qt.T7"])
            values_tensor(t, swa, lambda kt, h: kv_s[:, kt, 256 + SWA_D * (h // 4):256 + SWA_D * (h // 4 + 1)])
            turned_out_tensor(t, "swa_o", q_s, lambda i, c: f"swa.oc{i}.{c // 4}")
            row_from_col(t, "g1_1", None, 4, "T")
            gemm_M(t, "swa_out", "swa_out", DC, 2, D, yT, lambda c: [f"swa_o.T{c}"], bank=0)

        def swa_scalar(a):
            norm_scalar(a, "n1_1", ["peer0.res.x"])
            copy_scalar(a, "kv", token_tiles(kv_s, BANK), lambda n: 4 + n)
            copy_scalar(a, "swa_q", token_tiles(q_s), lambda n: n)
            softmax_scalar(a, swa, sinks=True)

        def swa_vector(v):
            double_norm_vector(v, "n1_1", col("norm1", 2), MOD1[1] + SC1, MOD1[1] + SH1,
                               col("kvn1"), KVMOD1 + 1, KVMOD1, kvT)
            for i in range(NT):
                v.wait_ge(*when(f"kv.out{i}"))
                rope_vector(v, kv_s3[i], i, ROT1, 0, rope_tmp)
            v.wait_ge(vector_steps, v.n)
            nc.vector.tensor_copy(stat[:, 63:64], stat[:, 63:64]).then_inc(vector_steps, v.step("swa.k_rot"))
            for i in range(NT):
                v.wait_ge(*when(f"swa_q.out{2 + i}"))
                rope_vector(v, q_s3[i], i, ROT1, 0, rope_tmp)
            v.wait_ge(vector_steps, v.n)
            nc.vector.tensor_copy(stat[:, 63:64], stat[:, 63:64]).then_inc(vector_steps, v.step("swa.q_rot"))
            turned_vector(v, "swa_k", kT_s, bank=4, chunks=2)
            turned_vector(v, "swa_qt", qT_s, bank=4)
            softmax_vector(v, swa, q_s, SWA_D ** -0.5, lambda i: band[:, P:2 * P] if i == 0 else band[:, :],
                           rows[:, ROWS["sinks"]:ROWS["sinks"] + SWA_H])
            turned_vector(v, "swa_o", yT, bank=0)
            row_from_col(v, "g1_1", modc[:, MOD1[1] + G1, :], 4, "V")
            row_store(v, "g1_1", 4)
            v.wait_ge(vector_steps, v.n)
            residual_vector(v, "swa_out", lambda nb, i: f"swa_out.full{2 * nb + i}")

        def last_norm_scalar(a):
            norm_scalar(a, "fin", ["peer1.res.x"])

        def last_norm_tensor(t):
            row_from_col(t, "fin", None, 0, "T")

        def last_norm_vector(v):
            row_from_col(v, "fin", col("fin"), 0, "V")
            row_store(v, "fin", 0)
            rstd_vector(v, "fin")
            for i in range(NT):
                nc.vector.scalar_tensor_tensor(out=x[:, i, :], in0=x[:, i, :], scalar=stat[:, 48 + i:49 + i],
                                               in1=row, op0=ALU.mult, op1=ALU.mult) \
                    .then_inc(vector_steps, v.step("fin.x"))
            v.wait_ge(vector_steps, v.n)

        def post_scalar(a, name, bank=0):
            for n in range(4):
                a.wait_ge(*when(f"{name}.full{n}"))
                nc.scalar.activation(junk(n, BANK), ps[:, bank + n, :], ACT.Square, accum_out=stat[:, n:n + 1]) \
                    .then_inc(scalar_steps, a.step(f"{name}.ss"))
            std_scalar(a, name)

        def post_tensor(t, name, bank):
            row_from_col(t, f"{name}.g", None, bank, "T")

        def post_vector(v, name, gain, g, row_bank, bank=0):
            nc.vector.tensor_tensor(scale_c2[:, :], modc[:, g, :], gain, ALU.mult).then_inc(vector_steps, v.step())
            row_from_col(v, f"{name}.g", scale_c2[:, :], row_bank, "V")
            row_store(v, f"{name}.g", row_bank)
            v.wait_ge(*when(f"{name}.ss"))
            nc.vector.tensor_tensor(stat[:, 0:2], stat[:, 0:2], stat[:, 2:4], ALU.add) \
                .then_inc(vector_steps, v.step())
            rstd_vector(v, name)
            residual_vector(v, name, lambda nb, i: f"{name}.full{2 * nb + i}", bank=bank,
                            scale=lambda i: stat[:, 48 + i:49 + i])

        L = Area(gate, LAYER)
        ml_q = L.take(H_GLA, SEQ)
        ml_k = L.take(H_GLA, SEQ)
        ml_v = L.take(NT, D)
        ml_o = L.take(NT, D)
        ml_h = L.take(NT, D)
        head_row = L.take(D)
        ml_diag = L.take(NT, H_GLA, P)
        ml_g = L.take(NT, 8)
        ml_lf = L.take(NT, H_GLA)
        ml_F = L.take(NT, H_GLA)
        ml_r = L.take(NT, H_GLA)
        ml_t = L.take(NT, H_GLA)
        mls = Attention("ml", H_GLA, L)
        assert L.at <= KEYS * SEQ

        def mlstm_tensor(t):
            norm_tensor(t, "m1")
            gemm_T(t, "ml_qk", "ml_qk", 8, DC, hT, lambda c: [f"m1.T{c}"], bank=0)
            for mark in free[4]:
                t.wait_ge(*when(mark))
            for i in range(NT):
                for c in range(DC):
                    ins = nc.tensor.matmul(ps[:, 4, 8 * i:8 * i + 8], hT[:, c, i * P:(i + 1) * P], w_gates[:, c, :],
                                           start=(c == 0), stop=(c == DC - 1))
            ins.then_inc(tensor_steps, t.step("ml.gates"))
            gemm_M(t, "ml_v", "ml_v", DC, 2, D, hT, lambda c: [], bank=0)
            free[4] = ["ml.pre"]
            t.wait_ge(*when("ml.lf"))
            for mark in free[4]:
                t.wait_ge(*when(mark))
            for mark in free[5]:
                t.wait_ge(*when(mark))
            nc.tensor.matmul(ps[:, 5, 0:4], upper[:, :], ml_lf[:, 0, :], start=True, stop=True)
            nc.tensor.matmul(ps[:, 5, 4:8], ones[:, :], ml_lf[:, 0, :], start=True, stop=False)
            nc.tensor.matmul(ps[:, 5, 4:8], upper[:, :], ml_lf[:, 1, :], start=False, stop=True) \
                .then_inc(tensor_steps, t.step("ml.F"))
            free[5] = ["ml.r"]
            t.wait_ge(*when("ml.diag"))
            for mark in free[6]:
                t.wait_ge(*when(mark))
            for mark in free[7]:
                t.wait_ge(*when(mark))
            for i in range(NT):
                nc.tensor.matmul(ps[:, 6 + i, :], ones[:, :], ml_diag[:, i, :, :].rearrange("p a b -> p (a b)"),
                                 start=True, stop=True).then_inc(tensor_steps, t.step(f"ml.rows{i}"))
                free[6 + i] = ["ml.logits"]
            gemm_M(t, "ml_o", "ml_o", DC, 2, D, hT, lambda c: [], bank=0)
            scores_tensor(t, mls, lambda h, i, kt: [(ml_q[:, h, i * P:(i + 1) * P], ml_k[:, h, kt * P:(kt + 1) * P])],
                          ["ml_qk.out3"])
            t.wait_ge(*when("ml_v.out3"))
            values_tensor(t, mls, lambda kt, h: ml_v[:, kt, h * DV:(h + 1) * DV])
            turned_out_tensor(t, "ml_turn", ml_h, lambda i, c: f"ml.gated{i}")
            post_tensor(t, "ml_out", 4)
            gemm_M(t, "ml_out", "ml_out", DC, 2, D, yT, lambda c: [f"ml_turn.T{c}"], bank=0)

        def mlstm_scalar(a):
            act = a.eng
            act.dma_start(head_row, io["rows"][0, ROWS["head_norm"]:ROWS["head_norm"] + D].partition_broadcast(P)) \
               .then_inc(head_norm_landed, 16)
            norm_scalar(a, "m1", ["fin.x"])
            copy_scalar(a, "ml_qk", [(ml_q, ml_k)[n // 2][:, 2 * (n % 2):2 * (n % 2) + 2, :].rearrange("p a b -> p (a b)")
                                     for n in range(4)], lambda n: n)
            a.wait_ge(*when("ml.pre"))
            nc.scalar.activation(ml_t, ml_g[:, :, 4:8], ACT.Abs).then_inc(scalar_steps, a.step())
            a.wait_ge(scalar_steps, a.n)
            nc.scalar.activation(ml_t, ml_t, ACT.Exp, scale=-1.0).then_inc(scalar_steps, a.step())
            a.wait_ge(scalar_steps, a.n)
            nc.scalar.activation(ml_t, ml_t, ACT.Ln, bias=1.0).then_inc(scalar_steps, a.step("ml.ln"))
            copy_scalar(a, "ml_v", token_tiles(ml_v), lambda n: n)
            a.wait_ge(*when("ml.nm"))
            for i in range(NT):
                for h in range(H_GLA):
                    nc.scalar.activation(mls.prob[i][:, h, :], mls.prob[i][:, h, :], ACT.Exp,
                                         bias=mls.st[:, i, NM, h:h + 1]).then_inc(scalar_steps, a.step(f"ml.e{i}"))
                nc.scalar.activation(mls.st[:, i, EX, 0:4], mls.st[:, i, EX, 0:4], ACT.Exp) \
                    .then_inc(scalar_steps, a.step(f"ml.e{i}"))
            copy_scalar(a, "ml_o", token_tiles(ml_o), lambda n: n, ACT.Sigmoid)
            for i in range(NT):
                a.wait_ge(*when(f"ml.oc{i}.1"))
                for h in range(H_GLA):
                    nc.scalar.activation(junk(4 * i + h, DV), ml_h[:, i, h * DV:(h + 1) * DV], ACT.Square,
                                         accum_out=stat[:, 4 * i + h:4 * i + h + 1]) \
                        .then_inc(scalar_steps, a.step("ml.r2.ss"))
            std_scalar(a, "ml.r2", 8)
            post_scalar(a, "ml_out")

        def mlstm_vector(v):
            norm_vector(v, "m1", col("norm2", 0), MOD2[0] + SC1, MOD2[0] + SH1)
            v.wait_ge(*when("ml.gates"))
            gb = rows[:, ROWS["gates_b"]:ROWS["gates_b"] + 8]
            nc.vector.tensor_tensor(ml_g, ps[:, 4, 0:16].rearrange("p (a b) -> p a b", a=NT),
                                    gb.unsqueeze(1).to_broadcast([P, NT, 8]), ALU.add) \
                .then_inc(vector_steps, v.step("ml.pre"))
            v.wait_ge(*when("ml.ln"))
            v.wait_ge(vector_steps, v.n)
            nc.vector.scalar_tensor_tensor(out=ml_lf, in0=ml_g[:, :, 4:8], scalar=0.0, in1=ml_t,
                                           op0=ALU.min, op1=ALU.subtract).then_inc(vector_steps, v.step("ml.lf"))
            v.wait_ge(*when("ml.F"))
            nc.vector.tensor_copy(ml_F, ps[:, 5, 0:8].rearrange("p (a b) -> p a b", a=NT)) \
                .then_inc(vector_steps, v.step())
            v.wait_ge(vector_steps, v.n)
            nc.vector.tensor_tensor(ml_r, ml_g[:, :, 0:4], ml_F, ALU.subtract).then_inc(vector_steps, v.step("ml.r"))
            v.wait_ge(vector_steps, v.n)
            nc.vector.tensor_tensor(ml_diag.rearrange("p a b c -> p (a b) c"),
                                    ident[:, :].unsqueeze(1).to_broadcast([P, NT * H_GLA, P]),
                                    ml_r.rearrange("p a b -> p (a b)").unsqueeze(2)
                                    .to_broadcast([P, NT * H_GLA, P]), ALU.mult) \
                .then_inc(vector_steps, v.step("ml.diag"))
            for i in range(NT):
                for kt in range(i + 1):
                    v.wait_ge(*when(f"ml.rows{kt}"))
                    mask = after[:, P:2 * P] if kt == i else after[:, 0:P]
                    nc.vector.tensor_tensor(mls.prob[i][:, :, kt * P:(kt + 1) * P],
                                            ps[:, 6 + kt, :].rearrange("p (a b) -> p a b", a=H_GLA),
                                            mask.unsqueeze(1).to_broadcast([P, H_GLA, P]), ALU.add) \
                        .then_inc(vector_steps, v.step("ml.logits"))
            v.wait_ge(vector_steps, v.n)
            for i in range(NT):
                st = mls.st[:, i]
                nc.vector.tensor_reduce(st[:, MX, 0:4], mls.prob[i], AX, ALU.max).then_inc(vector_steps, v.step())
                v.wait_ge(vector_steps, v.n)
                nc.vector.tensor_scalar(st[:, NM, 0:4], st[:, MX, 0:4], 0.0, -1.0, ALU.max, ALU.mult) \
                    .then_inc(vector_steps, v.step())
                v.wait_ge(vector_steps, v.n)
                nc.vector.tensor_tensor(st[:, EX, 0:4], st[:, NM, 0:4], ml_F[:, i, :], ALU.subtract) \
                    .then_inc(vector_steps, v.step("ml.nm"))
            for i in range(NT):
                st = mls.st[:, i]
                v.wait_ge(*when(f"ml.e{i}"))
                for g in range(mls.groups[i]):
                    v.wait_ge(*when(f"ml.s{i}.{g}"))
                    hs = slice(mls.per[i] * g, mls.per[i] * (g + 1))
                    pr = mls.prob[i][:, hs, :]
                    nc.vector.scalar_tensor_tensor(
                        out=pr, in0=ps[:, mls.bank["s", i, g], :].rearrange("p (h k) -> p h k", k=(i + 1) * P),
                        scalar=float(P) ** -0.5, in1=pr, op0=ALU.mult, op1=ALU.mult) \
                        .then_inc(vector_steps, v.step(f"ml.sc{i}.{g}"))
                    new_marks[f"ml.p{i}.{g}"] = ("V", v.n)
            v.wait_ge(vector_steps, v.n)
            for i in range(NT):
                st = mls.st[:, i]
                nc.vector.tensor_reduce(st[:, DEN, 0:4], mls.prob[i], AX, ALU.add).then_inc(vector_steps, v.step())
                v.wait_ge(vector_steps, v.n)
                nc.vector.tensor_scalar(st[:, MX, 0:4], st[:, DEN, 0:4], -1.0, None, ALU.mult) \
                    .then_inc(vector_steps, v.step())
                v.wait_ge(vector_steps, v.n)
                nc.vector.tensor_tensor(st[:, DEN, 0:4], st[:, DEN, 0:4], st[:, MX, 0:4], ALU.max) \
                    .then_inc(vector_steps, v.step())
                v.wait_ge(vector_steps, v.n)
                nc.vector.tensor_tensor(st[:, DEN, 0:4], st[:, DEN, 0:4], st[:, EX, 0:4], ALU.max) \
                    .then_inc(vector_steps, v.step())
                v.wait_ge(vector_steps, v.n)
                nc.vector.reciprocal(st[:, RD, 0:4], st[:, DEN, 0:4]).then_inc(vector_steps, v.step())
                probT_vector(v, mls, i)
                attended_vector(v, mls, ml_h, i)
            v.eng.wait_ge(head_norm_landed, 16)
            v.wait_ge(*when("ml_o.out3"))
            nc.vector.tensor_tensor(ml_o, ml_o, head_row.unsqueeze(1).to_broadcast([P, NT, D]), ALU.mult) \
                .then_inc(vector_steps, v.step())
            rstd_vector(v, "ml.r2", DV, 8)
            for i in range(NT):
                for h in range(H_GLA):
                    cut = slice(h * DV, (h + 1) * DV)
                    nc.vector.scalar_tensor_tensor(out=ml_h[:, i, cut], in0=ml_h[:, i, cut],
                                                   scalar=stat[:, 48 + 4 * i + h:49 + 4 * i + h],
                                                   in1=ml_o[:, i, cut], op0=ALU.mult, op1=ALU.mult) \
                        .then_inc(vector_steps, v.step(f"ml.gated{i}"))
            turned_vector(v, "ml_turn", yT, bank=0)
            post_vector(v, "ml_out", col("norm2", 1), MOD2[0] + G1, 4)

        hid = gate[:, LAYER:LAYER + FF // P * SEQ].rearrange("p (a b) -> p a b", a=FF // P)

        def mlp_tensor(t, l):
            norm_tensor(t, f"m2_{l}")
            gemm_T(t, f"f1_{l}", f"ffn1_{l}", FF // P, DC, hT, lambda c: [f"m2_{l}.T{c}"], bank=0, nbanks=4)
            gemm_M(t, f"f2_{l}", f"ffn2_{l}", FF // P, 2, D, hid, lambda c: [f"f1_{l}.sq{c // 2}"], bank=4)
            post_tensor(t, f"f2_{l}", 0)

        def mlp_scalar(a, l, after_):
            norm_scalar(a, f"m2_{l}", [after_])
            for g in range(FF // P // 2):
                a.wait_ge(*when(f"f1_{l}.full{g}"))
                nc.scalar.activation(hid[:, 2 * g:2 * g + 2, :].rearrange("p a b -> p (a b)"), ps[:, g % 4, :],
                                     ACT.Relu).then_inc(scalar_steps, a.step(f"f1_{l}.out{g}"))
            post_scalar(a, f"f2_{l}", 4)

        def mlp_vector(v, l):
            norm_vector(v, f"m2_{l}", col("norm2", 4 * l + 2), MOD2[l] + SC2, MOD2[l] + SH2)
            for g in range(FF // P // 2):
                v.wait_ge(*when(f"f1_{l}.out{g}"))
                h = hid[:, 2 * g:2 * g + 2, :]
                nc.vector.tensor_tensor(h, h, h, ALU.mult).then_inc(vector_steps, v.step(f"f1_{l}.sq{g}"))
            post_vector(v, f"f2_{l}", col("norm2", 4 * l + 3), MOD2[l] + G2, 0, bank=4)

        M_ = Area(gate, LAYER)
        kvT2 = M_.take(DC, SEQ)
        qa = M_.take(NT, LORA_Q)
        ckv = M_.take(NT, LORA_KV + ROPE)
        qaT = M_.take(3, SEQ)
        ckvT = M_.take(2, SEQ)
        qnT = M_.take(MLA_H, SEQ)
        knT = M_.take(MLA_H, SEQ)
        q_r = M_.take(NT, MLA_H * ROPE)
        k_r = M_.take(NT, 2 * ROPE)
        qrT = M_.take(4, SEQ)
        krT = M_.take(1, SEQ)
        v_m = M_.take(NT, D)
        tmp_m = M_.take(4 * MLA_H * ROT2)
        o_m = kvT2.rearrange("p a b -> p (a b)").rearrange("p (a b) -> p a b", a=NT)
        mla = Attention("mla", MLA_H, M_)
        assert M_.at <= KEYS * SEQ

        def mla_tensor(t):
            norm_tensor(t, "m1_1")
            gemm_M(t, "qa", "qa", DC, 4, LORA_Q, hT, lambda c: [f"m1_1.T{c}"], bank=4)
            gemm_M(t, "dkv", "dkv", DC, 4, LORA_KV + ROPE, kvT2, lambda c: [], bank=6)
            turn_tensor(t, "qat", lambda i, c: qa[:, i, c * P:(c + 1) * P], lambda i, c: ["mla.qa"], bank=0, chunks=3)
            turn_tensor(t, "ckvt", lambda i, c: ckv[:, i, c * P:(c + 1) * P], lambda i, c: ["mla.qa"], bank=2, chunks=2)
            gemm_T(t, "qn", "qb_nope", MLA_H, 3, qaT, lambda c: [f"qat.T{c}"], bank=4)
            gemm_M(t, "qr", "qb_rope", 3, 3, BANK, qaT, lambda c: [], bank=0)
            gemm_T(t, "kn", "ukv_k", MLA_H, 2, ckvT, lambda c: [f"ckvt.T{c}"], bank=4)
            gemm_M(t, "vm", "ukv_v", 2, 2, D, ckvT, lambda c: [], bank=0)
            turn_tensor(t, "krt", lambda i, c: k_r[:, i, :], lambda i, c: ["mla.rot"], bank=4, chunks=1)
            turn_tensor(t, "qrt", lambda i, c: q_r[:, i, c * P:(c + 1) * P], lambda i, c: ["mla.rot"], bank=5, chunks=4)

            def products(h, i, kt):
                lo = ROPE * (h // 4)
                return [(qnT[:, h, i * P:(i + 1) * P], knT[:, h, kt * P:(kt + 1) * P]),
                        (qrT[lo:lo + ROPE, h % 4, i * P:(i + 1) * P], krT[lo:lo + ROPE, 0, kt * P:(kt + 1) * P])]
            scores_tensor(t, mla, products, ["krt.T0", "qrt.T3", "qn.out3", "kn.out3"])
            t.wait_ge(*when("vm.out3"))
            values_tensor(t, mla, lambda kt, h: v_m[:, kt, h * P:(h + 1) * P])
            turned_out_tensor(t, "mla_turn", o_m, lambda i, c: f"mla.oc{i}.{c // 4}")
            post_tensor(t, "mla_out", 4)
            gemm_M(t, "mla_out", "mla_out", DC, 2, D, yT, lambda c: [f"mla_turn.T{c}"], bank=0)

        def mla_scalar(a):
            norm_scalar(a, "m1_1", ["f2_0.x"])
            copy_scalar(a, "qa", [qa[:, i, :] for i in range(NT)], lambda n: 4 + n, width=LORA_Q)
            copy_scalar(a, "dkv", [ckv[:, i, :] for i in range(NT)], lambda n: 6 + n, width=LORA_KV + ROPE)
            a.wait_ge(scalar_steps, a.n)
            for i in range(NT):
                nc.scalar.activation(junk(2 * i, BANK)[:, 0:LORA_Q], qa[:, i, :], ACT.Square,
                                     accum_out=stat[:, i:i + 1]).then_inc(scalar_steps, a.step("mla.ss"))
                nc.scalar.activation(junk(2 * i + 1, BANK)[:, 0:LORA_KV], ckv[:, i, 0:LORA_KV], ACT.Square,
                                     accum_out=stat[:, 2 + i:3 + i]).then_inc(scalar_steps, a.step("mla.ss"))
            std_scalar(a, "mla", 4)
            pair = [slice(2 * g, 2 * g + 2) for g in range(4)]
            copy_scalar(a, "qn", [qnT[:, c, :].rearrange("p a b -> p (a b)") for c in pair], lambda n: 4 + n)
            copy_scalar(a, "qr", [q_r[:, i, :] for i in range(NT)], lambda n: n)
            copy_scalar(a, "kn", [knT[:, c, :].rearrange("p a b -> p (a b)") for c in pair], lambda n: 4 + n)
            copy_scalar(a, "vm", token_tiles(v_m), lambda n: n)
            softmax_scalar(a, mla)
            post_scalar(a, "mla_out")

        def mla_vector(v):
            double_norm_vector(v, "m1_1", col("norm2", 4), MOD2[1] + SC1, MOD2[1] + SH1,
                               col("kvn2"), KVMOD2 + 1, KVMOD2, kvT2)
            v.wait_ge(*when("mla.ss"))
            for cut, n in (((0, 2), LORA_Q), ((2, 4), LORA_KV)):
                nc.vector.tensor_scalar(stat[:, 16 + cut[0]:16 + cut[1]], stat[:, cut[0]:cut[1]], 1.0 / n, EPS,
                                        ALU.mult, ALU.add).then_inc(vector_steps, v.step("mla.var"))
            v.wait_ge(*when("mla.std"))
            nc.vector.reciprocal(stat[:, 48:52], stat[:, 32:36]).then_inc(vector_steps, v.step())
            v.wait_ge(vector_steps, v.n)
            for i in range(NT):
                nc.vector.tensor_scalar(qa[:, i, :], qa[:, i, :], stat[:, 48 + i:49 + i], None, ALU.mult) \
                    .then_inc(vector_steps, v.step())
                nc.vector.tensor_scalar(ckv[:, i, 0:LORA_KV], ckv[:, i, 0:LORA_KV], stat[:, 50 + i:51 + i], None,
                                        ALU.mult).then_inc(vector_steps, v.step("mla.qa"))
            turned_vector(v, "qat", qaT, lambda c: cols[:, COLS["qn"] + c:COLS["qn"] + c + 1], bank=0, chunks=3)
            turned_vector(v, "ckvt", ckvT, lambda c: cols[:, COLS["kvl"] + c:COLS["kvl"] + c + 1], bank=2, chunks=2)
            for i in range(NT):
                rope_vector(v, ckv[:, i, LORA_KV:].unsqueeze(1), i, ROT2, ROT1, tmp_m)
            v.wait_ge(vector_steps, v.n)
            for i in range(NT):
                nc.vector.tensor_copy(k_r[:, i, :].rearrange("p (a b) -> p a b", a=2),
                                      ckv[:, i, LORA_KV:].unsqueeze(1).to_broadcast([P, 2, ROPE])) \
                    .then_inc(vector_steps, v.step())
            for i in range(NT):
                v.wait_ge(*when(f"qr.out{i}"))
                rope_vector(v, q_r[:, i, :].rearrange("p (h d) -> p h d", d=ROPE), i, ROT2, ROT1, tmp_m)
            v.wait_ge(vector_steps, v.n)
            nc.vector.tensor_copy(stat[:, 63:64], stat[:, 63:64]).then_inc(vector_steps, v.step("mla.rot"))
            turned_vector(v, "krt", krT, bank=4, chunks=1)
            turned_vector(v, "qrt", qrT, bank=5, chunks=4)
            softmax_vector(v, mla, o_m, float(NOPE + ROPE) ** -0.5,
                           lambda i: blockm[:, P:2 * P] if i == 0 else blockm[:, :])
            turned_vector(v, "mla_turn", yT, bank=0)
            post_vector(v, "mla_out", col("norm2", 5), MOD2[1] + G1, 4)

        def later_tensor(t):
            swa_tensor(t)
            norm_tensor(t, "n2_1")
            peer_score_tensor(t, 1)
            peer_out_tensor(t, 1)
            last_norm_tensor(t)
            mlstm_tensor(t)
            mlp_tensor(t, 0)
            mla_tensor(t)
            mlp_tensor(t, 1)

        def later_scalar(a):
            swa_scalar(a)
            norm_scalar(a, "n2_1", ["swa_out.x"])
            peer_score_scalar(a, 1)
            loop_mod_scalar(a, FIRST_STRIPS + LOOP_STRIPS)
            peer_out_scalar(a, 1)
            last_norm_scalar(a)
            mlstm_scalar(a)
            mlp_scalar(a, 0, "ml_out.x")
            mla_scalar(a)
            mlp_scalar(a, 1, "mla_out.x")

        def later_vector(v):
            swa_vector(v)
            norm_vector(v, "n2_1", col("norm1", 3), MOD1[1] + SC2, MOD1[1] + SH2)
            peer_choose_vector(v, 1)
            peer_routes_vector(v, 1)
            peer_out_vector(v, 1)
            last_norm_vector(v)
            mlstm_vector(v)
            mlp_vector(v, 0)
            mla_vector(v)
            mlp_vector(v, 1)

        block = ctx.enter_context(nc.Block())

        @block.sync
        def _(sp):
            load_inputs_sync(sp)
            for j in range(RING):
                sp.dma_start(ring[:, j, :], io["stream"][j]).then_inc(slab_landed[j], 16)
            last = N_SLABS
            with sp.Fori(1, last // RING) as i:
                for j in range(RING):
                    sp.wait_ge(slab_used, i * RING + (j + 1 - RING))
                    sp.dma_start(ring[:, j, :], io["stream"][bass.ds(i * RING + j, 1), :, :]
                                 .rearrange("a p n -> (a p) n")).then_inc(slab_landed[j], 16)
            for s in range(last // RING * RING, last):
                sp.wait_ge(slab_used, s - RING + 1)
                sp.dma_start(ring[:, s % RING, :], io["stream"][s]).then_inc(slab_landed[s % RING], 16)
            key, n = marks.get("x.final", ("V", 1))
            sp.wait_ge(sems[key], n)
            sp.dma_start(io["out"], x[:, :, :]).then_inc(out_written, 16)
            sp.wait_ge(out_written, 16)

        @block.gpsimd
        def _(pool):
            g = Steps(pool, "G")
            constants_gpsimd(g)
            for l in range(2):
                peer_routes_gpsimd(g, l)

        @block.scalar
        def _(act):
            a = Steps(act, "A")
            act.wait_ge(inputs_landed, ALL_INPUTS)
            nc.scalar.activation(c_act[:, :], cols[:, 0:16], ACT.Silu).then_inc(scalar_steps, a.step("c_act"))
            first_mod_loads(act)
            trig_scalar(a)
            norm_scalar(a, "n1", [])
            gla_scalar(a)
            norm_scalar(a, "n2_0", ["gla_out.x"])
            peer_score_scalar(a, 0)
            loop_mod_scalar(a, FIRST_STRIPS)
            peer_out_scalar(a, 0)
            later_scalar(a)

        @block.vector
        def _(dve):
            v = Steps(dve, "V")
            v.wait_ge(*when("constants"))
            trig_vector(v)
            first_mod_vector(v)
            norm_vector(v, "n1", col("norm1", 0), MOD1[0] + SC1, MOD1[0] + SH1)
            gla_vector(v)
            norm_vector(v, "n2_0", col("norm1", 1), MOD1[0] + SC2, MOD1[0] + SH2)
            peer_choose_vector(v, 0)
            peer_routes_vector(v, 0)
            peer_out_vector(v, 0)
            later_vector(v)
            v.wait_ge(vector_steps, v.n)
            nc.vector.tensor_copy(stat[:, 0:1], stat[:, 0:1]).then_inc(vector_steps, v.step("x.final"))

        @block.tensor
        def _(pe):
            t = Steps(pe, "T")
            first_mod_tensor(t)
            free[0] = free[1] = ["first_strip5"]
            norm_tensor(t, "n1")
            gla_tensor(t)
            norm_tensor(t, "n2_0")
            peer_score_tensor(t, 0)
            peer_out_tensor(t, 0)
            later_tensor(t)
    return new_marks


def pack(inputs):
    f = np.float32

    def T(w):
        k, n = w.shape
        b = w.reshape(k // P, P, n // P, P).transpose(2, 1, 0, 3).reshape(n // P, P, -1)
        per = 4 if k == LORA_Q else SLAB // b.shape[2]
        b = b.reshape(n // P // per, per, P, -1).transpose(0, 2, 1, 3).reshape(n // P // per, P, -1)
        return fill(b)

    def M(w, per):
        k, n = w.shape
        return fill(w.reshape(k // P // per, per, P, n).transpose(0, 2, 1, 3).reshape(k // P // per, P, -1))

    def fill(b):
        out = np.zeros((b.shape[0], P, SLAB), f)
        out[:, :, :b.shape[2]] = b
        return out

    def vec(a, n):
        return np.asarray(a).reshape(-1, n, P).transpose(2, 0, 1).reshape(P, -1)

    g = {k: np.asarray(v) for k, v in inputs.items()}
    gin, ain = g["gla_w_in"][0], g["a_w_in_2"][0]
    qb = g["b_w_qb_2"][0].reshape(LORA_Q, MLA_H, NOPE + ROPE)
    ukv = g["w_ukv_2"].reshape(LORA_KV, MLA_H, 2 * P)
    order = [8 * (c // 4) + c % 4 + 4 * j for c in range(8) for j in range(2)]
    swa_q = g["swa_w_q"][0].reshape(D, SWA_H, SWA_D)[:, order].reshape(D, D)
    parts = {
        "gla_qk": T(gin[:, :D]), "gla_v": M(gin[:, D:2 * D], 2), "gla_og": M(gin[:, 2 * D:3 * D], 2),
        "gla_out": M(g["gla_w_out"][0], 2), "kv": M(g["kv_w"], 4), "swa_q": M(swa_q, 2),
        "swa_out": M(g["swa_w_out"][0], 2),
        "ml_qk": T(ain[:, :D]), "ml_v": M(ain[:, D:2 * D], 2), "ml_o": M(ain[:, 2 * D:3 * D], 2),
        "ml_out": M(g["a_w_out_2"][0], 2), "qa": M(g["b_w_qa_2"][0], 4), "dkv": M(g["w_dkv_2"], 4),
        "qb_nope": T(np.ascontiguousarray(qb[:, :, :NOPE]).reshape(LORA_Q, -1)),
        "qb_rope": M(np.ascontiguousarray(qb[:, [0, 4, 1, 5, 2, 6, 3, 7], NOPE:]).reshape(LORA_Q, -1), 3),
        "ukv_k": T(np.ascontiguousarray(ukv[:, :, :P]).reshape(LORA_KV, -1)),
        "ukv_v": M(np.ascontiguousarray(ukv[:, :, P:]).reshape(LORA_KV, -1), 2),
        "mla_out": M(g["b_w_o_2"][0], 2),
    }
    for l in range(2):
        parts[f"peer_q{l}"] = T(g["peer_w_q"][l])
        u = g["peer_u"][l].reshape(64, 2, P, DC, P).transpose(0, 4, 1, 3, 2).reshape(64, P, SLAB)
        parts[f"u{l}"] = u
        parts[f"v{l}"] = g["peer_v"][l].reshape(64, 2, P, D).transpose(0, 2, 1, 3).reshape(64, P, SLAB)
        parts[f"ffn1_{l}"] = T(g["ffn_w1_2"][l])
        parts[f"ffn2_{l}"] = M(g["ffn_w2_2"][l], 2)
    stream = np.empty((N_SLABS, P, SLAB), f)
    for name, n in PLAN:
        assert parts[name].shape[0] == n, name
        stream[START[name]:START[name] + n] = parts[name]

    def strips(w):
        return w.reshape(DC, P, -1, D).transpose(2, 0, 1, 3).reshape(-1, P, D)
    mod = np.concatenate([strips(g["mod_w"][0]), strips(g["mod_w"][1]), strips(g["kv_mod_w"]),
                          strips(g["mod_w_2"][0]), strips(g["mod_w_2"][1]), strips(g["kv_mod_w_2"])])
    colv = np.concatenate([
        vec(g["c"], 8), vec(g["c_2"], 8), vec(g["mod_b"], 8), vec(g["kv_mod_b"], 8), vec(g["mod_b_2"], 8),
        vec(g["kv_mod_b_2"], 8), vec(g["norm_g"], 8), vec(g["kv_norm_g"], 8), vec(g["final_norm_g"], 8),
        vec(g["norm_g_2"], 8), vec(g["kv_norm_2"], 8), vec(g["gla_b_g2"], 4), vec(g["b_q_norm_2"], 3),
        vec(g["kv_lora_norm_2"], 2)], axis=1)
    inv1 = f(500000.0) ** (-np.arange(0, 2 * ROT1, 2, dtype=f) / f(2 * ROT1))
    inv2 = f(10000.0) ** (-np.arange(0, 2 * ROT2, 2, dtype=f) / f(2 * ROT2))
    rowv = np.concatenate([g["swa_sinks"].ravel(), g["a_b_gates_2"].ravel(), inv1, inv2, g["gla_norm_g"].ravel(),
                           g["a_head_norm_2"].ravel()])[None].astype(f)
    pos = np.concatenate([g["positions"].reshape(NT, P).T, g["positions_2"].reshape(NT, P).T], axis=1)

    def chunked(w):
        return w.reshape(DC, P, -1).transpose(1, 0, 2)
    c = np.ascontiguousarray
    return {
        "stream": stream, "mod": c(mod), "cols": c(colv), "rows": rowv, "pos": c(pos).astype(np.int32),
        "subk": c(g["peer_subkeys"].transpose(3, 0, 1, 2)), "w_gates": c(chunked(ain[:, 3 * D:])),
        "w_gl": c(chunked(gin[:, 3 * D:])), "w_g2": c(g["gla_w_g2"][0]),
        "x": c(g["x"].reshape(NT, P, D).transpose(1, 0, 2)),
    }


def kernel(**inputs):
    import concourse.bacc as bacc
    from concourse.bass_utils import run_bass_kernel_spmd

    arrays = pack(inputs)
    marks = {}
    for _ in range(2):
        nc = bacc.Bacc("TRN2", target_bir_lowering=False, num_devices=1)
        io = {name: nc.dram_tensor(f"in_{name}", a.shape, mybir.dt.from_np(a.dtype), kind="ExternalInput").ap()
              for name, a in arrays.items()}
        io["out"] = nc.dram_tensor("out_x", (P, NT, D), F32, kind="ExternalOutput").ap()
        marks = build(nc, io, marks)
    r = run_bass_kernel_spmd(nc, [{f"in_{name}": a for name, a in arrays.items()}], core_ids=[0])
    out = r.results[0]["out_x"]
    return np.ascontiguousarray(np.asarray(out).transpose(1, 0, 2)).reshape(1, SEQ, D)
```

```python
from contextlib import ExitStack

import numpy as np

import concourse.bass as bass
from concourse import mybir
from concourse.alu_op_type import AluOpType as ALU

ACT = mybir.ActivationFunctionType
AX = mybir.AxisListType.X
F32 = mybir.dt.float32
I32 = mybir.dt.int32
U32 = mybir.dt.uint32
F32R = mybir.dt.float32r

P = 128
D = 1024
DC = D // P
SEQ = 256
NT = SEQ // P
EPS = 1e-6
SLAB = 2048
RING = 2
BANK = 512
NEG = -1.0e30

H_GLA, DV = 4, 256
GATE_TAU = 16.0
CHUNK = 64
SWA_H, SWA_KV, SWA_D = 16, 4, 64
PEER_H, KEYS, TOPK = 8, 128, 16
N_EXP = KEYS * KEYS
HK = PEER_H * TOPK
LORA_Q, LORA_KV, NOPE, ROPE, MLA_H = 384, 256, 128, 64, 8
FF = 4096
ROT1, ROT2 = 8, 32

PLAN = [("gla_qk", 4), ("gla_v", 4), ("gla_og", 4), ("gla_out", 4),
        ("peer_q0", 8), ("u0", 64), ("v0", 64),
        ("kv", 2), ("swa_q", 4), ("swa_out", 4),
        ("peer_q1", 8), ("u1", 64), ("v1", 64),
        ("ml_qk", 4), ("ml_v", 4), ("ml_o", 4), ("ml_out", 4), ("ffn1_0", 16), ("ffn2_0", 16),
        ("qa", 2), ("dkv", 2), ("qb_nope", 2), ("qb_rope", 1), ("ukv_k", 1), ("ukv_v", 1),
        ("mla_out", 4), ("ffn1_1", 16), ("ffn2_1", 16)]
START = {}
N_SLABS = 0
MLP_ROOM = 8192
for _name, _n in PLAN:
    START[_name] = N_SLABS
    N_SLABS += _n

SPLIT = ["peer_q0", "u0", "v0", "peer_q1", "u1", "v1", "ffn1_0", "ffn2_0", "ffn1_1", "ffn2_1"]
PLAIN = []
for _name, _n in PLAN:
    for _ in range(_n):
        PLAIN.append((PLAIN[-1] if PLAIN else 0) + (_name not in SPLIT))
TILES = 128
TILE0 = {}
_at = 0
for _name, _n in PLAN:
    if _name in SPLIT:
        TILE0[_name] = _at
        _at += 2 * _n

STRIPS = 28
FIRST_STRIPS = 6
LOOP_STRIPS = 11
MOD1 = [0, 6]
KVMOD1 = 12
MOD2 = [14, 20]
KVMOD2 = 26
SH1, SC1, G1, SH2, SC2, G2 = range(6)

COLS = {}
N_COLS = 0
for _name, _n in [("c", 8), ("c2", 8), ("mod_b", STRIPS * 8), ("norm1", 32), ("kvn1", 8), ("fin", 8),
                  ("norm2", 64), ("kvn2", 8), ("b_g2", 4), ("qn", 3), ("kvl", 2), ("pos", 4)]:
    COLS[_name] = N_COLS
    N_COLS += _n
COLS_POS = COLS["pos"]
N_COLS -= 4

ROWS = {}
N_ROWS = 0
for _name, _n in [("sinks", 16), ("gates_b", 8), ("inv", ROT1 + ROT2), ("gla_norm", DV), ("head_norm", D)]:
    ROWS[_name] = N_ROWS
    N_ROWS += _n
N_ROWS_KEPT = ROWS["gla_norm"]

TWO_PI = 6.283185307179586
TWO_PI_A = 6.28125
TWO_PI_B = float(np.float32(round((TWO_PI - TWO_PI_A) * 2**21) / 2**21))
TWO_PI_C = float(np.float32(TWO_PI - TWO_PI_A - TWO_PI_B))


def build(nc, io, marks):
    new_marks = {}
    with ExitStack() as ctx:
        def sb(name, shape, dt=F32):
            return ctx.enter_context(nc.sbuf_tensor(name, shape, dt))

        def sem(name):
            return ctx.enter_context(nc.semaphore(name))

        with ExitStack() as scope:
            scope.enter_context(nc.sbuf_tensor("mlp_room", [P, MLP_ROOM], F32))
            mlp_hi, mlp_lo = (scope.enter_context(nc.sbuf_tensor(n, [P, DC, SEQ], F32R)) for n in ("mlp_hi", "mlp_lo"))
            hid_hi, hid_lo = (scope.enter_context(nc.sbuf_tensor(n, [P, FF // P, SEQ], F32R)) for n in ("hid_hi", "hid_lo"))
        gate = sb("gate", [P, KEYS * SEQ])
        ring = sb("ring", [P, RING, SLAB])
        small = sb("small", [P, 4224])
        cols = sb("cols", [P, N_COLS])
        rows = sb("rows", [P, N_ROWS_KEPT])
        subk = sb("subk", [P, 2, 2, KEYS])
        w_gates = sb("w_gates", [P, DC, 8])
        modc = sb("modc", [P, STRIPS, 8])
        c_act = sb("c_act", [P, 16])
        scale_c = sb("scale_c", [P, 8])
        scale_c2 = sb("scale_c2", [P, 8])
        ident = sb("ident", [P, P])
        ones = sb("ones", [P, P])
        zeros = sb("zeros", [P, P])
        iota = sb("iota", [P, P])
        band = sb("band", [P, 2 * P])
        after = sb("after", [P, 2 * P])
        blockm = sb("blockm", [P, 2 * P])
        upper = sb("upper", [P, P])
        trig = sb("trig", [P, 2, NT, ROT1 + ROT2])
        stat = sb("stat", [P, 64])
        ps = ctx.enter_context(nc.psum_tensor("ps", [P, 8, BANK], F32))
        pos_i = sb("pos_i", [P, 4], I32)
        q_i = sb("q_i", [P, NT * 40], I32)
        split_hi = sb("split_hi", [P, 2, D], F32R)
        split_lo = sb("split_lo", [P, 2, D], F32R)
        with ExitStack() as scope:
            hT = scope.enter_context(nc.sbuf_tensor("hT", [P, DC, SEQ], F32))
            x = scope.enter_context(nc.sbuf_tensor("x", [P, NT, D], F32))
        with ExitStack() as scope:
            hT_lo = scope.enter_context(nc.sbuf_tensor("hT_lo", [P, DC, SEQ], F32R))
            hT_hi = scope.enter_context(nc.sbuf_tensor("hT_hi", [P, DC, SEQ], F32R))
        mod_w = sb("mod_w", [P, 2, D])
        mod_acc = sb("mod_acc", [P, D])[:, :]
        gate_hi = sb("gate_hi", [P, 2, SEQ], F32R)
        gate_lo = sb("gate_lo", [P, 2, SEQ], F32R)

        class Area:
            def __init__(self, buf, at=0):
                self.buf, self.at = buf, at

            def take(self, *shape):
                n = int(np.prod(shape))
                ap = self.buf[:, self.at:self.at + n]
                self.at += n
                if len(shape) == 2:
                    return ap.rearrange("p (a b) -> p a b", a=shape[0])
                if len(shape) == 3:
                    return ap.rearrange("p (a b c) -> p a b c", a=shape[0], b=shape[1])
                if len(shape) == 4:
                    return ap.rearrange("p (a b c d) -> p a b c d", a=shape[0], b=shape[1], c=shape[2])
                return ap

        def bc(ap, *shape):
            return ap.to_broadcast([P, *shape])

        common = Area(gate)
        xn = common.take(NT, D)
        row = common.take(D)
        diag = common.take(8, P)
        yT = common.take(DC, SEQ)
        LAYER = common.at

        vector_steps, scalar_steps, tensor_steps, gpsimd_steps = (
            sem("vector_steps"), sem("scalar_steps"), sem("tensor_steps"), sem("gpsimd_steps"))
        slab_landed = [[sem(f"slab_landed{j}_{e}") for e in range(2)] for j in range(RING)]
        slab_used = sem("slab_used")
        hi_made, lo_made = sem("hi_made"), sem("lo_made")
        gate_lo_made = [sem("gate_lo_made_gpsimd"), sem("gate_lo_made_vector")]
        hi_free, lo_free = sem("hi_free"), sem("lo_free")
        banks_free = sem("routes_banks_free")
        x_kept, x_back = sem("x_kept"), sem("x_back")
        sems = {"V": vector_steps, "A": scalar_steps, "T": tensor_steps, "G": gpsimd_steps, "S": slab_used, "L": lo_free}
        inputs_landed = sem("inputs_landed")
        gla_in_landed = sem("gla_inputs_landed")
        head_norm_landed = sem("head_norm_landed")
        first_mod_landed = [[sem(f"first_mod_landed_{q}{k}") for k in range(DC)] for q in ("scalar", "gpsimd")]
        first_mod_used = sem("first_mod_used")
        mod_landed = [sem("mod_landed0"), sem("mod_landed1")]
        mod_used = sem("mod_used")
        strip_added = sem("strip_added")
        strip_summed = sem("strip_summed")
        strip_stored = sem("strip_stored")
        u_drained = sem("u_drained")
        hot_rows, hot_cols = sem("hot_rows"), sem("hot_cols")
        hot_equal = sem("hot_equal")
        mlp_drained, mlp_squared, hid_made = sem("mlp_drained"), sem("mlp_squared"), sem("hid_made")
        routes_full = sem("routes_full")
        out_written = sem("out_written")

        class Steps:
            def __init__(self, eng, key):
                self.eng, self.key, self.n, self.seen = eng, key, 0, {}

            def step(self, mark=None):
                self.n += 1
                if mark:
                    new_marks[mark] = (self.key, self.n)
                return 1

            def wait_ge(self, semaphore, value):
                if self.seen.get(id(semaphore), 0) < value:
                    self.seen[id(semaphore)] = value
                    self.eng.wait_ge(semaphore, value)

        def when(mark):
            key, value = marks.get(mark, ("V", 1))
            return sems[key], value

        def slab_done(s, mark=None):
            if mark:
                new_marks[mark] = ("S", PLAIN[s])
            return 1

        def ps_reg(bank, col, n):
            return ps[:, bank, col:col + n]

        G0 = Area(gate, LAYER)
        gla_wgl = G0.take(DC, 16)
        gla_wg2 = G0.take(512)
        gla_ng = G0.take(DV)
        first_mod = G0.take(DC, D)
        first_acc = gate[:, 2 * D:4 * D].rearrange("p (a b) -> p a b", a=2)
        ang = G0.take(NT, 40)
        angq = G0.take(NT, 40)
        GLA_AT = G0.at

        def load_inputs_sync(sp):
            sp.dma_start(cols[:, :], io["cols"]).then_inc(inputs_landed, 16)
            sp.dma_start(rows[:, :], io["rows"][0, 0:N_ROWS_KEPT].partition_broadcast(P)).then_inc(inputs_landed, 16)
            sp.dma_start(pos_i[:, :], io["pos"]).then_inc(inputs_landed, 16)
            sp.dma_start(subk[:, :, :, :], io["subk"]).then_inc(inputs_landed, 16)
            sp.dma_start(w_gates[:, :, :], io["w_gates"]).then_inc(inputs_landed, 16)
            sp.dma_start(x[:, :, :], io["x"]).then_inc(inputs_landed, 16)
            sp.dma_start(gla_wgl, io["w_gl"]).then_inc(inputs_landed, 16)
            sp.dma_start(gla_wg2[0:16], io["w_g2"]).then_inc(inputs_landed, 16)
            sp.dma_start(gla_ng, io["rows"][0, ROWS["gla_norm"]:ROWS["gla_norm"] + DV].partition_broadcast(P)).then_inc(inputs_landed, 16)
        ALL_INPUTS = 9 * 16

        def col(name, i=0):
            return cols[:, COLS[name] + 8 * i:COLS[name] + 8 * i + 8]

        mod_slots = [mod_w[:, k, :] for k in range(2)]

        def first_mod_loads(eng, strips):
            for s in strips:
                for k in range(DC):
                    if s:
                        eng.wait_ge(first_mod_used, (s - 1) * DC + k + 1)
                    eng.dma_start(first_mod[:, k, :], io["mod"][s * DC + k]).then_inc(first_mod_landed[s >= 2][k], 16)

        def first_mod_vector(v, strips):
            v.wait_ge(*when("c_act"))
            for s in strips:
                acc = first_acc[:, s % 2, :]
                if s >= 2:
                    v.wait_ge(*when(f"first_strip{s - 2}.sum"))
                for k in range(DC):
                    v.eng.wait_ge(first_mod_landed[s >= 2][k], 16 * (s + 1 - 2 * (s >= 2)))
                    w = first_mod[:, k, :]
                    if k == 0:
                        ins = nc.vector.tensor_scalar(acc, w, c_act[:, 0:1], None, ALU.mult)
                    else:
                        v.eng.wait_ge(first_mod_used, s * DC + k)
                        ins = nc.vector.scalar_tensor_tensor(out=acc, in0=w, scalar=c_act[:, k:k + 1], in1=acc,
                                                             op0=ALU.mult, op1=ALU.add)
                    ins.then_inc(first_mod_used, 1)

        def first_mod_store(v, strips, bank):
            v.wait_ge(*when(f"first_strip{strips[1]}.sum"))
            for n, s in enumerate(strips):
                nc.vector.tensor_tensor(modc[:, s, :], ps_reg(bank, 8 * n, 8),
                                        cols[:, COLS["mod_b"] + 8 * s:COLS["mod_b"] + 8 * s + 8], ALU.add) \
                    .then_inc(vector_steps, v.step(f"first_strip{s}"))

        def strip_sum_tensor(acc, bank, at=0):
            for j in range(8):
                last = nc.tensor.matmul(ps[:, bank, at + j:at + j + 1], acc[:, j * P:(j + 1) * P], ones[:, 0:1],
                                        start=True, stop=True)
            return last

        def first_mod_tensor(t, strips, bank):
            for mark in free[bank]:
                t.wait_ge(*when(mark))
            for n, s in enumerate(strips):
                t.eng.wait_ge(first_mod_used, (s + 1) * DC)
                strip_sum_tensor(first_acc[:, s % 2, :], bank, 8 * n) \
                    .then_inc(tensor_steps, t.step(f"first_strip{s}.sum"))
            free[bank] = [f"first_strip{strips[1]}"]

        def strip_chunk_load(a, i, s0, k, head):
            done = s0 - FIRST_STRIPS
            if not (head and done == 0 and k < 2):
                a.eng.wait_ge(mod_used, i * DC + (done * DC + k - 1))
            a.eng.dma_start(mod_slots[k % 2], io["mod"][bass.ds(i * DC + (s0 * DC + k), 1), :, :]
                            .rearrange("a p n -> (a p) n")).then_inc(mod_landed[k % 2], 16)

        def strip_chunk_vector(v, i, s0, k, c0):
            done = s0 - FIRST_STRIPS
            v.eng.wait_ge(mod_landed[k % 2], i * 64 + (64 * done + 16 * (k // 2) + 16))
            if k == 0:
                ins = nc.vector.tensor_scalar(mod_acc, mod_slots[0], c_act[:, c0:c0 + 1], None, ALU.mult)
            else:
                v.eng.wait_ge(mod_used, i * DC + (done * DC + k))
                ins = nc.vector.scalar_tensor_tensor(out=mod_acc, in0=mod_slots[k % 2],
                                                     scalar=c_act[:, c0 + k:c0 + k + 1], in1=mod_acc,
                                                     op0=ALU.mult, op1=ALU.add)
            ins.then_inc(mod_used, 1)

        def strip_store_vector(v, i, s0):
            v.eng.wait_ge(strip_summed, i + (s0 - FIRST_STRIPS + 1))
            nc.vector.tensor_tensor(
                modc[:, bass.ds(i + s0, 1), :].rearrange("p a n -> p (a n)"), ps_reg(4, 0, 8),
                cols[:, bass.ds(i * 8 + (COLS["mod_b"] + 8 * s0), 8)], ALU.add).then_inc(strip_stored, 1)

        def row_from_col(v_or_t, name, source, bank, who):
            if who == "V":
                v = v_or_t
                v.wait_ge(vector_steps, v.n)
                nc.vector.tensor_tensor(diag, ident[:, :].unsqueeze(1).to_broadcast([P, 8, P]),
                                        source.unsqueeze(2).to_broadcast([P, 8, P]), ALU.mult) \
                    .then_inc(vector_steps, v.step(f"{name}.diag"))
            else:
                t = v_or_t
                t.wait_ge(*when(f"{name}.diag"))
                for mark in free[bank]:
                    t.wait_ge(*when(mark))
                for mark in free[bank + 1]:
                    t.wait_ge(*when(mark))
                for n in range(2):
                    nc.tensor.matmul(ps[:, bank + n, :], ones[:, :],
                                     diag[:, 4 * n:4 * n + 4, :].rearrange("p a b -> p (a b)"),
                                     start=True, stop=True).then_inc(tensor_steps, t.step(f"{name}.sum{n}"))
                    free[bank + n] = [f"{name}.row{n}"]

        def row_store(v, name, bank):
            for n in range(2):
                v.wait_ge(*when(f"{name}.sum{n}"))
                nc.vector.tensor_copy(row[:, n * BANK:(n + 1) * BANK], ps[:, bank + n, :]) \
                    .then_inc(vector_steps, v.step(f"{name}.row{n}"))

        free = {b: [] for b in range(8)}

        def junk(n, size):
            return xn.rearrange("p a b -> p (a b)")[:, n * size:(n + 1) * size]

        def stats_scalar(a, name, after, src=None, n=D, parts=NT):
            for i in range(parts):
                for mark in after:
                    a.wait_ge(*when(f"{mark}{i}" if f"{mark}{i}" in marks else mark))
                s = x[:, i, :] if src is None else src(i)
                nc.scalar.activation(junk(i, n), s, ACT.Square,
                                     accum_out=stat[:, i:i + 1]).then_inc(scalar_steps, a.step(f"{name}.ss"))

        def rstd_vector(v, name, n=D, parts=NT):
            v.wait_ge(*when(f"{name}.ss"))
            v.wait_ge(vector_steps, v.n)
            nc.vector.tensor_scalar(stat[:, 16:16 + parts], stat[:, 0:parts], 1.0 / n, EPS, ALU.mult, ALU.add) \
                .then_inc(vector_steps, v.step(f"{name}.var"))
            v.wait_ge(*when(f"{name}.std"))
            nc.vector.reciprocal(stat[:, 48:48 + parts], stat[:, 32:32 + parts]) \
                .then_inc(vector_steps, v.step(f"{name}.rstd"))
            v.wait_ge(vector_steps, v.n)

        def std_scalar(a, name, parts=NT):
            a.wait_ge(*when(f"{name}.var"))
            nc.scalar.activation(stat[:, 32:32 + parts], stat[:, 16:16 + parts], ACT.Sqrt) \
                .then_inc(scalar_steps, a.step(f"{name}.std"))

        def norm_scalar(a, name, after):
            stats_scalar(a, name, after)
            std_scalar(a, name)
            a.wait_ge(*when(f"{name}.rstd"))
            nc.scalar.activation(xn[:, 1, :], x[:, 1, :], ACT.Copy, scale=stat[:, 49:50]) \
                .then_inc(scalar_steps, a.step(f"{name}.xn1"))

        def norm_vector(v, name, gain, sc, sh):
            rstd_vector(v, name)
            nc.vector.tensor_scalar(xn[:, 0, :], x[:, 0, :], stat[:, 48:49], None, ALU.mult) \
                .then_inc(vector_steps, v.step(f"{name}.xn0"))
            nc.vector.scalar_tensor_tensor(out=scale_c[:, :], in0=modc[:, sc, :], scalar=1.0, in1=gain,
                                           op0=ALU.add, op1=ALU.mult).then_inc(vector_steps, v.step())
            v.wait_ge(vector_steps, v.n)
            turned_vector(v, name, hT, lambda c: scale_c[:, c:c + 1], lambda c: modc[:, sh, c:c + 1])

        def turn_tensor(t, name, src, ready, bank=0, chunks=DC):
            for c in range(chunks):
                b = bank + c // 2
                if c % 2 == 0:
                    for mark in free[b]:
                        t.wait_ge(*when(mark))
                for i in range(NT):
                    for mark in ready(i, c):
                        t.wait_ge(*when(mark))
                    ins = nc.tensor.transpose(ps[:, b, (c % 2) * SEQ + i * P:(c % 2) * SEQ + (i + 1) * P],
                                              src(i, c), ident[:, :])
                if c % 2 or c == chunks - 1:
                    ins.then_inc(tensor_steps, t.step(f"{name}.turned{c // 2}"))
                    free[b] = [f"{name}.T{c}"]

        def turned_vector(v, name, dst, mul=None, add=None, bank=0, chunks=DC, out=None):
            for c in range(chunks):
                v.wait_ge(*when(f"{name}.turned{c // 2}"))
                src = ps[:, bank + c // 2, (c % 2) * SEQ:(c % 2 + 1) * SEQ]
                if mul is None:
                    ins = nc.vector.tensor_copy(dst[:, c, :], src)
                elif add is None:
                    ins = nc.vector.tensor_scalar(dst[:, c, :], src, mul(c), None, ALU.mult)
                else:
                    ins = nc.vector.tensor_scalar(dst[:, c, :], src, mul(c), add(c), ALU.mult, ALU.add)
                ins.then_inc(vector_steps, v.step(f"{out or name}.T{c}"))

        def norm_tensor(t, name):
            turn_tensor(t, name, lambda i, c: xn[:, i, c * P:(c + 1) * P], lambda i, c: [f"{name}.xn{i}"])

        def slab(t, s):
            for e in range(2):
                t.eng.wait_ge(slab_landed[s % RING][e], 16 * (s // RING + 1))
            return ring[:, s % RING, :]

        def gemm_T(t, name, weights, blocks, chunks, src, ready, bank=0, nbanks=4):
            per = min(blocks, 4 if chunks == 3 else SLAB // (chunks * P))
            for b in range(blocks):
                s = START[weights] + b // per
                w = slab(t, s) if b % per == 0 else ring[:, s % RING, :]
                bk = bank + (b // 2) % nbanks
                if b % 2 == 0:
                    for mark in free[bk]:
                        t.wait_ge(*when(mark))
                for c in range(chunks):
                    for mark in ready(c):
                        t.wait_ge(*when(mark))
                    at = (b % per) * chunks * P + c * P
                    ins = nc.tensor.matmul(ps[:, bk, (b % 2) * SEQ:(b % 2 + 1) * SEQ], w[:, at:at + P], src[:, c, :],
                                           start=(c == 0), stop=(c == chunks - 1))
                if b % per == per - 1:
                    ins.then_inc(slab_used, slab_done(s, f"{name}.full{b // 2}"))
                elif b % 2:
                    ins.then_inc(tensor_steps, t.step(f"{name}.full{b // 2}"))
                if b % 2:
                    free[bk] = [f"{name}.out{b // 2}"]

        def gemm_M(t, name, weights, chunks, per, width, src, ready, bank=0):
            nbs = (width + BANK - 1) // BANK
            for nb in range(nbs):
                for i in range(NT):
                    for mark in free[bank + 2 * nb + i]:
                        t.wait_ge(*when(mark))
            for c in range(chunks):
                s = START[weights] + c // per
                w = slab(t, s) if c % per == 0 else ring[:, s % RING, :]
                for mark in ready(c):
                    t.wait_ge(*when(mark))
                for nb in range(nbs):
                    n = min(BANK, width - nb * BANK)
                    at = (c % per) * width + nb * BANK
                    for i in range(NT):
                        ins = nc.tensor.matmul(ps[:, bank + 2 * nb + i, 0:n], src[:, c, i * P:(i + 1) * P],
                                               w[:, at:at + n], start=(c == 0), stop=(c == chunks - 1))
                        if c == chunks - 1:
                            if (nb, i) != (nbs - 1, NT - 1):
                                ins.then_inc(tensor_steps, t.step(f"{name}.full{2 * nb + i}"))
                            free[bank + 2 * nb + i] = [f"{name}.out{2 * nb + i}"]
                if c == chunks - 1:
                    ins.then_inc(slab_used, slab_done(s, f"{name}.full{2 * nbs - 1}"))
                elif c % per == per - 1:
                    ins.then_inc(slab_used, slab_done(s))

        def residual_vector(v, name, ready, bank=0, scale=None, returned=0):
            for i in range(NT):
                for nb in range(2):
                    b = bank + 2 * nb + i
                    cut = slice(nb * BANK, (nb + 1) * BANK)
                    v.wait_ge(*when(ready(nb, i)))
                    s = 1.0 if scale is None else scale(i)
                    nc.vector.scalar_tensor_tensor(out=xn[:, i, cut], in0=ps[:, b, :], scalar=s, in1=row[:, cut],
                                                   op0=ALU.mult, op1=ALU.mult) \
                        .then_inc(vector_steps, v.step(f"{name}.out{2 * nb + i}"))
                v.wait_ge(vector_steps, v.n)
                if returned:
                    v.wait_ge(x_back, 16 * returned)
                nc.vector.tensor_tensor(x[:, i, :], x[:, i, :], xn[:, i, :], ALU.add) \
                    .then_inc(vector_steps, v.step(f"{name}.x{i}"))
            new_marks[f"{name}.x"] = new_marks[f"{name}.x{NT - 1}"]
            v.wait_ge(vector_steps, v.n)

        def constants_gpsimd(g):
            for buf, val in ((ident, 0.0), (ones, 1.0), (zeros, 0.0), (band, 0.0), (after, 0.0),
                             (blockm, 0.0), (upper, 1.0), (gmask_f, 1.0)):
                nc.gpsimd.memset(buf[:, :], val).then_inc(gpsimd_steps, g.step())
            nc.gpsimd.iota(iota[:, :], pattern=[[1, P]], base=0, channel_multiplier=0,
                           allow_small_or_imprecise_dtypes=True).then_inc(gpsimd_steps, g.step())
            g.wait_ge(gpsimd_steps, g.n)
            nc.gpsimd.affine_select(out=ident[:, :], in_=ident[:, :], compare_op=ALU.not_equal, fill=1.0, base=0,
                                    pattern=[[-1, P]], channel_multiplier=1).then_inc(gpsimd_steps, g.step())
            for m in (band, after):
                nc.gpsimd.affine_select(out=m[:, P:], in_=m[:, P:], compare_op=ALU.is_ge, fill=NEG, base=0,
                                        pattern=[[-1, P]], channel_multiplier=1).then_inc(gpsimd_steps, g.step())
            nc.gpsimd.affine_select(out=band[:, 0:P], in_=band[:, 0:P], compare_op=ALU.is_ge, fill=NEG, base=-1,
                                    pattern=[[1, P]], channel_multiplier=-1).then_inc(gpsimd_steps, g.step())
            nc.gpsimd.affine_select(out=upper[:, :], in_=upper[:, :], compare_op=ALU.is_ge, fill=0.0, base=0,
                                    pattern=[[1, P]], channel_multiplier=-1).then_inc(gpsimd_steps, g.step())
            nc.gpsimd.memset(blockm[0:CHUNK, P + CHUNK:], NEG).then_inc(gpsimd_steps, g.step())
            nc.gpsimd.affine_select(out=gmask_f[:, :], in_=gmask_f[:, :], compare_op=ALU.is_ge, fill=0.0, base=0,
                                    pattern=[[1, P]], channel_multiplier=-1).then_inc(gpsimd_steps, g.step())
            g.wait_ge(gpsimd_steps, g.n)
            nc.gpsimd.memset(gmask_f[0:CHUNK, CHUNK:P], 0.0).then_inc(gpsimd_steps, g.step("constants"))

        def trig_vector(v):
            v.eng.wait_ge(inputs_landed, ALL_INPUTS)
            posf = stat[:, 56:60]
            nc.vector.tensor_copy(posf, pos_i[:, :]).then_inc(vector_steps, v.step())
            v.wait_ge(vector_steps, v.n)
            inv = rows[:, ROWS["inv"]:ROWS["inv"] + 40]
            for i in range(NT):
                for (k, a, b) in ((0, 0, ROT1), (1, ROT1, ROT1 + ROT2)):
                    nc.vector.tensor_scalar(ang[:, i, a:b], inv[:, a:b], posf[:, 2 * k + i:2 * k + i + 1], None,
                                            ALU.mult).then_inc(vector_steps, v.step())
            v.wait_ge(vector_steps, v.n)
            af = ang.rearrange("p a b -> p (a b)")
            qf = angq.rearrange("p a b -> p (a b)")
            nc.vector.tensor_scalar(qf, af, 1.0 / TWO_PI, None, ALU.mult).then_inc(vector_steps, v.step())
            v.wait_ge(vector_steps, v.n)
            nc.vector.tensor_copy(q_i[:, :], qf).then_inc(vector_steps, v.step())
            v.wait_ge(vector_steps, v.n)
            nc.vector.tensor_copy(qf, q_i[:, :]).then_inc(vector_steps, v.step())
            v.wait_ge(vector_steps, v.n)
            for part in (TWO_PI_A, TWO_PI_B, TWO_PI_C):
                nc.vector.scalar_tensor_tensor(out=af, in0=qf, scalar=-part, in1=af, op0=ALU.mult, op1=ALU.add) \
                    .then_inc(vector_steps, v.step())
                v.wait_ge(vector_steps, v.n)

            def fold(dst):
                for cmp, lim, add in ((ALU.is_gt, TWO_PI / 2, -TWO_PI), (ALU.is_lt, -TWO_PI / 2, TWO_PI)):
                    nc.vector.tensor_scalar(qf, dst, lim, add, cmp, ALU.mult).then_inc(vector_steps, v.step())
                    v.wait_ge(vector_steps, v.n)
                    nc.vector.tensor_tensor(dst, dst, qf, ALU.add).then_inc(vector_steps, v.step())
                    v.wait_ge(vector_steps, v.n)
                nc.vector.tensor_scalar(dst, dst, 3.1415925, -3.1415925, ALU.min, ALU.max) \
                    .then_inc(vector_steps, v.step())
                v.wait_ge(vector_steps, v.n)
            ts = trig[:, 0, :, :].rearrange("p a b -> p (a b)")
            tc = trig[:, 1, :, :].rearrange("p a b -> p (a b)")
            fold(af)
            nc.vector.tensor_copy(ts, af).then_inc(vector_steps, v.step())
            nc.vector.tensor_scalar(tc, af, TWO_PI / 4, None, ALU.add).then_inc(vector_steps, v.step())
            v.wait_ge(vector_steps, v.n)
            fold(tc)
            nc.vector.tensor_copy(qf, tc).then_inc(vector_steps, v.step("angles"))

        def trig_scalar(a):
            a.wait_ge(*when("angles"))
            ts = trig[:, :, :, :].rearrange("p q a b -> p (q a b)")
            nc.scalar.activation(ts, ts, ACT.Sin).then_inc(scalar_steps, a.step("trig"))

        S1 = Area(gate, GLA_AT)
        q = S1.take(H_GLA, SEQ)
        k = S1.take(H_GLA, SEQ)
        b_ = S1.take(H_GLA, SEQ)
        e_pos = S1.take(H_GLA, SEQ)
        e_neg = S1.take(H_GLA, SEQ)
        e_dec = S1.take(H_GLA, SEQ)
        kd = S1.take(NT, H_GLA, P)
        q_own = S1.take(H_GLA, NT, 2, P)
        sc_T = S1.take(NT, H_GLA, P)
        state = S1.take(3, H_GLA, DV)
        glT = S1.take(SEQ)
        gmask_f = S1.take(P)
        o_ = S1.take(NT, D)
        assert S1.at <= KEYS * SEQ
        v_, og = (small[:, n * NT * D:(n + 1) * NT * D].rearrange("p (a b) -> p a b", a=NT) for n in range(2))
        b_flat = b_.rearrange("p a b -> p (a b)")
        NCH = SEQ // CHUNK

        def gla_tensor(t):
            gemm_T(t, "gla_qk", "gla_qk", 8, DC, hT, lambda c: [f"n1.T{c}"])
            for mark in free[4]:
                t.wait_ge(*when(mark))
            for c in range(DC):
                ins = nc.tensor.matmul(ps[0:16, 4, 0:SEQ], gla_wgl[:, c, :], hT[:, c, :], start=(c == 0), stop=(c == DC - 1))
            ins.then_inc(tensor_steps, t.step("gl.full"))
            gemm_z(t)
            gemm_M(t, "gla_v", "gla_v", DC, 2, D, hT, lambda c: [], bank=0)
            first_mod_tensor(t, (2, 3), 7)
            for i in range(NT):
                for mark in free[4 + i]:
                    t.wait_ge(*when(mark))
                t.wait_ge(*when("gla.kd_T"))
                for h in range(H_GLA):
                    ins = nc.tensor.transpose(ps[:, 4 + i, h * P:(h + 1) * P], kdT[:, h, i * P:(i + 1) * P], ident[:, :])
                ins.then_inc(tensor_steps, t.step(f"gla.kd_turned{i}"))
                free[4 + i] = [f"gla.kd{i}"]
            for i in range(NT):
                for mark in free[6 + i]:
                    t.wait_ge(*when(mark))
                t.wait_ge(*when("gla.kt"))
                for h in range(H_GLA):
                    ins = nc.tensor.matmul(ps[:, 6 + i, h * P:(h + 1) * P], kt[:, h, i * P:(i + 1) * P],
                                           q[:, h, i * P:(i + 1) * P], start=True, stop=True)
                ins.then_inc(tensor_steps, t.step(f"gla.scores{i}"))
                free[6 + i] = [f"gla.masked{i}"]
            gemm_M(t, "gla_og", "gla_og", DC, 2, D, hT, lambda c: [], bank=0)
            first_mod_tensor(t, (4, 5), 7)
            for n in range(NCH - 1):
                i, lo = n // 2, (n % 2) * CHUNK
                bk = 4 + 2 * (n % 2)
                for mark in free[bk]:
                    t.wait_ge(*when(mark))
                for mark in free[bk + 1]:
                    t.wait_ge(*when(mark))
                t.wait_ge(*when(f"gla.kd{i}"))
                t.wait_ge(*when(f"gla_v.out{i}"))
                t.wait_ge(*when(f"gla_v.out{2 + i}"))
                for h in range(H_GLA):
                    ins = nc.tensor.matmul(ps[:, bk + h // 2, (h % 2) * DV:(h % 2 + 1) * DV],
                                           kd[lo:lo + CHUNK, i, h, :], v_[lo:lo + CHUNK, i, h * DV:(h + 1) * DV],
                                           start=True, stop=True)
                ins.then_inc(tensor_steps, t.step(f"gla.kv{n}"))
                free[bk] = free[bk + 1] = [f"gla.state{n}"]
            for i in range(NT):
                t.wait_ge(*when(f"gla.masked{i}"))
                t.wait_ge(*when("gla.q_own"))
                for g in range(2):
                    bk = (0 if i == 0 else 2) + g
                    for mark in free[bk]:
                        t.wait_ge(*when(mark))
                    for h in (2 * g, 2 * g + 1):
                        o = ps[:, bk, (h % 2) * DV:(h % 2 + 1) * DV]
                        srcs = [n for n in (2 * i, 2 * i + 1) if n > 0]
                        nc.tensor.matmul(o, sc_T[:, i, h, :], v_[:, i, h * DV:(h + 1) * DV], start=True, stop=False)
                        for n in srcs:
                            t.wait_ge(*when(f"gla.state{n - 1}"))
                            ins = nc.tensor.matmul(o, q_own[:, h, i, n % 2, :], state[:, n - 1, h, :],
                                                   start=False, stop=(n == srcs[-1]))
                    ins.then_inc(tensor_steps, t.step(f"gla.o{i}{g}"))
                    free[bk] = [f"gla.oc{i}{g}"]
            turn_tensor(t, "gla.on", lambda i, c: o_[:, i, c * P:(c + 1) * P], lambda i, c: [f"gla.gated{i}"], bank=4)
            row_from_col(t, "g1_0", None, 0, "T")
            gemm_M(t, "gla_out", "gla_out", DC, 2, D, yT, lambda c: [f"gla.on.T{c}"], bank=0)

        kdT, kt = e_dec, k

        def gemm_z(t):
            t.wait_ge(*when("glT"))
            for h in range(H_GLA):
                for mark in free[5 + h // 2]:
                    t.wait_ge(*when(mark))
                ins = nc.tensor.matmul(ps[:, 5 + h // 2, (h % 2) * SEQ:(h % 2 + 1) * SEQ],
                                       gla_wg2[0:16, h * P:(h + 1) * P], glT[0:16, :], start=True, stop=True)
                if h % 2:
                    ins.then_inc(tensor_steps, t.step(f"z.full{h // 2}"))
            free[5], free[6] = ["gla.z"], ["gla.z"]
            free[4] = ["glT"]

        def gla_scalar(a):
            for g in range(4):
                a.wait_ge(*when(f"gla_qk.full{g}"))
                dst = (q if g < 2 else k)[:, 2 * (g % 2):2 * (g % 2) + 2, :].rearrange("p a b -> p (a b)")
                nc.scalar.activation(dst, ps[:, g, :], ACT.Copy).then_inc(scalar_steps, a.step(f"gla_qk.out{g}"))
            a.wait_ge(*when("gl.full"))
            nc.scalar.activation(glT[0:16, :], ps[0:16, 4, 0:SEQ], ACT.Copy).then_inc(scalar_steps, a.step("glT"))
            a.wait_ge(*when("gla.z"))
            ep = e_pos.rearrange("p a b -> p (a b)")
            nc.scalar.activation(ep, b_flat, ACT.Abs).then_inc(scalar_steps, a.step())
            a.wait_ge(scalar_steps, a.n)
            nc.scalar.activation(ep, ep, ACT.Exp, scale=-1.0).then_inc(scalar_steps, a.step())
            a.wait_ge(scalar_steps, a.n)
            nc.scalar.activation(ep, ep, ACT.Ln, bias=1.0).then_inc(scalar_steps, a.step("gla.ln"))
            for g in range(4):
                a.wait_ge(*when(f"gla_v.full{g}"))
                nc.scalar.activation(v_[:, g % 2, (g // 2) * BANK:(g // 2 + 1) * BANK], ps[:, g, :], ACT.Copy) \
                    .then_inc(scalar_steps, a.step(f"gla_v.out{g}"))
            a.wait_ge(*when("gla.b"))
            nc.scalar.activation(ep, b_flat, ACT.Exp).then_inc(scalar_steps, a.step("gla.e_pos"))
            nc.scalar.activation(e_neg.rearrange("p a b -> p (a b)"), b_flat, ACT.Exp, scale=-1.0) \
                .then_inc(scalar_steps, a.step("gla.e_neg"))
            a.wait_ge(*when("gla.bdec"))
            nc.scalar.activation(e_dec.rearrange("p a b -> p (a b)"), e_dec.rearrange("p a b -> p (a b)"), ACT.Exp) \
                .then_inc(scalar_steps, a.step("gla.e_dec"))
            for i in range(NT):
                a.wait_ge(*when(f"gla.kd_turned{i}"))
                nc.scalar.activation(kd[:, i, :, :].rearrange("p a b -> p (a b)"), ps[:, 4 + i, :], ACT.Copy) \
                    .then_inc(scalar_steps, a.step(f"gla.kd{i}"))
            for g in range(4):
                a.wait_ge(*when(f"gla_og.full{g}"))
                nc.scalar.activation(og[:, g % 2, (g // 2) * BANK:(g // 2 + 1) * BANK], ps[:, g, :], ACT.Silu) \
                    .then_inc(scalar_steps, a.step(f"gla_og.out{g}"))
            for i in range(NT):
                for g in range(2):
                    bk = 2 * i + g
                    a.wait_ge(*when(f"gla.o{i}{g}"))
                    for h in (2 * g, 2 * g + 1):
                        nc.scalar.activation(junk(4 * i + h, DV), ps[:, bk, (h % 2) * DV:(h % 2 + 1) * DV], ACT.Square,
                                             accum_out=stat[:, 4 * i + h:4 * i + h + 1]) \
                            .then_inc(scalar_steps, a.step("gla.r.ss"))
                    nc.scalar.activation(o_[:, i, g * BANK:(g + 1) * BANK], ps[:, bk, :], ACT.Copy) \
                        .then_inc(scalar_steps, a.step(f"gla.oc{i}{g}"))
            std_scalar(a, "gla.r", 8)

        def gla_vector(v):
            for h in range(H_GLA):
                v.wait_ge(*when(f"z.full{h // 2}"))
                nc.vector.tensor_scalar(b_[:, h, :], ps[:, 5 + h // 2, (h % 2) * SEQ:(h % 2 + 1) * SEQ],
                                        cols[:, COLS["b_g2"] + h:COLS["b_g2"] + h + 1], None, ALU.add) \
                    .then_inc(vector_steps, v.step("gla.z"))
            v.wait_ge(vector_steps, v.n)
            ep = e_pos.rearrange("p a b -> p (a b)")
            en = e_neg.rearrange("p a b -> p (a b)")
            v.wait_ge(*when("gla.ln"))
            nc.vector.scalar_tensor_tensor(out=en, in0=b_flat, scalar=0.0, in1=ep, op0=ALU.min, op1=ALU.subtract) \
                .then_inc(vector_steps, v.step())
            v.wait_ge(vector_steps, v.n)
            nc.vector.tensor_scalar(en, en, 1.0 / GATE_TAU, None, ALU.mult).then_inc(vector_steps, v.step())
            restart = e_dec.rearrange("p a b -> p (a b)")
            nc.vector.memset(restart, 1.0).then_inc(vector_steps, v.step())
            v.wait_ge(vector_steps, v.n)
            nc.vector.memset(restart.rearrange("p (n c) -> p n c", c=CHUNK)[:, :, 0:1], 0.0) \
                .then_inc(vector_steps, v.step())
            v.wait_ge(vector_steps, v.n)
            nc.vector.tensor_tensor_scan(b_flat, restart, en, 0.0, ALU.mult, ALU.add) \
                .then_inc(vector_steps, v.step("gla.b"))
            v.wait_ge(vector_steps, v.n)
            b4 = b_flat.rearrange("p (n c) -> p n c", c=CHUNK)
            nc.vector.tensor_tensor(restart.rearrange("p (n c) -> p n c", c=CHUNK),
                                    b4[:, :, CHUNK - 1:CHUNK].to_broadcast([P, H_GLA * NCH, CHUNK]), b4,
                                    ALU.subtract).then_inc(vector_steps, v.step("gla.bdec"))
            qf, kf = q.rearrange("p a b -> p (a b)"), k.rearrange("p a b -> p (a b)")
            v.wait_ge(*when("gla_qk.out3"))
            v.wait_ge(*when("gla.e_pos"))
            nc.vector.scalar_tensor_tensor(out=qf, in0=qf, scalar=float(P) ** -0.5, in1=ep,
                                           op0=ALU.mult, op1=ALU.mult).then_inc(vector_steps, v.step())
            v.wait_ge(*when("gla.e_dec"))
            nc.vector.tensor_tensor(restart, kf, restart, ALU.mult).then_inc(vector_steps, v.step("gla.kd_T"))
            nc.vector.tensor_tensor(kf, kf, en, ALU.mult).then_inc(vector_steps, v.step("gla.kt"))
            qo = q_own.rearrange("p a b c d -> p (a b c d)")
            nc.vector.memset(qo, 0.0).then_inc(vector_steps, v.step())
            v.wait_ge(vector_steps, v.n)
            for n in range(2):
                for i in range(NT):
                    nc.vector.tensor_copy(q_own[:, :, i, n, n * CHUNK:(n + 1) * CHUNK],
                                          q[:, :, i * P + n * CHUNK:i * P + (n + 1) * CHUNK]) \
                        .then_inc(vector_steps, v.step("gla.q_own"))
            first_mod_store(v, (2, 3), 7)
            for i in range(NT):
                st = sc_T[:, i, :, :]
                nc.vector.memset(st.rearrange("p a b -> p (a b)"), 0.0).then_inc(vector_steps, v.step())
                v.wait_ge(vector_steps, v.n)
                v.wait_ge(*when(f"gla.scores{i}"))
                nc.vector.copy_predicated(st, gmask_f.bitcast(U32).unsqueeze(1).to_broadcast([P, H_GLA, P]),
                                          ps[:, 6 + i, :].rearrange("p (a b) -> p a b", a=H_GLA)) \
                    .then_inc(vector_steps, v.step(f"gla.masked{i}"))
            first_mod_vector(v, (4, 5))
            first_mod_store(v, (4, 5), 7)
            for n in range(NCH - 1):
                bk = 4 + 2 * (n % 2)
                v.wait_ge(*when(f"gla.kv{n}"))
                for h in range(H_GLA):
                    src = ps[:, bk + h // 2, (h % 2) * DV:(h % 2 + 1) * DV]
                    if n == 0:
                        ins = nc.vector.tensor_copy(state[:, 0, h, :], src)
                    else:
                        at = (n + 1) * CHUNK - 1
                        ins = nc.vector.scalar_tensor_tensor(out=state[:, n, h, :], in0=state[:, n - 1, h, :],
                                                             scalar=e_pos[:, h, at:at + 1], in1=src,
                                                             op0=ALU.mult, op1=ALU.add)
                    ins.then_inc(vector_steps, v.step(f"gla.state{n}"))
                v.wait_ge(vector_steps, v.n)
            v.wait_ge(*when("gla_og.out3"))
            nc.vector.tensor_tensor(og.rearrange("p a (h e) -> p (a h) e", e=DV),
                                    og.rearrange("p a (h e) -> p (a h) e", e=DV),
                                    gla_ng.unsqueeze(1).to_broadcast([P, NT * H_GLA, DV]), ALU.mult) \
                .then_inc(vector_steps, v.step())
            rstd_vector(v, "gla.r", DV, 8)
            for i in range(NT):
                v.wait_ge(*when(f"gla.oc{i}0"))
                v.wait_ge(*when(f"gla.oc{i}1"))
                for h in range(H_GLA):
                    cut = slice(h * DV, (h + 1) * DV)
                    nc.vector.scalar_tensor_tensor(out=o_[:, i, cut], in0=o_[:, i, cut],
                                                   scalar=stat[:, 48 + 4 * i + h:49 + 4 * i + h], in1=og[:, i, cut],
                                                   op0=ALU.mult, op1=ALU.mult) \
                        .then_inc(vector_steps, v.step(f"gla.gated{i}"))
            row_from_col(v, "g1_0", modc[:, MOD1[0] + G1, :], 0, "V")
            turned_vector(v, "gla.on", yT, bank=4)
            row_store(v, "g1_0", 0)
            v.wait_ge(vector_steps, v.n)
            residual_vector(v, "gla_out", lambda nb, i: f"gla_out.full{2 * nb + i}")

        SCORES = 112 * SEQ
        scores = gate[:, SCORES:].rearrange("p (t g n) -> p t g n", t=NT, g=2 * PEER_H)
        peer_qT = gate[:, LAYER:LAYER + 2 * PEER_H * SEQ].rearrange("p (g n) -> p g n", g=2 * PEER_H)
        A = Area(small)
        e_sel = A.take(3, NT, HK)
        top_v = A.take(2 * PEER_H, TOPK)
        top_if = A.take(2 * PEER_H, TOPK)
        top_i = A.take(2 * PEER_H * TOPK).bitcast(U32).rearrange("p (a b) -> p a b", b=TOPK)
        cand = A.take(TOPK * TOPK)
        cand2 = A.take(TOPK * TOPK)
        c_i = A.take(HK).bitcast(U32)
        c_part = A.take(HK).bitcast(U32)
        c_pf = A.take(HK)
        match = A.take(4, TOPK, TOPK)
        s_left = cand2[:, 0:KEYS]
        assert A.at <= 4224
        B = Area(small)
        selT = B.take(3, SEQ)
        hot_c = [B.take(8, KEYS) for _ in range(2)]
        hot_r = [B.take(8, KEYS // 2) for _ in range(2)]
        assert B.at <= 4224

        def split_gemm_T(t, name, weights, blocks, hi, lo, nbanks=4):
            for b in range(blocks):
                tile = TILE0[weights] + b
                bk = (b // 2) % nbanks
                out = ps[:, bk, (b % 2) * SEQ:(b % 2 + 1) * SEQ]
                if b % 2 == 0:
                    for mark in free[bk]:
                        t.wait_ge(*when(mark))
                t.eng.wait_ge(hi_made, tile + 1)
                for part, src in (("hi", hi), ("lo", lo)):
                    for c in range(DC):
                        t.wait_ge(*when(f"{name}.{part}{c}"))
                        nc.tensor.matmul(out, split_hi[:, b % 2, c * P:(c + 1) * P], src[:, c, :],
                                         start=(src is hi and c == 0), stop=False)
                t.eng.wait_ge(lo_made, tile + 1)
                for c in range(DC):
                    ins = nc.tensor.matmul(out, split_lo[:, b % 2, c * P:(c + 1) * P], hi[:, c, :],
                                           start=False, stop=(c == DC - 1))
                    if c == 0:
                        ins.then_inc(hi_free, 1)
                ins.then_inc(lo_free, 1)
                if b % 2:
                    new_marks[f"{name}.full{b // 2}"] = ("L", 2 + tile + 1)
                    free[bk] = [f"{name}.out{b // 2}"]

        def peer_score_tensor(t, l):
            split_gemm_T(t, f"pq{l}", f"peer_q{l}", 2 * PEER_H, hT_hi, hT_lo)
            for i in range(NT):
                for g in range(2 * PEER_H):
                    bk = 4 + (4 * i + g // 4) % 4
                    if g % 4 == 0:
                        for mark in free[bk]:
                            t.wait_ge(*when(mark))
                        t.wait_ge(*when(f"pq{l}.out{min(7, 2 * (g // 4) + 1)}"))
                    ins = nc.tensor.matmul(ps[:, bk, (g % 4) * KEYS:(g % 4 + 1) * KEYS], peer_qT[:, g, i * P:(i + 1) * P],
                                           subk[:, l, g % 2, :], start=True, stop=True)
                    if g % 4 == 3:
                        ins.then_inc(tensor_steps, t.step(f"sc{l}.full{i}{g // 4}"))
                        free[bk] = [f"sc{l}.out{i}{g // 4}"]
            for b in range(4):
                for mark in free[b]:
                    t.wait_ge(*when(mark))
            first_tile = TILE0[f"u{l}"]

            def u_slab(i, j):
                t.eng.wait_ge(u_drained, i * 4 + (l * 68 + j + 1))
                for e in range(2):
                    tile = first_tile + 2 * j + e
                    out = ps[:, j, e * SEQ:(e + 1) * SEQ]
                    t.eng.wait_ge(hi_made, i * 8 + (tile + 1))
                    for part in (hT_hi, hT_lo):
                        for c in range(DC):
                            nc.tensor.matmul(out, split_hi[:, e, c * P:(c + 1) * P], part[:, c, :],
                                             start=(part is hT_hi and c == 0), stop=False)
                    t.eng.wait_ge(lo_made, i * 8 + (tile + 1))
                    for c in range(DC):
                        ins = nc.tensor.matmul(out, split_lo[:, e, c * P:(c + 1) * P], hT_hi[:, c, :],
                                               start=False, stop=(c == DC - 1))
                        if c == 0:
                            ins.then_inc(hi_free, 1)
                    ins.then_inc(lo_free, 1)

            with t.eng.Fori(0, 11) as i:
                for j in range(4):
                    u_slab(i, j)
            for j in range(3):
                u_slab(11, j)
            peer_turn_tensor(t, l)
            u_slab(11, 3)
            with t.eng.Fori(12, 16) as i:
                for j in range(4):
                    for r in range(2):
                        routes_group_tensor(t, i * 8 + (2 * l * GROUPS + 2 * j + r - 96), r)
                    u_slab(i, j)
            t.seen.clear()

        def split_hi_scalar(a, name, i, j, e):
            tile = TILE0[name] + 2 * j + e
            s = START[name] + j
            slot = s % RING
            if name in ("v0", "v1"):
                a.eng.wait_ge(lo_free, i * 8 + (tile + 1))
                nc.scalar.activation(gate_hi[:, e, :], gate[:, bass.ds(i * (8 * SEQ) + (2 * j + e) * SEQ, SEQ)], ACT.Copy)
            a.eng.wait_ge(slab_landed[slot][e], i * 32 + 16 * (s // RING + 1))
            a.eng.wait_ge(hi_free, i * 8 + (tile + 1))
            nc.scalar.activation(split_hi[:, e, :], ring[:, slot, e * D:(e + 1) * D], ACT.Copy).then_inc(hi_made, 1)

        def split_lo_gpsimd(g, name, i0, i1):
            with g.eng.Fori(i0, i1) as i:
                for j in range(4):
                    slot = (START[name] + j) % RING
                    for e in range(2):
                        tile = TILE0[name] + 2 * j + e
                        g.eng.wait_ge(hi_made, i * 8 + (tile + 1))
                        g.eng.wait_ge(lo_free, i * 8 + (tile + 1))
                        if name in ("v0", "v1") and i0 == 0:
                            cut = gate[:, bass.ds(i * (8 * SEQ) + (2 * j + e) * SEQ, SEQ)]
                            nc.gpsimd.tensor_tensor(gate_lo[:, e, :], cut, gate_hi[:, e, :].bitcast(F32),
                                                    ALU.subtract).then_inc(gate_lo_made[0], 1)
                        nc.gpsimd.tensor_tensor(split_lo[:, e, :], ring[:, slot, e * D:(e + 1) * D],
                                                split_hi[:, e, :].bitcast(F32), ALU.subtract).then_inc(lo_made, 1)
            g.seen.clear()

        def gate_lo_vector(v, l, i, j, e):
            tile = TILE0[f"v{l}"] + 2 * j + e
            v.eng.wait_ge(hi_made, i * 8 + (tile + 1))
            v.eng.wait_ge(lo_free, i * 8 + (tile + 1))
            cut = gate[:, bass.ds(i * (8 * SEQ) + (2 * j + e) * SEQ, SEQ)]
            nc.vector.tensor_tensor(gate_lo[:, e, :], cut, gate_hi[:, e, :].bitcast(F32), ALU.subtract) \
                .then_inc(gate_lo_made[1], 1)

        def peer_score_scalar(a, l):
            for e in range(2):
                split_hi_scalar(a, f"peer_q{l}", 0, 0, e)
            a.wait_ge(x_kept, 16 * (l + 1))
            for c in range(DC):
                a.wait_ge(*when(f"n2_{l}.T{c}"))
                nc.scalar.activation(hT_hi[:, c, :], hT[:, c, :], ACT.Copy) \
                    .then_inc(scalar_steps, a.step(f"pq{l}.hi{c}"))
            for g in range(8):
                for e in range(2):
                    if g < 7:
                        split_hi_scalar(a, f"peer_q{l}", 0, g + 1, e)
                a.wait_ge(*when(f"pq{l}.full{g}"))
                nc.scalar.activation(peer_qT[:, 2 * g:2 * g + 2, :].rearrange("p a b -> p (a b)"),
                                     ps[:, g % 4, :], ACT.Copy).then_inc(scalar_steps, a.step(f"pq{l}.out{g}"))
            for i in range(NT):
                for g in range(4):
                    a.wait_ge(*when(f"sc{l}.full{i}{g}"))
                    nc.scalar.activation(scores[:, i, 4 * g:4 * g + 4, :].rearrange("p a b -> p (a b)"),
                                         ps[:, 4 + g, :], ACT.Copy).then_inc(scalar_steps, a.step(f"sc{l}.out{i}{g}"))
            for j in range(4):
                nc.scalar.activation(stat[:, 60 + j:61 + j], zeros[:, 0:1], ACT.Copy).then_inc(u_drained, 1)

            def drain(i, j):
                a.eng.wait_ge(lo_free, i * 8 + (TILE0[f"u{l}"] + 2 * j + 4))
                nc.scalar.activation(gate[:, bass.ds(i * (8 * SEQ) + 2 * j * SEQ, 2 * SEQ)] if not isinstance(i, int)
                                     else gate[:, i * 8 * SEQ + 2 * j * SEQ:i * 8 * SEQ + 2 * (j + 1) * SEQ],
                                     ps[:, j, :], ACT.Gelu).then_inc(u_drained, 1)

            def step(i, first=False):
                for j in range(4):
                    for e in range(2):
                        split_hi_scalar(a, f"u{l}", i, j, e)
                    if j:
                        drain(i, j - 1)
                    elif not first:
                        drain(i - 1, 3)
            step(0, True)
            with a.eng.Fori(1, 11) as i:
                step(i)
            a.seen.clear()
            a.wait_ge(*when(f"chosen{l}"))
            w = e_sel[:, 2, :, :].rearrange("p a b -> p (a b)")
            nc.scalar.activation(w, w, ACT.Exp).then_inc(scalar_steps, a.step(f"weights{l}.exp"))
            with a.eng.Fori(11, 16) as i:
                step(i)
            drain(15, 3)
            a.seen.clear()

        def top16(v, src, left, vals, idx):
            nc.vector.max(vals[:, 0:8], src).then_inc(vector_steps, v.step())
            v.wait_ge(vector_steps, v.n)
            nc.vector.max_index(idx[:, 0:8], vals[:, 0:8], src).then_inc(vector_steps, v.step())
            nc.vector.match_replace(left, vals[:, 0:8], src, -3.0e38).then_inc(vector_steps, v.step())
            v.wait_ge(vector_steps, v.n)
            nc.vector.max(vals[:, 8:16], left).then_inc(vector_steps, v.step())
            v.wait_ge(vector_steps, v.n)
            nc.vector.max_index(idx[:, 8:16], vals[:, 8:16], left).then_inc(vector_steps, v.step())

        def peer_choose_vector(v, l):
            for c in range(DC):
                v.wait_ge(*when(f"pq{l}.hi{c}"))
                nc.vector.tensor_tensor(hT_lo[:, c, :], hT[:, c, :], hT_hi[:, c, :].bitcast(F32), ALU.subtract) \
                    .then_inc(vector_steps, v.step(f"pq{l}.lo{c}"))
            for i in range(NT):
                for g in range(4):
                    v.wait_ge(*when(f"sc{l}.out{i}{g}"))
                for g in range(2 * PEER_H):
                    top16(v, scores[:, i, g, :], s_left, top_v[:, g, :], top_i[:, g, :])
                v.wait_ge(vector_steps, v.n)
                nc.vector.tensor_copy(top_if, top_i).then_inc(vector_steps, v.step())
                for h in range(PEER_H):
                    v.wait_ge(vector_steps, v.n)
                    nc.vector.tensor_tensor(
                        cand.rearrange("p (a b) -> p a b", a=TOPK),
                        top_v[:, 2 * h, :].unsqueeze(2).to_broadcast([P, TOPK, TOPK]),
                        top_v[:, 2 * h + 1, :].unsqueeze(1).to_broadcast([P, TOPK, TOPK]), ALU.add) \
                        .then_inc(vector_steps, v.step())
                    v.wait_ge(vector_steps, v.n)
                    top16(v, cand, cand2, e_sel[:, 2, i, h * TOPK:(h + 1) * TOPK], c_i[:, h * TOPK:(h + 1) * TOPK])
                v.wait_ge(vector_steps, v.n)
                for part, (op, n) in enumerate(((ALU.logical_shift_right, 4), (ALU.bitwise_and, 15))):
                    nc.vector.tensor_scalar(c_part, c_i, n, None, op).then_inc(vector_steps, v.step())
                    v.wait_ge(vector_steps, v.n)
                    nc.vector.tensor_copy(c_pf, c_part).then_inc(vector_steps, v.step())
                    v.wait_ge(vector_steps, v.n)
                    for hh in range(2):
                        cut = slice(hh * 64, hh * 64 + 64)
                        for h in range(4):
                            hg = 4 * hh + h
                            nc.vector.tensor_tensor(
                                match[:, h, :, :],
                                c_pf[:, hg * TOPK:(hg + 1) * TOPK].unsqueeze(2).to_broadcast([P, TOPK, TOPK]),
                                iota[:, 0:TOPK].unsqueeze(1).to_broadcast([P, TOPK, TOPK]), ALU.is_equal) \
                                .then_inc(vector_steps, v.step())
                        v.wait_ge(vector_steps, v.n)
                        for h in range(4):
                            hg = 4 * hh + h
                            nc.vector.tensor_tensor(
                                match[:, h, :, :], match[:, h, :, :],
                                top_if[:, 2 * hg + part, :].unsqueeze(1).to_broadcast([P, TOPK, TOPK]), ALU.mult) \
                                .then_inc(vector_steps, v.step())
                        v.wait_ge(vector_steps, v.n)
                        nc.vector.tensor_reduce(e_sel[:, part, i, cut], match.rearrange("p a b c -> p (a b) c"),
                                                AX, ALU.add).then_inc(vector_steps, v.step())
                        v.wait_ge(vector_steps, v.n)
            w = e_sel[:, 2, :, :].rearrange("p t (h k) -> p (t h) k", k=TOPK)
            big = stat[:, 0:NT * PEER_H]
            nc.vector.tensor_copy(big.unsqueeze(2), w[:, :, 0:1]).then_inc(vector_steps, v.step())
            v.wait_ge(vector_steps, v.n)
            nc.vector.tensor_tensor(w, w, big.unsqueeze(2).to_broadcast([P, NT * PEER_H, TOPK]), ALU.subtract) \
                .then_inc(vector_steps, v.step(f"chosen{l}"))
            v.wait_ge(*when(f"weights{l}.exp"))
            nc.vector.tensor_reduce(big, w, AX, ALU.add).then_inc(vector_steps, v.step())
            v.wait_ge(vector_steps, v.n)
            nc.vector.reciprocal(stat[:, 16:32], big).then_inc(vector_steps, v.step())
            v.wait_ge(vector_steps, v.n)
            nc.vector.tensor_tensor(w, w, stat[:, 16:32].unsqueeze(2).to_broadcast([P, NT * PEER_H, TOPK]), ALU.mult) \
                .then_inc(vector_steps, v.step(f"weights{l}"))
            for i in range(NT):
                v.wait_ge(*when(f"sel{l}.turned{i}"))
                if i == 0:
                    v.wait_ge(*when(f"sel{l}.turned1"))
                nc.vector.tensor_copy(selT[:, :, i * P:(i + 1) * P],
                                      ps[:, 4 + i, 0:3 * P].rearrange("p (a b) -> p a b", a=3)) \
                    .then_inc(vector_steps, v.step(f"selT{l}"))
            v.wait_ge(vector_steps, v.n)

        def peer_turn_tensor(t, l):
            t.wait_ge(*when(f"weights{l}"))
            for i in range(NT):
                for mark in free[4 + i]:
                    t.wait_ge(*when(mark))
                for part in range(3):
                    ins = nc.tensor.transpose(ps[:, 4 + i, part * P:(part + 1) * P], e_sel[:, part, i, :], ident[:, :])
                ins.then_inc(tensor_steps, t.step(f"sel{l}.turned{i}"))

        GROUPS = SEQ // 8
        HALF = KEYS // 2

        def at(ap2d, i, step, off, n):
            if isinstance(i, int):
                return ap2d[:, i * step + off:i * step + off + n]
            return ap2d[:, bass.ds(i * step + off, n)]

        def routes_group_vector(v, p, i, r, first):
            if not (first and r < 2 and p == 0):
                v.eng.wait_ge(routes_full, i * 4 + (p * GROUPS + r - 1))
            keys = iota[:, (p % 2) * HALF:(p % 2 + 1) * HALF].unsqueeze(1).to_broadcast([P, 8, HALF])
            part = [at(selT[:, n, :], i, 32, 8 * r, 8) for n in range(3)]
            nc.vector.tensor_tensor(hot_r[r % 2], keys, part[0].unsqueeze(2).to_broadcast([P, 8, HALF]),
                                    ALU.is_equal).then_inc(hot_equal, 1)
            nc.vector.tensor_tensor(hot_c[r % 2], iota[:, :].unsqueeze(1).to_broadcast([P, 8, KEYS]),
                                    part[1].unsqueeze(2).to_broadcast([P, 8, KEYS]), ALU.is_equal).then_inc(hot_cols, 1)
            v.eng.wait_ge(hot_equal, i * 4 + (p * GROUPS + r + 1))
            nc.vector.tensor_tensor(hot_r[r % 2], hot_r[r % 2], part[2].unsqueeze(2).to_broadcast([P, 8, HALF]),
                                    ALU.mult).then_inc(hot_rows, 1)
            if r:
                routes_merge_vector(v, p, i, r - 1)
            elif not first:
                routes_merge_vector(v, p, i - 1, 3)

        def routes_merge_vector(v, p, i, r):
            v.eng.wait_ge(routes_full, i * 4 + (p * GROUPS + r + 1))
            gv = gate[:, :].rearrange("p (n t) -> p n t", t=SEQ)[:, (p % 2) * HALF:(p % 2 + 1) * HALF, :]
            if isinstance(i, int):
                dst = gv[:, :, 32 * i + 8 * r:32 * i + 8 * r + 8]
            else:
                dst = gv[:, :, bass.ds(i * 32 + 8 * r, 8)]
            nc.vector.tensor_tensor(dst, dst, ps[:, 5 + r % 2, :].rearrange("p (t n) -> p n t", t=8),
                                    ALU.mult).then_inc(banks_free, 1)

        def peer_routes_vector(v, l):
            s0 = FIRST_STRIPS + l * LOOP_STRIPS
            p = 2 * l
            v.eng.wait_ge(u_drained, l * 68 + 4 + 32)
            for r in range(4):
                routes_group_vector(v, p, 0, r, True)
            with v.eng.Fori(1, 8) as i:
                for r in range(4):
                    routes_group_vector(v, p, i, r, False)
            routes_merge_vector(v, p, 7, 3)
            p = 2 * l + 1
            v.eng.wait_ge(u_drained, (l + 1) * 68)

            def both(i, first):
                for r in range(4):
                    routes_group_vector(v, p, i, r, first)
                    if r == 0 and not first:
                        strip_store_vector(v, i - 1, s0)
                    for k in (2 * r, 2 * r + 1):
                        strip_chunk_vector(v, i, s0, k, 0 if s0 < MOD2[0] else 8)
            both(0, True)
            with v.eng.Fori(1, 8) as i:
                both(i, False)
            routes_merge_vector(v, p, 7, 3)
            assert s0 + 8 == MOD2[0] or s0 > MOD2[0]
            with v.eng.Fori(8, LOOP_STRIPS) as i:
                for k in range(DC):
                    gate_lo_vector(v, l, i, k // 2, k % 2)
                    if k == 0:
                        strip_store_vector(v, i - 1, s0)
                    strip_chunk_vector(v, i, s0, k, 8)
            strip_store_vector(v, LOOP_STRIPS - 1, s0)
            with v.eng.Fori(LOOP_STRIPS, 16) as i:
                for k in range(DC):
                    gate_lo_vector(v, l, i, k // 2, k % 2)
            v.seen.clear()

        def routes_group_tensor(t, n_group, r):
            t.eng.wait_ge(hot_rows, n_group + 1)
            t.eng.wait_ge(hot_cols, n_group + 1)
            t.eng.wait_ge(banks_free, n_group + 1)
            for n in range(8):
                ins = nc.tensor.matmul(ps[:, 5 + r % 2, n * HALF:(n + 1) * HALF], hot_c[r % 2][:, n, :],
                                       hot_r[r % 2][:, n, :], start=True, stop=True)
            ins.then_inc(routes_full, 1)

        def peer_out_tensor(t, l):
            t.eng.wait_ge(u_drained, (l + 1) * 68)
            for b in range(4):
                for n in range(4):
                    nc.tensor.matmul(ps[:, b, n * P:(n + 1) * P], zeros[:, :], zeros[:, :], start=(n == 0), stop=True,
                                     skip_group_check=True)
            first_tile = TILE0[f"v{l}"]
            done = l * LOOP_STRIPS

            def body(i, strip, routes):
                for j in range(4):
                    if routes:
                        routes_group_tensor(t, i * 4 + ((2 * l + 1) * GROUPS + j), j)
                    for e in range(2):
                        tile = first_tile + 2 * j + e
                        t.eng.wait_ge(hi_made, i * 8 + (tile + 1))
                        for w, g in ((split_hi, gate_hi), (split_hi, gate_lo), (split_lo, gate_hi)):
                            if g is gate_lo:
                                half = 0 if routes else 1
                                t.eng.wait_ge(gate_lo_made[half], i * 8 + (64 * (l - half) + 2 * j + e + 1))
                            if w is split_lo:
                                t.eng.wait_ge(lo_made, i * 8 + (tile + 1))
                            for d in range(DC):
                                ins = nc.tensor.matmul(ps[:, d // 2, (d % 2) * SEQ:(d % 2 + 1) * SEQ],
                                                       w[:, e, d * P:(d + 1) * P], g[:, e, :],
                                                       start=False, stop=True, skip_group_check=True)
                                if d == 0 and w is split_lo:
                                    ins.then_inc(hi_free, 1)
                        ins.then_inc(lo_free, 1)
                if strip:
                    t.eng.wait_ge(mod_used, i * DC + (done * DC + DC))
                    strip_sum_tensor(mod_acc, 4).then_inc(strip_summed, 1)
            with t.eng.Fori(0, 8) as i:
                body(i, True, True)
            with t.eng.Fori(8, LOOP_STRIPS) as i:
                body(i, True, False)
            with t.eng.Fori(LOOP_STRIPS, 16) as i:
                body(i, False, False)
            t.seen.clear()
            new_marks[f"peer{l}.full"] = ("L", 2 + first_tile + TILES)
            t.eng.wait_ge(strip_stored, (l + 1) * LOOP_STRIPS)
            turn_name = f"peer{l}"
            for c in range(DC):
                b = 4 + 2 * (c // 4)
                for i in range(NT):
                    t.wait_ge(*when(f"peer{l}.y{c // 2}"))
                    ins = nc.tensor.transpose(ps[:, b + i, (c % 4) * P:(c % 4 + 1) * P], yT[:, c, i * P:(i + 1) * P],
                                              ident[:, :])
                    if c % 4 == 3:
                        ins.then_inc(tensor_steps, t.step(f"{turn_name}.back{2 * (c // 4) + i}"))
                        free[b + i] = [f"peer{l}.res.out{2 * (c // 4) + i}"]
            free[0] = free[1] = [f"peer{l}.y3"]
            free[2] = free[3] = [f"peer{l}.y3"]
            row_from_col(t, f"g2_{l}", None, 0, "T")

        def peer_out_scalar(a, l):
            v0 = FIRST_STRIPS + l * LOOP_STRIPS
            a.eng.wait_ge(banks_free, (2 * l + 1) * GROUPS + 2)
            for i0, i1 in ((0, 8), (8, LOOP_STRIPS), (LOOP_STRIPS, 16)):
                if i0 == 8:
                    a.eng.wait_ge(banks_free, (2 * l + 2) * GROUPS + 2)
                if i0 == 0:
                    for j in range(4):
                        for e in range(2):
                            strip_chunk_load(a, 0, v0, 2 * j + e, True)
                            split_hi_scalar(a, f"v{l}", 0, j, e)
                    i0 = 1
                with a.eng.Fori(i0, i1) as i:
                    for j in range(4):
                        for e in range(2):
                            if i1 <= LOOP_STRIPS:
                                strip_chunk_load(a, i, v0, 2 * j + e, False)
                            split_hi_scalar(a, f"v{l}", i, j, e)
            a.seen.clear()
            a.wait_ge(*when(f"peer{l}.full"))
            for b in range(4):
                nc.scalar.activation(yT[:, 2 * b:2 * b + 2, :].rearrange("p a b -> p (a b)"), ps[:, b, :], ACT.Copy) \
                    .then_inc(scalar_steps, a.step(f"peer{l}.y{b}"))

        def peer_out_vector(v, l):
            v.eng.wait_ge(strip_stored, (l + 1) * LOOP_STRIPS)
            v.wait_ge(*when(f"peer{l}.full"))
            row_from_col(v, f"g2_{l}", modc[:, MOD1[l] + G2, :], 0, "V")
            row_store(v, f"g2_{l}", 0)
            v.wait_ge(vector_steps, v.n)
            residual_vector(v, f"peer{l}.res", lambda nb, i: f"peer{l}.back{2 * nb + i}", bank=4,
                            returned=l + 1)

        def double_norm_vector(v, name, gain, sc, sh, gain2, sc2, sh2, dst2):
            rstd_vector(v, name)
            nc.vector.tensor_scalar(xn[:, 0, :], x[:, 0, :], stat[:, 48:49], None, ALU.mult) \
                .then_inc(vector_steps, v.step(f"{name}.xn0"))
            nc.vector.scalar_tensor_tensor(out=scale_c[:, :], in0=modc[:, sc, :], scalar=1.0, in1=gain,
                                           op0=ALU.add, op1=ALU.mult).then_inc(vector_steps, v.step())
            nc.vector.scalar_tensor_tensor(out=scale_c2[:, :], in0=modc[:, sc2, :], scalar=1.0, in1=gain2,
                                           op0=ALU.add, op1=ALU.mult).then_inc(vector_steps, v.step())
            v.wait_ge(vector_steps, v.n)
            turned_vector(v, name, dst2, lambda c: scale_c2[:, c:c + 1], lambda c: modc[:, sh2, c:c + 1], out=f"{name}.kv")
            turned_vector(v, name, hT, lambda c: scale_c[:, c:c + 1], lambda c: modc[:, sh, c:c + 1])

        def rope_vector(v, buf, i, half, off, tmp):
            heads = buf.shape[1]
            x1, x2 = buf[:, :, 0:half], buf[:, :, half:2 * half]
            s, c = (trig[:, n, i, off:off + half].unsqueeze(1).to_broadcast([P, heads, half]) for n in range(2))
            t4 = [tmp[:, n * heads * half:(n + 1) * heads * half].rearrange("p (h d) -> p h d", h=heads)
                  for n in range(4)]
            v.wait_ge(vector_steps, v.n)
            for dst, a, b in zip(t4, (x1, x2, x2, x1), (c, s, c, s)):
                nc.vector.tensor_tensor(dst, a, b, ALU.mult).then_inc(vector_steps, v.step())
            v.wait_ge(vector_steps, v.n)
            nc.vector.tensor_tensor(x1, t4[0], t4[1], ALU.subtract).then_inc(vector_steps, v.step())
            nc.vector.tensor_tensor(x2, t4[2], t4[3], ALU.add).then_inc(vector_steps, v.step())

        def copy_scalar(a, name, dsts, bank, func=ACT.Copy, width=BANK):
            for n, dst in enumerate(dsts):
                a.wait_ge(*when(f"{name}.full{n}"))
                nc.scalar.activation(dst, ps[:, bank(n), 0:width], func) \
                    .then_inc(scalar_steps, a.step(f"{name}.out{n}"))

        def token_tiles(buf, width=D):
            return [buf[:, n % 2, (n // 2) * BANK:min(width, (n // 2 + 1) * BANK)]
                    for n in range(2 * ((width + BANK - 1) // BANK))]

        class Attention:
            def __init__(self, name, heads, area):
                self.name, self.heads, self.dv = name, heads, D // heads
                self.per = [4, 2]
                self.groups = [heads // p for p in self.per]
                self.prob = [area.take(heads, P), area.take(heads, 2 * P)]
                self.probT = [area.take(heads, P), area.take(heads, 2 * P)]
                self.st = area.take(2, 6, 16)
                self.bank, n = {}, 0
                for i in range(NT):
                    for g in range(self.groups[i]):
                        self.bank["s", i, g] = n % 8
                        n += 1
                for i in range(NT):
                    for g in range(self.groups[i]):
                        self.bank["t", i, g] = n % 8
                        n += 1
                    for b in range(2):
                        self.bank["o", i, b] = n % 8
                        n += 1

        def scores_tensor(t, at_, products, ready):
            for mark in ready:
                t.wait_ge(*when(mark))
            for i in range(NT):
                for g in range(at_.groups[i]):
                    bk = at_.bank["s", i, g]
                    for mark in free[bk]:
                        t.wait_ge(*when(mark))
                    for hh in range(at_.per[i]):
                        for kt in range(i + 1):
                            pairs = products(at_.per[i] * g + hh, i, kt)
                            to = ps[:, bk, (hh * (i + 1) + kt) * P:(hh * (i + 1) + kt + 1) * P]
                            for n, (a, b) in enumerate(pairs):
                                ins = nc.tensor.matmul(to, a, b, start=(n == 0), stop=(n == len(pairs) - 1))
                    ins.then_inc(tensor_steps, t.step(f"{at_.name}.s{i}.{g}"))
                    free[bk] = [f"{at_.name}.sc{i}.{g}"]

        def values_tensor(t, at_, values):
            nm = at_.name
            for i in range(NT):
                for g in range(at_.groups[i]):
                    bk = at_.bank["t", i, g]
                    for mark in free[bk]:
                        t.wait_ge(*when(mark))
                    t.wait_ge(*when(f"{nm}.p{i}.{g}"))
                    flat = at_.prob[i].rearrange("p h k -> p (h k)")
                    for n in range(4):
                        ins = nc.tensor.transpose(ps[:, bk, n * P:(n + 1) * P],
                                                  flat[:, (4 * g + n) * P:(4 * g + n + 1) * P], ident[:, :])
                    ins.then_inc(tensor_steps, t.step(f"{nm}.t{i}.{g}"))
                    free[bk] = [f"{nm}.tc{i}.{g}"]
                hb = at_.heads // 2
                for b in range(2):
                    bk = at_.bank["o", i, b]
                    for mark in free[bk]:
                        t.wait_ge(*when(mark))
                    for h in range(b * hb, (b + 1) * hb):
                        t.wait_ge(*when(f"{nm}.tc{i}.{h // at_.per[i]}"))
                        for kt in range(i + 1):
                            ins = nc.tensor.matmul(ps[:, bk, (h - b * hb) * at_.dv:(h - b * hb + 1) * at_.dv],
                                                   at_.probT[i][:, h, kt * P:(kt + 1) * P], values(kt, h),
                                                   start=(kt == 0), stop=(kt == i))
                    ins.then_inc(tensor_steps, t.step(f"{nm}.o{i}.{b}"))
                    free[bk] = [f"{nm}.oc{i}.{b}"]

        MX, NM, DEN, RD, EX = range(5)

        def softmax_vector(v, at_, dst, scale, mask, sinks=None):
            nm, H = at_.name, at_.heads
            for i in range(NT):
                for g in range(at_.groups[i]):
                    v.wait_ge(*when(f"{nm}.s{i}.{g}"))
                    hs = slice(at_.per[i] * g, at_.per[i] * (g + 1))
                    n = (i + 1) * P
                    nc.vector.scalar_tensor_tensor(
                        out=at_.prob[i][:, hs, :],
                        in0=ps[:, at_.bank["s", i, g], :].rearrange("p (h k) -> p h k", k=n), scalar=scale,
                        in1=mask(i).unsqueeze(1).to_broadcast([P, at_.per[i], n]), op0=ALU.mult, op1=ALU.add) \
                        .then_inc(vector_steps, v.step(f"{nm}.sc{i}.{g}"))
            v.wait_ge(vector_steps, v.n)
            for i in range(NT):
                st = at_.st[:, i]
                nc.vector.tensor_reduce(st[:, MX, 0:H], at_.prob[i], AX, ALU.max).then_inc(vector_steps, v.step())
                v.wait_ge(vector_steps, v.n)
                if sinks is not None:
                    nc.vector.tensor_tensor(st[:, MX, 0:H], st[:, MX, 0:H], sinks, ALU.max) \
                        .then_inc(vector_steps, v.step())
                    v.wait_ge(vector_steps, v.n)
                nc.vector.tensor_scalar(st[:, NM, 0:H], st[:, MX, 0:H], -1.0, None, ALU.mult) \
                    .then_inc(vector_steps, v.step(f"{nm}.nm{i}"))
                if sinks is not None:
                    nc.vector.tensor_tensor(st[:, EX, 0:H], sinks, st[:, MX, 0:H], ALU.subtract) \
                        .then_inc(vector_steps, v.step(f"{nm}.nm{i}"))
            for i in range(NT):
                st = at_.st[:, i]
                v.wait_ge(*when(f"{nm}.p{i}.{at_.groups[i] - 1}"))
                if sinks is not None:
                    v.wait_ge(*when(f"{nm}.sink{i}"))
                    nc.vector.tensor_tensor(st[:, DEN, 0:H], st[:, DEN, 0:H], st[:, EX, 0:H], ALU.add) \
                        .then_inc(vector_steps, v.step())
                    v.wait_ge(vector_steps, v.n)
                nc.vector.reciprocal(st[:, RD, 0:H], st[:, DEN, 0:H]).then_inc(vector_steps, v.step())
                probT_vector(v, at_, i)
                attended_vector(v, at_, dst, i)

        def softmax_scalar(a, at_, sinks=False):
            nm, H = at_.name, at_.heads
            for i in range(NT):
                st = at_.st[:, i]
                a.wait_ge(*when(f"{nm}.nm{i}"))
                for h in range(H):
                    nc.scalar.activation(at_.prob[i][:, h, :], at_.prob[i][:, h, :], ACT.Exp,
                                         bias=st[:, NM, h:h + 1], accum_out=st[:, DEN, h:h + 1]) \
                        .then_inc(scalar_steps, a.step(f"{nm}.p{i}.{h // at_.per[i]}"))
                if sinks:
                    nc.scalar.activation(st[:, EX, 0:H], st[:, EX, 0:H], ACT.Exp) \
                        .then_inc(scalar_steps, a.step(f"{nm}.sink{i}"))

        def probT_vector(v, at_, i):
            nm = at_.name
            flat = at_.probT[i].rearrange("p h k -> p (h k)")
            for g in range(at_.groups[i]):
                v.wait_ge(*when(f"{nm}.t{i}.{g}"))
                nc.vector.tensor_copy(flat[:, g * BANK:(g + 1) * BANK], ps[:, at_.bank["t", i, g], :]) \
                    .then_inc(vector_steps, v.step(f"{nm}.tc{i}.{g}"))

        def attended_vector(v, at_, dst, i):
            nm, hb = at_.name, at_.heads // 2
            v.wait_ge(vector_steps, v.n)
            for b in range(2):
                v.wait_ge(*when(f"{nm}.o{i}.{b}"))
                nc.vector.tensor_tensor(
                    dst[:, i, b * BANK:(b + 1) * BANK].rearrange("p (h e) -> p h e", h=hb),
                    ps[:, at_.bank["o", i, b], :].rearrange("p (h e) -> p h e", h=hb),
                    at_.st[:, i, RD, b * hb:(b + 1) * hb].unsqueeze(2).to_broadcast([P, hb, at_.dv]), ALU.mult) \
                    .then_inc(vector_steps, v.step(f"{nm}.oc{i}.{b}"))

        def turned_out_tensor(t, name, src, ready):
            turn_tensor(t, name, lambda i, c: src[:, i, c * P:(c + 1) * P], lambda i, c: [ready(i, c)], bank=0)

        W = Area(gate, LAYER)
        kvT = W.take(DC, SEQ)
        kv_s = W.take(NT, BANK)
        q_s = W.take(NT, D)
        kT_s = W.take(2, SEQ)
        qT_s = W.take(8, SEQ)
        rope_tmp = W.take(4 * SWA_H * ROT1)
        swa = Attention("swa", SWA_H, W)
        assert W.at <= KEYS * SEQ
        q_s3 = [q_s[:, i, :].rearrange("p (h d) -> p h d", d=SWA_D) for i in range(NT)]
        kv_s3 = [kv_s[:, i, 0:SWA_KV * SWA_D].rearrange("p (h d) -> p h d", d=SWA_D) for i in range(NT)]

        def swa_tensor(t):
            norm_tensor(t, "n1_1")
            gemm_M(t, "kv", "kv", DC, 4, BANK, kvT, lambda c: [f"n1_1.kv.T{c}"], bank=4)
            gemm_M(t, "swa_q", "swa_q", DC, 2, D, hT, lambda c: [f"n1_1.T{c}"], bank=0)
            turn_tensor(t, "swa_k", lambda i, c: kv_s[:, i, c * P:(c + 1) * P], lambda i, c: ["swa.k_rot"], bank=4,
                        chunks=2)
            turn_tensor(t, "swa_qt", lambda i, c: q_s[:, i, c * P:(c + 1) * P], lambda i, c: ["swa.q_rot"], bank=4)

            def products(h, i, kt):
                lo = SWA_D * (h // 4 % 2)
                own = kt if i else 0
                return [(qT_s[lo:lo + SWA_D, 4 * (h // 8) + h % 4, i * P:(i + 1) * P],
                         kT_s[lo:lo + SWA_D, h // 8, own * P:(own + 1) * P])]
            scores_tensor(t, swa, products, ["swa_k.T1", "swa_qt.T7"])
            values_tensor(t, swa, lambda kt, h: kv_s[:, kt, 256 + SWA_D * (h // 4):256 + SWA_D * (h // 4 + 1)])
            turned_out_tensor(t, "swa_o", q_s, lambda i, c: f"swa.oc{i}.{c // 4}")
            row_from_col(t, "g1_1", None, 4, "T")
            gemm_M(t, "swa_out", "swa_out", DC, 2, D, yT, lambda c: [f"swa_o.T{c}"], bank=0)

        def swa_scalar(a):
            norm_scalar(a, "n1_1", ["peer0.res.x"])
            copy_scalar(a, "kv", token_tiles(kv_s, BANK), lambda n: 4 + n)
            copy_scalar(a, "swa_q", token_tiles(q_s), lambda n: n)
            softmax_scalar(a, swa, sinks=True)

        def swa_vector(v):
            double_norm_vector(v, "n1_1", col("norm1", 2), MOD1[1] + SC1, MOD1[1] + SH1,
                               col("kvn1"), KVMOD1 + 1, KVMOD1, kvT)
            for i in range(NT):
                v.wait_ge(*when(f"kv.out{i}"))
                rope_vector(v, kv_s3[i], i, ROT1, 0, rope_tmp)
            v.wait_ge(vector_steps, v.n)
            nc.vector.tensor_copy(stat[:, 63:64], stat[:, 63:64]).then_inc(vector_steps, v.step("swa.k_rot"))
            for i in range(NT):
                v.wait_ge(*when(f"swa_q.out{2 + i}"))
                rope_vector(v, q_s3[i], i, ROT1, 0, rope_tmp)
            v.wait_ge(vector_steps, v.n)
            nc.vector.tensor_copy(stat[:, 63:64], stat[:, 63:64]).then_inc(vector_steps, v.step("swa.q_rot"))
            turned_vector(v, "swa_k", kT_s, bank=4, chunks=2)
            turned_vector(v, "swa_qt", qT_s, bank=4)
            softmax_vector(v, swa, q_s, SWA_D ** -0.5, lambda i: band[:, P:2 * P] if i == 0 else band[:, :],
                           rows[:, ROWS["sinks"]:ROWS["sinks"] + SWA_H])
            turned_vector(v, "swa_o", yT, bank=0)
            row_from_col(v, "g1_1", modc[:, MOD1[1] + G1, :], 4, "V")
            row_store(v, "g1_1", 4)
            v.wait_ge(vector_steps, v.n)
            residual_vector(v, "swa_out", lambda nb, i: f"swa_out.full{2 * nb + i}")

        def last_norm_scalar(a):
            stats_scalar(a, "fin", ["peer1.res.x"])
            std_scalar(a, "fin")

        def last_norm_tensor(t):
            row_from_col(t, "fin", None, 0, "T")

        def last_norm_vector(v):
            row_from_col(v, "fin", col("fin"), 0, "V")
            row_store(v, "fin", 0)
            rstd_vector(v, "fin")
            for i in range(NT):
                nc.vector.scalar_tensor_tensor(out=x[:, i, :], in0=x[:, i, :], scalar=stat[:, 48 + i:49 + i],
                                               in1=row, op0=ALU.mult, op1=ALU.mult) \
                    .then_inc(vector_steps, v.step("fin.x"))
            v.wait_ge(vector_steps, v.n)

        def post_scalar(a, name, bank=0):
            for n in range(4):
                a.wait_ge(*when(f"{name}.full{n}"))
                nc.scalar.activation(junk(n, BANK), ps[:, bank + n, :], ACT.Square, accum_out=stat[:, n:n + 1]) \
                    .then_inc(scalar_steps, a.step(f"{name}.ss"))
            std_scalar(a, name)

        def post_tensor(t, name, bank):
            row_from_col(t, f"{name}.g", None, bank, "T")

        def post_vector(v, name, gain, g, row_bank, bank=0):
            post_gain_vector(v, name, gain, g, row_bank)
            post_rest_vector(v, name, row_bank, bank)

        def post_gain_vector(v, name, gain, g, row_bank):
            nc.vector.tensor_tensor(scale_c2[:, :], modc[:, g, :], gain, ALU.mult).then_inc(vector_steps, v.step())
            row_from_col(v, f"{name}.g", scale_c2[:, :], row_bank, "V")

        def post_rest_vector(v, name, row_bank, bank):
            row_store(v, f"{name}.g", row_bank)
            v.wait_ge(*when(f"{name}.ss"))
            nc.vector.tensor_tensor(stat[:, 0:2], stat[:, 0:2], stat[:, 2:4], ALU.add) \
                .then_inc(vector_steps, v.step())
            rstd_vector(v, name)
            residual_vector(v, name, lambda nb, i: f"{name}.full{2 * nb + i}", bank=bank,
                            scale=lambda i: stat[:, 48 + i:49 + i])

        L = Area(gate, LAYER)
        ml_q = L.take(H_GLA, SEQ)
        ml_k = L.take(H_GLA, SEQ)
        ml_v = L.take(NT, D)
        ml_o = L.take(NT, D)
        ml_h = L.take(NT, D)
        head_row = L.take(D)
        ml_diag = L.take(NT, H_GLA, P)
        ml_g = L.take(NT, 8)
        ml_lf = L.take(NT, H_GLA)
        ml_F = L.take(NT, H_GLA)
        ml_r = L.take(NT, H_GLA)
        ml_t = L.take(NT, H_GLA)
        mls = Attention("ml", H_GLA, L)
        assert L.at <= KEYS * SEQ

        def mlstm_tensor(t):
            norm_tensor(t, "m1")
            gemm_T(t, "ml_qk", "ml_qk", 8, DC, hT, lambda c: [f"m1.T{c}"], bank=0)
            for mark in free[4]:
                t.wait_ge(*when(mark))
            for i in range(NT):
                for c in range(DC):
                    ins = nc.tensor.matmul(ps[:, 4, 8 * i:8 * i + 8], hT[:, c, i * P:(i + 1) * P], w_gates[:, c, :],
                                           start=(c == 0), stop=(c == DC - 1))
            ins.then_inc(tensor_steps, t.step("ml.gates"))
            gemm_M(t, "ml_v", "ml_v", DC, 2, D, hT, lambda c: [], bank=0)
            free[4] = ["ml.pre"]
            t.wait_ge(*when("ml.lf"))
            for mark in free[4]:
                t.wait_ge(*when(mark))
            for mark in free[5]:
                t.wait_ge(*when(mark))
            nc.tensor.matmul(ps[:, 5, 0:4], upper[:, :], ml_lf[:, 0, :], start=True, stop=True)
            nc.tensor.matmul(ps[:, 5, 4:8], ones[:, :], ml_lf[:, 0, :], start=True, stop=False)
            nc.tensor.matmul(ps[:, 5, 4:8], upper[:, :], ml_lf[:, 1, :], start=False, stop=True) \
                .then_inc(tensor_steps, t.step("ml.F"))
            free[5] = ["ml.r"]
            t.wait_ge(*when("ml.diag"))
            for mark in free[6]:
                t.wait_ge(*when(mark))
            for mark in free[7]:
                t.wait_ge(*when(mark))
            for i in range(NT):
                nc.tensor.matmul(ps[:, 6 + i, :], ones[:, :], ml_diag[:, i, :, :].rearrange("p a b -> p (a b)"),
                                 start=True, stop=True).then_inc(tensor_steps, t.step(f"ml.rows{i}"))
                free[6 + i] = ["ml.logits"]
            gemm_M(t, "ml_o", "ml_o", DC, 2, D, hT, lambda c: [], bank=0)
            scores_tensor(t, mls, lambda h, i, kt: [(ml_q[:, h, i * P:(i + 1) * P], ml_k[:, h, kt * P:(kt + 1) * P])],
                          ["ml_qk.out3"])
            t.wait_ge(*when("ml_v.out3"))
            values_tensor(t, mls, lambda kt, h: ml_v[:, kt, h * DV:(h + 1) * DV])
            turned_out_tensor(t, "ml_turn", ml_h, lambda i, c: f"ml.gated{i}")
            post_tensor(t, "ml_out", 4)
            gemm_M(t, "ml_out", "ml_out", DC, 2, D, yT, lambda c: [f"ml_turn.T{c}"], bank=0)

        def mlstm_scalar(a):
            act = a.eng
            act.dma_start(head_row, io["rows"][0, ROWS["head_norm"]:ROWS["head_norm"] + D].partition_broadcast(P)) \
               .then_inc(head_norm_landed, 16)
            norm_scalar(a, "m1", ["fin.x"])
            copy_scalar(a, "ml_qk", [(ml_q, ml_k)[n // 2][:, 2 * (n % 2):2 * (n % 2) + 2, :].rearrange("p a b -> p (a b)")
                                     for n in range(4)], lambda n: n)
            a.wait_ge(*when("ml.pre"))
            nc.scalar.activation(ml_t, ml_g[:, :, 4:8], ACT.Abs).then_inc(scalar_steps, a.step())
            a.wait_ge(scalar_steps, a.n)
            nc.scalar.activation(ml_t, ml_t, ACT.Exp, scale=-1.0).then_inc(scalar_steps, a.step())
            a.wait_ge(scalar_steps, a.n)
            nc.scalar.activation(ml_t, ml_t, ACT.Ln, bias=1.0).then_inc(scalar_steps, a.step("ml.ln"))
            copy_scalar(a, "ml_v", token_tiles(ml_v), lambda n: n)
            a.wait_ge(*when("ml.nm"))
            for i in range(NT):
                for h in range(H_GLA):
                    nc.scalar.activation(mls.prob[i][:, h, :], mls.prob[i][:, h, :], ACT.Exp,
                                         bias=mls.st[:, i, NM, h:h + 1]).then_inc(scalar_steps, a.step(f"ml.e{i}"))
                nc.scalar.activation(mls.st[:, i, EX, 0:4], mls.st[:, i, EX, 0:4], ACT.Exp) \
                    .then_inc(scalar_steps, a.step(f"ml.e{i}"))
            copy_scalar(a, "ml_o", token_tiles(ml_o), lambda n: n, ACT.Sigmoid)
            for i in range(NT):
                a.wait_ge(*when(f"ml.oc{i}.1"))
                for h in range(H_GLA):
                    nc.scalar.activation(junk(4 * i + h, DV), ml_h[:, i, h * DV:(h + 1) * DV], ACT.Square,
                                         accum_out=stat[:, 4 * i + h:4 * i + h + 1]) \
                        .then_inc(scalar_steps, a.step("ml.r2.ss"))
            std_scalar(a, "ml.r2", 8)
            post_scalar(a, "ml_out")

        def mlstm_vector(v):
            norm_vector(v, "m1", col("norm2", 0), MOD2[0] + SC1, MOD2[0] + SH1)
            v.wait_ge(*when("ml.gates"))
            gb = rows[:, ROWS["gates_b"]:ROWS["gates_b"] + 8]
            nc.vector.tensor_tensor(ml_g, ps[:, 4, 0:16].rearrange("p (a b) -> p a b", a=NT),
                                    gb.unsqueeze(1).to_broadcast([P, NT, 8]), ALU.add) \
                .then_inc(vector_steps, v.step("ml.pre"))
            v.wait_ge(*when("ml.ln"))
            v.wait_ge(vector_steps, v.n)
            nc.vector.scalar_tensor_tensor(out=ml_lf, in0=ml_g[:, :, 4:8], scalar=0.0, in1=ml_t,
                                           op0=ALU.min, op1=ALU.subtract).then_inc(vector_steps, v.step("ml.lf"))
            v.wait_ge(*when("ml.F"))
            nc.vector.tensor_copy(ml_F, ps[:, 5, 0:8].rearrange("p (a b) -> p a b", a=NT)) \
                .then_inc(vector_steps, v.step())
            v.wait_ge(vector_steps, v.n)
            nc.vector.tensor_tensor(ml_r, ml_g[:, :, 0:4], ml_F, ALU.subtract).then_inc(vector_steps, v.step("ml.r"))
            v.wait_ge(vector_steps, v.n)
            nc.vector.tensor_tensor(ml_diag.rearrange("p a b c -> p (a b) c"),
                                    ident[:, :].unsqueeze(1).to_broadcast([P, NT * H_GLA, P]),
                                    ml_r.rearrange("p a b -> p (a b)").unsqueeze(2)
                                    .to_broadcast([P, NT * H_GLA, P]), ALU.mult) \
                .then_inc(vector_steps, v.step("ml.diag"))
            for i in range(NT):
                for kt in range(i + 1):
                    v.wait_ge(*when(f"ml.rows{kt}"))
                    mask = after[:, P:2 * P] if kt == i else after[:, 0:P]
                    nc.vector.tensor_tensor(mls.prob[i][:, :, kt * P:(kt + 1) * P],
                                            ps[:, 6 + kt, :].rearrange("p (a b) -> p a b", a=H_GLA),
                                            mask.unsqueeze(1).to_broadcast([P, H_GLA, P]), ALU.add) \
                        .then_inc(vector_steps, v.step("ml.logits"))
            v.wait_ge(vector_steps, v.n)
            for i in range(NT):
                st = mls.st[:, i]
                nc.vector.tensor_reduce(st[:, MX, 0:4], mls.prob[i], AX, ALU.max).then_inc(vector_steps, v.step())
                v.wait_ge(vector_steps, v.n)
                nc.vector.tensor_scalar(st[:, NM, 0:4], st[:, MX, 0:4], 0.0, -1.0, ALU.max, ALU.mult) \
                    .then_inc(vector_steps, v.step())
                v.wait_ge(vector_steps, v.n)
                nc.vector.tensor_tensor(st[:, EX, 0:4], st[:, NM, 0:4], ml_F[:, i, :], ALU.subtract) \
                    .then_inc(vector_steps, v.step("ml.nm"))
            for i in range(NT):
                st = mls.st[:, i]
                v.wait_ge(*when(f"ml.e{i}"))
                for g in range(mls.groups[i]):
                    v.wait_ge(*when(f"ml.s{i}.{g}"))
                    hs = slice(mls.per[i] * g, mls.per[i] * (g + 1))
                    pr = mls.prob[i][:, hs, :]
                    nc.vector.scalar_tensor_tensor(
                        out=pr, in0=ps[:, mls.bank["s", i, g], :].rearrange("p (h k) -> p h k", k=(i + 1) * P),
                        scalar=float(P) ** -0.5, in1=pr, op0=ALU.mult, op1=ALU.mult) \
                        .then_inc(vector_steps, v.step(f"ml.sc{i}.{g}"))
                    new_marks[f"ml.p{i}.{g}"] = ("V", v.n)
            v.wait_ge(vector_steps, v.n)
            for i in range(NT):
                st = mls.st[:, i]
                nc.vector.tensor_reduce(st[:, DEN, 0:4], mls.prob[i], AX, ALU.add).then_inc(vector_steps, v.step())
                v.wait_ge(vector_steps, v.n)
                nc.vector.tensor_scalar(st[:, MX, 0:4], st[:, DEN, 0:4], -1.0, None, ALU.mult) \
                    .then_inc(vector_steps, v.step())
                v.wait_ge(vector_steps, v.n)
                nc.vector.tensor_tensor(st[:, DEN, 0:4], st[:, DEN, 0:4], st[:, MX, 0:4], ALU.max) \
                    .then_inc(vector_steps, v.step())
                v.wait_ge(vector_steps, v.n)
                nc.vector.tensor_tensor(st[:, DEN, 0:4], st[:, DEN, 0:4], st[:, EX, 0:4], ALU.max) \
                    .then_inc(vector_steps, v.step())
                v.wait_ge(vector_steps, v.n)
                nc.vector.reciprocal(st[:, RD, 0:4], st[:, DEN, 0:4]).then_inc(vector_steps, v.step())
                probT_vector(v, mls, i)
                attended_vector(v, mls, ml_h, i)
            v.eng.wait_ge(head_norm_landed, 16)
            v.wait_ge(*when("ml_o.out3"))
            nc.vector.tensor_tensor(ml_o, ml_o, head_row.unsqueeze(1).to_broadcast([P, NT, D]), ALU.mult) \
                .then_inc(vector_steps, v.step())
            rstd_vector(v, "ml.r2", DV, 8)
            for i in range(NT):
                for h in range(H_GLA):
                    cut = slice(h * DV, (h + 1) * DV)
                    nc.vector.scalar_tensor_tensor(out=ml_h[:, i, cut], in0=ml_h[:, i, cut],
                                                   scalar=stat[:, 48 + 4 * i + h:49 + 4 * i + h],
                                                   in1=ml_o[:, i, cut], op0=ALU.mult, op1=ALU.mult) \
                        .then_inc(vector_steps, v.step(f"ml.gated{i}"))
            turned_vector(v, "ml_turn", yT, bank=0)
            post_vector(v, "ml_out", col("norm2", 1), MOD2[0] + G1, 4)

        MLP = Area(gate, LAYER)
        hid = MLP.take(4, 2 * SEQ)
        assert MLP.at <= MLP_ROOM
        MLP_STEPS = FF // P // 8

        def mlp_tensor(t, l):
            norm_tensor(t, f"m2_{l}")
            for b in range(4):
                for mark in free[b]:
                    t.wait_ge(*when(mark))
            for c in range(DC):
                t.wait_ge(*when(f"m2_{l}.hi{c}"))
                t.wait_ge(*when(f"m2_{l}.lo{c}"))
            with t.eng.Fori(0, MLP_STEPS) as i:
                for j in range(4):
                    t.eng.wait_ge(mlp_drained, i * 4 + (l * 20 + j + 1))
                    for e in range(2):
                        tile = TILE0[f"ffn1_{l}"] + 2 * j + e
                        out = ps[:, j, e * SEQ:(e + 1) * SEQ]
                        t.eng.wait_ge(hi_made, i * 8 + (tile + 1))
                        for part in (mlp_hi, mlp_lo):
                            for c in range(DC):
                                nc.tensor.matmul(out, split_hi[:, e, c * P:(c + 1) * P], part[:, c, :],
                                                 start=(part is mlp_hi and c == 0), stop=False)
                        t.eng.wait_ge(lo_made, i * 8 + (tile + 1))
                        for c in range(DC):
                            ins = nc.tensor.matmul(out, split_lo[:, e, c * P:(c + 1) * P], mlp_hi[:, c, :],
                                                   start=False, stop=(c == DC - 1))
                            if c == 0:
                                ins.then_inc(hi_free, 1)
                        ins.then_inc(lo_free, 1)
            t.seen.clear()
            for b in range(4, 8):
                for mark in free[b]:
                    t.wait_ge(*when(mark))
            t.eng.wait_ge(mlp_drained, l * 20 + 20)
            free[0] = free[1] = free[2] = free[3] = []
            post_tensor(t, f"f2_{l}", 0)

            def step(i, first):
                for j in range(4):
                    t.eng.wait_ge(hid_made, i * 4 + (l * 16 + j + 1))
                    for e in range(2):
                        tile = TILE0[f"ffn2_{l}"] + 2 * j + e
                        c0 = 2 * j + e
                        t.eng.wait_ge(hi_made, i * 8 + (tile + 1))
                        for w, h in ((split_hi, hid_hi), (split_hi, hid_lo), (split_lo, hid_hi)):
                            if w is split_lo:
                                t.eng.wait_ge(lo_made, i * 8 + (tile + 1))
                            for nb in range(2):
                                for n in range(NT):
                                    src = h[:, 8 * i + c0, n * P:(n + 1) * P]
                                    ins = nc.tensor.matmul(ps[:, 4 + 2 * nb + n, :], src,
                                                           w[:, e, nb * BANK:(nb + 1) * BANK],
                                                           start=(first and c0 == 0 and h is hid_hi and w is split_hi),
                                                           stop=True, skip_group_check=True)
                                    if w is split_lo and nb == 0 and n == 0:
                                        ins.then_inc(hi_free, 1)
                        ins.then_inc(lo_free, 1)
            for i in range(MLP_STEPS):
                step(i, i == 0)
            for n in range(4):
                new_marks[f"f2_{l}.full{n}"] = ("L", 2 + TILE0[f"ffn2_{l}"] + 8 * MLP_STEPS)
                free[4 + n] = [f"f2_{l}.out{n}"]

        def mlp_scalar(a, l, after_):
            norm_scalar(a, f"m2_{l}", [after_])
            for c in range(DC):
                a.wait_ge(*when(f"m2_{l}.T{c}"))
                nc.scalar.activation(mlp_hi[:, c, :], hT[:, c, :], ACT.Copy) \
                    .then_inc(scalar_steps, a.step(f"m2_{l}.hi{c}"))
            for j in range(4):
                nc.scalar.activation(stat[:, 60 + j:61 + j], zeros[:, 0:1], ACT.Copy).then_inc(mlp_drained, 1)

            def drain(i, j):
                a.eng.wait_ge(lo_free, i * 8 + (TILE0[f"ffn1_{l}"] + 2 * j + 4))
                a.eng.wait_ge(hid_made, i * 4 + (l * 16 + j - 3))
                nc.scalar.activation(hid[:, j, :], ps[:, j, :], ACT.Relu).then_inc(mlp_drained, 1)

            def step(i):
                for j in range(4):
                    for e in range(2):
                        split_hi_scalar(a, f"ffn1_{l}", i, j, e)
                    if j:
                        drain(i, j - 1)
                    else:
                        drain(i - 1, 3)
            for j in range(4):
                for e in range(2):
                    split_hi_scalar(a, f"ffn1_{l}", 0, j, e)
                if j:
                    a.eng.wait_ge(lo_free, TILE0[f"ffn1_{l}"] + 2 * j + 2)
                    nc.scalar.activation(hid[:, j - 1, :], ps[:, j - 1, :], ACT.Relu).then_inc(mlp_drained, 1)
            a.eng.wait_ge(lo_free, TILE0[f"ffn1_{l}"] + 10)
            nc.scalar.activation(hid[:, 3, :], ps[:, 3, :], ACT.Relu).then_inc(mlp_drained, 1)
            for j in range(4):
                for e in range(2):
                    split_hi_scalar(a, f"ffn1_{l}", 1, j, e)
                if j:
                    drain(1, j - 1)
            with a.eng.Fori(2, MLP_STEPS) as i:
                step(i)
            drain(MLP_STEPS - 1, 3)
            with a.eng.Fori(0, MLP_STEPS) as i:
                for j in range(4):
                    for e in range(2):
                        split_hi_scalar(a, f"ffn2_{l}", i, j, e)
            a.seen.clear()
            post_scalar(a, f"f2_{l}", 4)

        def mlp_vector(v, l):
            norm_vector(v, f"m2_{l}", col("norm2", 4 * l + 2), MOD2[l] + SC2, MOD2[l] + SH2)
            for c in range(DC):
                v.wait_ge(*when(f"m2_{l}.hi{c}"))
                nc.vector.tensor_tensor(mlp_lo[:, c, :], hT[:, c, :], mlp_hi[:, c, :].bitcast(F32), ALU.subtract) \
                    .then_inc(vector_steps, v.step(f"m2_{l}.lo{c}"))
            post_gain_vector(v, f"f2_{l}", col("norm2", 4 * l + 3), MOD2[l] + G2, 0)
            with v.eng.Fori(0, MLP_STEPS) as i:
                for j in range(4):
                    h = hid[:, j, :]
                    hi, lo = (part[:, bass.ds(i * 8 + 2 * j, 2), :].rearrange("p a b -> p (a b)")
                              for part in (hid_hi, hid_lo))
                    v.eng.wait_ge(mlp_drained, i * 4 + (l * 20 + 4 + j + 1))
                    nc.vector.tensor_tensor(h, h, h, ALU.mult).then_inc(mlp_squared, 1)
                    v.eng.wait_ge(mlp_squared, i * 8 + (l * 32 + 2 * j + 1))
                    nc.vector.tensor_copy(hi, h).then_inc(mlp_squared, 1)
                    v.eng.wait_ge(mlp_squared, i * 8 + (l * 32 + 2 * j + 2))
                    nc.vector.tensor_tensor(lo, h, hi.bitcast(F32), ALU.subtract).then_inc(hid_made, 1)
            v.seen.clear()
            post_rest_vector(v, f"f2_{l}", 0, bank=4)

        M_ = Area(gate, LAYER)
        kvT2 = M_.take(DC, SEQ)
        qa = M_.take(NT, LORA_Q)
        ckv = M_.take(NT, LORA_KV + ROPE)
        qaT = M_.take(3, SEQ)
        ckvT = M_.take(2, SEQ)
        qnT = M_.take(MLA_H, SEQ)
        knT = M_.take(MLA_H, SEQ)
        q_r = M_.take(NT, MLA_H * ROPE)
        k_r = M_.take(NT, 2 * ROPE)
        qrT = M_.take(4, SEQ)
        krT = M_.take(1, SEQ)
        v_m = M_.take(NT, D)
        tmp_m = M_.take(4 * MLA_H * ROT2)
        o_m = kvT2.rearrange("p a b -> p (a b)").rearrange("p (a b) -> p a b", a=NT)
        mla = Attention("mla", MLA_H, M_)
        assert M_.at <= KEYS * SEQ

        def mla_tensor(t):
            norm_tensor(t, "m1_1")
            gemm_M(t, "qa", "qa", DC, 4, LORA_Q, hT, lambda c: [f"m1_1.T{c}"], bank=4)
            gemm_M(t, "dkv", "dkv", DC, 4, LORA_KV + ROPE, kvT2, lambda c: [], bank=6)
            turn_tensor(t, "qat", lambda i, c: qa[:, i, c * P:(c + 1) * P], lambda i, c: ["mla.qa"], bank=0, chunks=3)
            turn_tensor(t, "ckvt", lambda i, c: ckv[:, i, c * P:(c + 1) * P], lambda i, c: ["mla.qa"], bank=2, chunks=2)
            gemm_T(t, "qn", "qb_nope", MLA_H, 3, qaT, lambda c: [f"qat.T{c}"], bank=4)
            gemm_M(t, "qr", "qb_rope", 3, 3, BANK, qaT, lambda c: [], bank=0)
            gemm_T(t, "kn", "ukv_k", MLA_H, 2, ckvT, lambda c: [f"ckvt.T{c}"], bank=4)
            gemm_M(t, "vm", "ukv_v", 2, 2, D, ckvT, lambda c: [], bank=0)
            turn_tensor(t, "krt", lambda i, c: k_r[:, i, :], lambda i, c: ["mla.rot"], bank=4, chunks=1)
            turn_tensor(t, "qrt", lambda i, c: q_r[:, i, c * P:(c + 1) * P], lambda i, c: ["mla.rot"], bank=5, chunks=4)

            def products(h, i, kt):
                lo = ROPE * (h // 4)
                return [(qnT[:, h, i * P:(i + 1) * P], knT[:, h, kt * P:(kt + 1) * P]),
                        (qrT[lo:lo + ROPE, h % 4, i * P:(i + 1) * P], krT[lo:lo + ROPE, 0, kt * P:(kt + 1) * P])]
            scores_tensor(t, mla, products, ["krt.T0", "qrt.T3", "qn.out3", "kn.out3"])
            t.wait_ge(*when("vm.out3"))
            values_tensor(t, mla, lambda kt, h: v_m[:, kt, h * P:(h + 1) * P])
            turned_out_tensor(t, "mla_turn", o_m, lambda i, c: f"mla.oc{i}.{c // 4}")
            post_tensor(t, "mla_out", 4)
            gemm_M(t, "mla_out", "mla_out", DC, 2, D, yT, lambda c: [f"mla_turn.T{c}"], bank=0)

        def mla_scalar(a):
            norm_scalar(a, "m1_1", ["f2_0.x"])
            copy_scalar(a, "qa", [qa[:, i, :] for i in range(NT)], lambda n: 4 + n, width=LORA_Q)
            copy_scalar(a, "dkv", [ckv[:, i, :] for i in range(NT)], lambda n: 6 + n, width=LORA_KV + ROPE)
            a.wait_ge(scalar_steps, a.n)
            for i in range(NT):
                nc.scalar.activation(junk(2 * i, BANK)[:, 0:LORA_Q], qa[:, i, :], ACT.Square,
                                     accum_out=stat[:, i:i + 1]).then_inc(scalar_steps, a.step("mla.ss"))
                nc.scalar.activation(junk(2 * i + 1, BANK)[:, 0:LORA_KV], ckv[:, i, 0:LORA_KV], ACT.Square,
                                     accum_out=stat[:, 2 + i:3 + i]).then_inc(scalar_steps, a.step("mla.ss"))
            std_scalar(a, "mla", 4)
            pair = [slice(2 * g, 2 * g + 2) for g in range(4)]
            copy_scalar(a, "qn", [qnT[:, c, :].rearrange("p a b -> p (a b)") for c in pair], lambda n: 4 + n)
            copy_scalar(a, "qr", [q_r[:, i, :] for i in range(NT)], lambda n: n)
            copy_scalar(a, "kn", [knT[:, c, :].rearrange("p a b -> p (a b)") for c in pair], lambda n: 4 + n)
            copy_scalar(a, "vm", token_tiles(v_m), lambda n: n)
            softmax_scalar(a, mla)
            post_scalar(a, "mla_out")

        def mla_vector(v):
            double_norm_vector(v, "m1_1", col("norm2", 4), MOD2[1] + SC1, MOD2[1] + SH1,
                               col("kvn2"), KVMOD2 + 1, KVMOD2, kvT2)
            v.wait_ge(*when("mla.ss"))
            for cut, n in (((0, 2), LORA_Q), ((2, 4), LORA_KV)):
                nc.vector.tensor_scalar(stat[:, 16 + cut[0]:16 + cut[1]], stat[:, cut[0]:cut[1]], 1.0 / n, EPS,
                                        ALU.mult, ALU.add).then_inc(vector_steps, v.step("mla.var"))
            v.wait_ge(*when("mla.std"))
            nc.vector.reciprocal(stat[:, 48:52], stat[:, 32:36]).then_inc(vector_steps, v.step())
            v.wait_ge(vector_steps, v.n)
            for i in range(NT):
                nc.vector.tensor_scalar(qa[:, i, :], qa[:, i, :], stat[:, 48 + i:49 + i], None, ALU.mult) \
                    .then_inc(vector_steps, v.step())
                nc.vector.tensor_scalar(ckv[:, i, 0:LORA_KV], ckv[:, i, 0:LORA_KV], stat[:, 50 + i:51 + i], None,
                                        ALU.mult).then_inc(vector_steps, v.step("mla.qa"))
            turned_vector(v, "qat", qaT, lambda c: cols[:, COLS["qn"] + c:COLS["qn"] + c + 1], bank=0, chunks=3)
            turned_vector(v, "ckvt", ckvT, lambda c: cols[:, COLS["kvl"] + c:COLS["kvl"] + c + 1], bank=2, chunks=2)
            for i in range(NT):
                rope_vector(v, ckv[:, i, LORA_KV:].unsqueeze(1), i, ROT2, ROT1, tmp_m)
            v.wait_ge(vector_steps, v.n)
            for i in range(NT):
                nc.vector.tensor_copy(k_r[:, i, :].rearrange("p (a b) -> p a b", a=2),
                                      ckv[:, i, LORA_KV:].unsqueeze(1).to_broadcast([P, 2, ROPE])) \
                    .then_inc(vector_steps, v.step())
            for i in range(NT):
                v.wait_ge(*when(f"qr.out{i}"))
                rope_vector(v, q_r[:, i, :].rearrange("p (h d) -> p h d", d=ROPE), i, ROT2, ROT1, tmp_m)
            v.wait_ge(vector_steps, v.n)
            nc.vector.tensor_copy(stat[:, 63:64], stat[:, 63:64]).then_inc(vector_steps, v.step("mla.rot"))
            turned_vector(v, "krt", krT, bank=4, chunks=1)
            turned_vector(v, "qrt", qrT, bank=5, chunks=4)
            softmax_vector(v, mla, o_m, float(NOPE + ROPE) ** -0.5,
                           lambda i: blockm[:, P:2 * P] if i == 0 else blockm[:, :])
            turned_vector(v, "mla_turn", yT, bank=0)
            post_vector(v, "mla_out", col("norm2", 5), MOD2[1] + G1, 4)

        def later_tensor(t):
            swa_tensor(t)
            norm_tensor(t, "n2_1")
            peer_score_tensor(t, 1)
            peer_out_tensor(t, 1)
            last_norm_tensor(t)
            mlstm_tensor(t)
            mlp_tensor(t, 0)
            mla_tensor(t)
            mlp_tensor(t, 1)

        def later_scalar(a):
            swa_scalar(a)
            norm_scalar(a, "n2_1", ["swa_out.x"])
            peer_score_scalar(a, 1)
            peer_out_scalar(a, 1)
            last_norm_scalar(a)
            mlstm_scalar(a)
            mlp_scalar(a, 0, "ml_out.x")
            mla_scalar(a)
            mlp_scalar(a, 1, "mla_out.x")

        def later_vector(v):
            swa_vector(v)
            norm_vector(v, "n2_1", col("norm1", 3), MOD1[1] + SC2, MOD1[1] + SH2)
            peer_choose_vector(v, 1)
            peer_routes_vector(v, 1)
            peer_out_vector(v, 1)
            last_norm_vector(v)
            mlstm_vector(v)
            mlp_vector(v, 0)
            mla_vector(v)
            mlp_vector(v, 1)

        block = ctx.enter_context(nc.Block())

        @block.sync
        def _(sp):
            load_inputs_sync(sp)
            spans = []
            for name, n in PLAN:
                tiles = TILE0.get(name)
                if spans and tiles is None and spans[-1][2] is None:
                    spans[-1] = (spans[-1][0], START[name] + n, None)
                else:
                    spans.append((START[name], START[name] + n, tiles))

            def used_up(a, tiles, n, e):
                if tiles is None:
                    return slab_used, n + (PLAIN[a])
                return lo_made, n * 2 + (tiles + e + 1)

            halves = [slice(e * D, (e + 1) * D) for e in range(2)]
            for k, (a, end, tiles) in enumerate(spans):
                for s in (a, a + 1):
                    for e in range(2):
                        if k:
                            before, _, tiles_before = spans[k - 1]
                            sp.wait_ge(*used_up(before, tiles_before, s - RING - before, e))
                        sp.dma_start(ring[:, s % RING, halves[e]], io["stream"][s, :, halves[e]]) \
                            .then_inc(slab_landed[s % RING][e], 16)
                with sp.Fori(1, (end - a) // RING) as i:
                    for j in range(RING):
                        for e in range(2):
                            sp.wait_ge(*used_up(a, tiles, i * RING + (j - RING), e))
                            sp.dma_start(ring[:, (a + j) % RING, halves[e]],
                                         io["stream"][bass.ds(i * RING + (a + j), 1), :, halves[e]]
                                         .rearrange("a p n -> (a p) n")).then_inc(slab_landed[(a + j) % RING][e], 16)
                for s in range(a + (end - a) // RING * RING, end):
                    for e in range(2):
                        sp.wait_ge(*used_up(a, tiles, s - RING - a, e))
                        sp.dma_start(ring[:, s % RING, halves[e]], io["stream"][s, :, halves[e]]) \
                            .then_inc(slab_landed[s % RING][e], 16)
            key, n = marks.get("x.final", ("V", 1))
            sp.wait_ge(sems[key], n)
            sp.dma_start(io["out"], x[:, :, :]).then_inc(out_written, 16)
            sp.wait_ge(out_written, 16)

        @block.gpsimd
        def _(pool):
            g = Steps(pool, "G")
            constants_gpsimd(g)
            first_mod_loads(pool, range(2, FIRST_STRIPS))
            for free_at_first in (hi_free, lo_free, banks_free):
                pool.sem_inc(free_at_first, 2)
            for l in range(2):
                for i in range(NT):
                    g.wait_ge(*when(f"n2_{l}.xn{i}"))
                pool.dma_start(io["x_kept"], x[:, :, :]).then_inc(x_kept, 16)
                split_lo_gpsimd(g, f"peer_q{l}", 0, 2)
                split_lo_gpsimd(g, f"u{l}", 0, 16)
                split_lo_gpsimd(g, f"v{l}", 0, 8)
                split_lo_gpsimd(g, f"v{l}", 8, 16)
                g.wait_ge(*when(f"peer{l}.full"))
                pool.wait_ge(strip_stored, (l + 1) * LOOP_STRIPS)
                pool.wait_ge(x_kept, 16 * (l + 1))
                pool.dma_start(x[:, :, :], io["x_kept"]).then_inc(x_back, 16)
            for name in ("ffn1_0", "ffn2_0", "ffn1_1", "ffn2_1"):
                split_lo_gpsimd(g, name, 0, 4)

        @block.scalar
        def _(act):
            a = Steps(act, "A")
            act.wait_ge(inputs_landed, ALL_INPUTS)
            nc.scalar.activation(c_act[:, :], cols[:, 0:16], ACT.Silu).then_inc(scalar_steps, a.step("c_act"))
            first_mod_loads(act, (0, 1))
            trig_scalar(a)
            norm_scalar(a, "n1", [])
            gla_scalar(a)
            norm_scalar(a, "n2_0", ["gla_out.x"])
            peer_score_scalar(a, 0)
            peer_out_scalar(a, 0)
            later_scalar(a)

        @block.vector
        def _(dve):
            v = Steps(dve, "V")
            v.wait_ge(*when("constants"))
            trig_vector(v)
            first_mod_vector(v, (0, 1))
            first_mod_store(v, (0, 1), 0)
            norm_vector(v, "n1", col("norm1", 0), MOD1[0] + SC1, MOD1[0] + SH1)
            first_mod_vector(v, (2, 3))
            gla_vector(v)
            norm_vector(v, "n2_0", col("norm1", 1), MOD1[0] + SC2, MOD1[0] + SH2)
            peer_choose_vector(v, 0)
            peer_routes_vector(v, 0)
            peer_out_vector(v, 0)
            later_vector(v)
            v.wait_ge(vector_steps, v.n)
            nc.vector.tensor_copy(stat[:, 0:1], stat[:, 0:1]).then_inc(vector_steps, v.step("x.final"))

        @block.tensor
        def _(pe):
            t = Steps(pe, "T")
            t.wait_ge(*when("constants"))
            first_mod_tensor(t, (0, 1), 0)
            norm_tensor(t, "n1")
            gla_tensor(t)
            norm_tensor(t, "n2_0")
            peer_score_tensor(t, 0)
            peer_out_tensor(t, 0)
            later_tensor(t)
    return new_marks


def pack(inputs):
    f = np.float32

    def T(w):
        k, n = w.shape
        b = w.reshape(k // P, P, n // P, P).transpose(2, 1, 0, 3).reshape(n // P, P, -1)
        per = 4 if k == LORA_Q else SLAB // b.shape[2]
        b = b.reshape(n // P // per, per, P, -1).transpose(0, 2, 1, 3).reshape(n // P // per, P, -1)
        return fill(b)

    def M(w, per):
        k, n = w.shape
        return fill(w.reshape(k // P // per, per, P, n).transpose(0, 2, 1, 3).reshape(k // P // per, P, -1))

    def fill(b):
        out = np.zeros((b.shape[0], P, SLAB), f)
        out[:, :, :b.shape[2]] = b
        return out

    def vec(a, n):
        return np.asarray(a).reshape(-1, n, P).transpose(2, 0, 1).reshape(P, -1)

    g = {k: np.asarray(v) for k, v in inputs.items()}
    gin, ain = g["gla_w_in"][0], g["a_w_in_2"][0]
    qb = g["b_w_qb_2"][0].reshape(LORA_Q, MLA_H, NOPE + ROPE)
    ukv = g["w_ukv_2"].reshape(LORA_KV, MLA_H, 2 * P)
    order = [8 * (c // 4) + c % 4 + 4 * j for c in range(8) for j in range(2)]
    swa_q = g["swa_w_q"][0].reshape(D, SWA_H, SWA_D)[:, order].reshape(D, D)
    parts = {
        "gla_qk": T(gin[:, :D]), "gla_v": M(gin[:, D:2 * D], 2), "gla_og": M(gin[:, 2 * D:3 * D], 2),
        "gla_out": M(g["gla_w_out"][0], 2), "kv": M(g["kv_w"], 4), "swa_q": M(swa_q, 2),
        "swa_out": M(g["swa_w_out"][0], 2),
        "ml_qk": T(ain[:, :D]), "ml_v": M(ain[:, D:2 * D], 2), "ml_o": M(ain[:, 2 * D:3 * D], 2),
        "ml_out": M(g["a_w_out_2"][0], 2), "qa": M(g["b_w_qa_2"][0], 4), "dkv": M(g["w_dkv_2"], 4),
        "qb_nope": T(np.ascontiguousarray(qb[:, :, :NOPE]).reshape(LORA_Q, -1)),
        "qb_rope": M(np.ascontiguousarray(qb[:, [0, 4, 1, 5, 2, 6, 3, 7], NOPE:]).reshape(LORA_Q, -1), 3),
        "ukv_k": T(np.ascontiguousarray(ukv[:, :, :P]).reshape(LORA_KV, -1)),
        "ukv_v": M(np.ascontiguousarray(ukv[:, :, P:]).reshape(LORA_KV, -1), 2),
        "mla_out": M(g["b_w_o_2"][0], 2),
    }
    for l in range(2):
        parts[f"peer_q{l}"] = T(g["peer_w_q"][l])
        u = g["peer_u"][l].reshape(64, 2, P, DC, P).transpose(0, 4, 1, 3, 2).reshape(64, P, SLAB)
        parts[f"u{l}"] = u
        parts[f"v{l}"] = g["peer_v"][l].reshape(64, 2, P, D).transpose(0, 2, 1, 3).reshape(64, P, SLAB)
        parts[f"ffn1_{l}"] = T(g["ffn_w1_2"][l])
        parts[f"ffn2_{l}"] = M(g["ffn_w2_2"][l], 2)
    stream = np.empty((N_SLABS, P, SLAB), f)
    for name, n in PLAN:
        assert parts[name].shape[0] == n, name
        stream[START[name]:START[name] + n] = parts[name]

    def strips(w):
        return w.reshape(DC, P, -1, D).transpose(2, 0, 1, 3).reshape(-1, P, D)
    mod = np.concatenate([strips(g["mod_w"][0]), strips(g["mod_w"][1]), strips(g["kv_mod_w"]),
                          strips(g["mod_w_2"][0]), strips(g["mod_w_2"][1]), strips(g["kv_mod_w_2"])])
    colv = np.concatenate([
        vec(g["c"], 8), vec(g["c_2"], 8), vec(g["mod_b"], 8), vec(g["kv_mod_b"], 8), vec(g["mod_b_2"], 8),
        vec(g["kv_mod_b_2"], 8), vec(g["norm_g"], 8), vec(g["kv_norm_g"], 8), vec(g["final_norm_g"], 8),
        vec(g["norm_g_2"], 8), vec(g["kv_norm_2"], 8), vec(g["gla_b_g2"], 4), vec(g["b_q_norm_2"], 3),
        vec(g["kv_lora_norm_2"], 2)], axis=1)
    inv1 = f(500000.0) ** (-np.arange(0, 2 * ROT1, 2, dtype=f) / f(2 * ROT1))
    inv2 = f(10000.0) ** (-np.arange(0, 2 * ROT2, 2, dtype=f) / f(2 * ROT2))
    rowv = np.concatenate([g["swa_sinks"].ravel(), g["a_b_gates_2"].ravel(), inv1, inv2, g["gla_norm_g"].ravel(),
                           g["a_head_norm_2"].ravel()])[None].astype(f)
    pos = np.concatenate([g["positions"].reshape(NT, P).T, g["positions_2"].reshape(NT, P).T], axis=1)

    def chunked(w):
        return w.reshape(DC, P, -1).transpose(1, 0, 2)
    c = np.ascontiguousarray
    return {
        "stream": stream, "mod": c(mod), "cols": c(colv), "rows": rowv, "pos": c(pos).astype(np.int32),
        "subk": c(g["peer_subkeys"].transpose(3, 0, 1, 2)), "w_gates": c(chunked(ain[:, 3 * D:])),
        "w_gl": c(chunked(gin[:, 3 * D:])), "w_g2": c(g["gla_w_g2"][0]),
        "x": c(g["x"].reshape(NT, P, D).transpose(1, 0, 2)),
    }


def kernel(**inputs):
    import concourse.bacc as bacc
    from concourse.bass_utils import run_bass_kernel_spmd

    arrays = pack(inputs)
    marks = {}
    for _ in range(2):
        nc = bacc.Bacc("TRN2", target_bir_lowering=False, num_devices=1)
        io = {name: nc.dram_tensor(f"in_{name}", a.shape, mybir.dt.from_np(a.dtype), kind="ExternalInput").ap()
              for name, a in arrays.items()}
        io["out"] = nc.dram_tensor("out_x", (P, NT, D), F32, kind="ExternalOutput").ap()
        io["x_kept"] = nc.dram_tensor("x_kept", (P, NT, D), F32, kind="Internal").ap()
        marks = build(nc, io, marks)
    r = run_bass_kernel_spmd(nc, [{f"in_{name}": a for name, a in arrays.items()}], core_ids=[0])
    out = r.results[0]["out_x"]
    return np.ascontiguousarray(np.asarray(out).transpose(1, 0, 2)).reshape(1, SEQ, D)
```
